# Optimizing a Trainium2 kernel written in Bass

```python
import math
import jax, jax.numpy as jnp
from jax import lax
import numpy as np

D_MODEL = 1024
BATCH = 1
SEQ = 256
DEPTH = 2

N_A_LAYERS = DEPTH // 2
N_B_LAYERS = DEPTH - N_A_LAYERS
N_DENSE = (DEPTH + 1) // 2
N_MOE = DEPTH // 2

DN_ALPHA = (2.0 * DEPTH) ** 0.25
DN_BETA = (8.0 * DEPTH) ** -0.25
LN_EPS = 1e-5
RMS_EPS = 1e-6

SSM_EXPAND = 2
SSM_D_INNER = SSM_EXPAND * D_MODEL
SSM_HEAD_DIM = 64
SSM_N_HEADS = SSM_D_INNER // SSM_HEAD_DIM
SSM_N_GROUPS = 4
SSM_D_STATE = 128
SSM_CONV = 4
SSM_CHUNK = 128
SSM_GN = SSM_N_GROUPS * SSM_D_STATE
SSM_CONV_DIM = SSM_D_INNER + 2 * SSM_GN
SSM_IN_DIM = 2 * SSM_D_INNER + 2 * SSM_GN + SSM_N_HEADS
SSM_DT_MIN = 1e-3
SSM_DT_MAX = 1e-1

MLA_N_HEADS = 8
MLA_NOPE = 128
MLA_ROPE = 64
MLA_V = 128
MLA_Q_LORA = 384
MLA_KV_LORA = 256
MLA_QK = MLA_NOPE + MLA_ROPE
MLA_SCALE = MLA_QK ** -0.5
ROPE_BASE = 10000.0
Q_BLOCK = 128
MAX_POS_OFFSET = 1024

FFN_D_FF = 2816
N_EXPERTS = 8
TOP_K = 2
EXPERT_D_FF = 2816

kernel_name = "yoco_mamba2_mla_moe_deepnorm"

def layer_norm(x, g, b):
    xf = x.astype(jnp.float32)
    mu = jnp.mean(xf, axis=-1, keepdims=True)
    var = jnp.mean(jnp.square(xf - mu), axis=-1, keepdims=True)
    return ((xf - mu) * lax.rsqrt(var + LN_EPS) * g + b).astype(x.dtype)

def rms_norm(x, g):
    xf = x.astype(jnp.float32)
    xf = xf * lax.rsqrt(jnp.mean(jnp.square(xf), axis=-1, keepdims=True) + RMS_EPS)
    return (xf * g).astype(x.dtype)

def rope_cos_sin(positions):
    inv_freq = ROPE_BASE ** (-jnp.arange(0, MLA_ROPE, 2, dtype=jnp.float32) / MLA_ROPE)
    ang = positions.astype(jnp.float32)[..., None] * inv_freq
    return jnp.cos(ang), jnp.sin(ang)

def apply_rope(x, cos, sin):
    xf = x.astype(jnp.float32)
    x1, x2 = jnp.split(xf, 2, axis=-1)
    return jnp.concatenate([x1 * cos - x2 * sin, x2 * cos + x1 * sin], axis=-1).astype(x.dtype)

def swiglu(x, w_gate, w_up, w_down):
    return (jax.nn.silu(x @ w_gate) * (x @ w_up)) @ w_down

def causal_depthwise_conv(u, w, b):
    k = w.shape[0]
    out = lax.conv_general_dilated(
        u, w[:, None, :], window_strides=(1,), padding=[(k - 1, 0)],
        dimension_numbers=("NWC", "WIO", "NWC"), feature_group_count=u.shape[-1])
    return out + b

def ssd_chunked(xs, dt, a, bm, cm):
    f32 = jnp.float32
    bsz, s, h, p = xs.shape
    g, n = bm.shape[2], bm.shape[3]
    e = h // g
    nc = s // SSM_CHUNK
    l = SSM_CHUNK
    xd = (xs.astype(f32) * dt[..., None]).reshape(bsz, nc, l, g, e, p)
    la = jnp.transpose((dt * a).reshape(bsz, nc, l, g, e), (0, 1, 3, 4, 2))
    cum = jnp.cumsum(la, axis=-1)
    bc = bm.astype(f32).reshape(bsz, nc, l, g, n)
    cc = cm.astype(f32).reshape(bsz, nc, l, g, n)
    causal = jnp.tril(jnp.ones((l, l), dtype=bool))
    seg = cum[..., :, None] - cum[..., None, :]
    decay = jnp.exp(jnp.where(causal, seg, -jnp.inf))
    cb = jnp.einsum("bclgn,bcsgn->bcgls", cc, bc)
    y_diag = jnp.einsum("bcgels,bcsgep->bclgep", cb[:, :, :, None] * decay, xd)
    decay_to_end = jnp.exp(cum[..., -1:] - cum)
    states = jnp.einsum("bclgn,bcgel,bclgep->bcgepn", bc, decay_to_end, xd)
    chunk_decay = jnp.exp(cum[..., -1])

    def step(carry, inp):
        st, dec = inp
        return carry * dec[..., None, None] + st, carry

    h0 = jnp.zeros((bsz, g, e, p, n), f32)
    _, prev = lax.scan(step, h0, (jnp.moveaxis(states, 1, 0), jnp.moveaxis(chunk_decay, 1, 0)))
    prev = jnp.moveaxis(prev, 0, 1)
    y_off = jnp.einsum("bclgn,bcgepn,bcgel->bclgep", cc, prev, jnp.exp(cum))
    return (y_diag + y_off).reshape(bsz, s, h, p)

def mamba2_mixer(x, w_in, conv_w, conv_b, dt_bias, a_log, d_skip, norm_g, w_out):
    bsz, s, _ = x.shape
    zxbcdt = x @ w_in
    z, xbc, dt = jnp.split(zxbcdt, [SSM_D_INNER, SSM_D_INNER + SSM_CONV_DIM], axis=-1)
    xbc = jax.nn.silu(causal_depthwise_conv(xbc, conv_w, conv_b))
    xs, bm, cm = jnp.split(xbc, [SSM_D_INNER, SSM_D_INNER + SSM_GN], axis=-1)
    xs = xs.reshape(bsz, s, SSM_N_HEADS, SSM_HEAD_DIM)
    bm = bm.reshape(bsz, s, SSM_N_GROUPS, SSM_D_STATE)
    cm = cm.reshape(bsz, s, SSM_N_GROUPS, SSM_D_STATE)
    dt = jax.nn.softplus(dt.astype(jnp.float32) + dt_bias)
    a = -jnp.exp(a_log.astype(jnp.float32))
    y = ssd_chunked(xs, dt, a, bm, cm) + d_skip[:, None] * xs
    y = y.reshape(bsz, s, SSM_D_INNER) * jax.nn.silu(z)
    yg = y.astype(jnp.float32).reshape(bsz, s, SSM_N_GROUPS, -1)
    yg = yg * lax.rsqrt(jnp.mean(jnp.square(yg), axis=-1, keepdims=True) + LN_EPS)
    y = (yg.reshape(bsz, s, SSM_D_INNER) * norm_g).astype(x.dtype)
    return y @ w_out

def mla_shared_kv(h, w_kv_a, kv_norm_g, w_kv_b, cos, sin):
    bsz, s, _ = h.shape
    kv_a = h @ w_kv_a
    c_kv, k_rope = jnp.split(kv_a, [MLA_KV_LORA], axis=-1)
    c_kv = rms_norm(c_kv, kv_norm_g)
    kv = (c_kv @ w_kv_b).reshape(bsz, s, MLA_N_HEADS, MLA_NOPE + MLA_V)
    k_nope, v = jnp.split(kv, [MLA_NOPE], axis=-1)
    k_rope = apply_rope(k_rope, cos, sin)
    return k_nope, k_rope, v

def mla_attention(x, k_nope, k_rope, v, w_q_a, q_norm_g, w_q_b, w_o, cos, sin):
    bsz, s, _ = x.shape
    q = rms_norm(x @ w_q_a, q_norm_g) @ w_q_b
    q = q.reshape(bsz, s, MLA_N_HEADS, MLA_QK)
    q_nope, q_rope = jnp.split(q, [MLA_NOPE], axis=-1)
    q_rope = apply_rope(q_rope, cos[:, :, None, :], sin[:, :, None, :])
    nb = s // Q_BLOCK
    k_pos = jnp.arange(s)

    def block(args):
        qn, qr, i = args
        sc = (jnp.einsum("bqhd,bkhd->bhqk", qn, k_nope)
              + jnp.einsum("bqhr,bkr->bhqk", qr, k_rope)).astype(jnp.float32) * MLA_SCALE
        q_pos = i * Q_BLOCK + jnp.arange(Q_BLOCK)
        sc = jnp.where(k_pos[None, :] <= q_pos[:, None], sc, -jnp.inf)
        pr = jax.nn.softmax(sc, axis=-1).astype(v.dtype)
        return jnp.einsum("bhqk,bkhd->bqhd", pr, v)

    qn_b = jnp.moveaxis(q_nope.reshape(bsz, nb, Q_BLOCK, MLA_N_HEADS, MLA_NOPE), 1, 0)
    qr_b = jnp.moveaxis(q_rope.reshape(bsz, nb, Q_BLOCK, MLA_N_HEADS, MLA_ROPE), 1, 0)
    o = lax.map(block, (qn_b, qr_b, jnp.arange(nb)))
    o = jnp.moveaxis(o, 0, 1).reshape(bsz, s, MLA_N_HEADS * MLA_V)
    return o @ w_o

def moe_swiglu(x, w_router, b_router, w_gate, w_up, w_down):
    logits = (x @ w_router).astype(jnp.float32) + b_router
    top_val, top_idx = lax.top_k(logits, TOP_K)
    top_w = jax.nn.softmax(top_val, axis=-1)
    gates = jnp.einsum("bsk,bske->bse", top_w,
                       jax.nn.one_hot(top_idx, N_EXPERTS, dtype=jnp.float32))
    out = jnp.zeros_like(x)
    for e in range(N_EXPERTS):
        out = out + gates[..., e:e + 1].astype(x.dtype) * swiglu(x, w_gate[e], w_up[e], w_down[e])
    return out

def setup_inputs(seed: int = 0) -> dict:
    key = jax.random.key(seed)
    ks = iter(jax.random.split(key, 40))
    f32 = jnp.float32

    def nrm(shape, scale):
        return jax.random.normal(next(ks), shape, f32) * scale

    x = jax.random.normal(next(ks), (BATCH, SEQ, D_MODEL), f32)
    offset = jax.random.randint(next(ks), (BATCH, 1), 0, MAX_POS_OFFSET, dtype=jnp.int32)
    positions = offset + jnp.arange(SEQ, dtype=jnp.int32)[None, :]
    ln_g = 1.0 + nrm((DEPTH, 2, D_MODEL), 0.02)
    ln_b = nrm((DEPTH, 2, D_MODEL), 0.02)
    ssm_w_in = nrm((N_A_LAYERS, D_MODEL, SSM_IN_DIM), D_MODEL ** -0.5)
    ssm_conv_w = nrm((N_A_LAYERS, SSM_CONV, SSM_CONV_DIM), SSM_CONV ** -0.5)
    ssm_conv_b = nrm((N_A_LAYERS, SSM_CONV_DIM), 0.02)
    dt0 = jnp.exp(jax.random.uniform(next(ks), (N_A_LAYERS, SSM_N_HEADS), f32,
                                     math.log(SSM_DT_MIN), math.log(SSM_DT_MAX)))
    ssm_dt_bias = dt0 + jnp.log(-jnp.expm1(-dt0))
    ssm_a_log = jnp.log(jax.random.uniform(next(ks), (N_A_LAYERS, SSM_N_HEADS), f32, 1.0, 16.0))
    ssm_d = 1.0 + nrm((N_A_LAYERS, SSM_N_HEADS), 0.1)
    ssm_norm_g = 1.0 + nrm((N_A_LAYERS, SSM_D_INNER), 0.02)
    ssm_w_out = nrm((N_A_LAYERS, SSM_D_INNER, D_MODEL), SSM_D_INNER ** -0.5 * DN_BETA)
    mla_w_kv_a = nrm((D_MODEL, MLA_KV_LORA + MLA_ROPE), D_MODEL ** -0.5)
    mla_kv_norm_g = 1.0 + nrm((MLA_KV_LORA,), 0.02)
    mla_w_kv_b = nrm((MLA_KV_LORA, MLA_N_HEADS * (MLA_NOPE + MLA_V)), MLA_KV_LORA ** -0.5)
    mla_w_q_a = nrm((N_B_LAYERS, D_MODEL, MLA_Q_LORA), D_MODEL ** -0.5)
    mla_q_norm_g = 1.0 + nrm((N_B_LAYERS, MLA_Q_LORA), 0.02)
    mla_w_q_b = nrm((N_B_LAYERS, MLA_Q_LORA, MLA_N_HEADS * MLA_QK), MLA_Q_LORA ** -0.5)
    mla_w_o = nrm((N_B_LAYERS, MLA_N_HEADS * MLA_V, D_MODEL), (MLA_N_HEADS * MLA_V) ** -0.5 * DN_BETA)
    ffn_w_gate = nrm((N_DENSE, D_MODEL, FFN_D_FF), D_MODEL ** -0.5)
    ffn_w_up = nrm((N_DENSE, D_MODEL, FFN_D_FF), D_MODEL ** -0.5)
    ffn_w_down = nrm((N_DENSE, FFN_D_FF, D_MODEL), FFN_D_FF ** -0.5 * DN_BETA)
    moe_w_router = nrm((N_MOE, D_MODEL, N_EXPERTS), D_MODEL ** -0.5)
    moe_b_router = nrm((N_MOE, N_EXPERTS), 0.01)
    moe_w_gate = nrm((N_MOE, N_EXPERTS, D_MODEL, EXPERT_D_FF), D_MODEL ** -0.5)
    moe_w_up = nrm((N_MOE, N_EXPERTS, D_MODEL, EXPERT_D_FF), D_MODEL ** -0.5)
    moe_w_down = nrm((N_MOE, N_EXPERTS, EXPERT_D_FF, D_MODEL), EXPERT_D_FF ** -0.5 * DN_BETA)
    return {
        "x": x, "positions": positions, "ln_g": ln_g, "ln_b": ln_b,
        "ssm_w_in": ssm_w_in, "ssm_conv_w": ssm_conv_w, "ssm_conv_b": ssm_conv_b,
        "ssm_dt_bias": ssm_dt_bias, "ssm_a_log": ssm_a_log, "ssm_d": ssm_d,
        "ssm_norm_g": ssm_norm_g, "ssm_w_out": ssm_w_out,
        "mla_w_kv_a": mla_w_kv_a, "mla_kv_norm_g": mla_kv_norm_g, "mla_w_kv_b": mla_w_kv_b,
        "mla_w_q_a": mla_w_q_a, "mla_q_norm_g": mla_q_norm_g, "mla_w_q_b": mla_w_q_b,
        "mla_w_o": mla_w_o,
        "ffn_w_gate": ffn_w_gate, "ffn_w_up": ffn_w_up, "ffn_w_down": ffn_w_down,
        "moe_w_router": moe_w_router, "moe_b_router": moe_b_router,
        "moe_w_gate": moe_w_gate, "moe_w_up": moe_w_up, "moe_w_down": moe_w_down,
    }

def reference(x, positions, ln_g, ln_b,
              ssm_w_in, ssm_conv_w, ssm_conv_b, ssm_dt_bias, ssm_a_log, ssm_d,
              ssm_norm_g, ssm_w_out,
              mla_w_kv_a, mla_kv_norm_g, mla_w_kv_b,
              mla_w_q_a, mla_q_norm_g, mla_w_q_b, mla_w_o,
              ffn_w_gate, ffn_w_up, ffn_w_down,
              moe_w_router, moe_b_router, moe_w_gate, moe_w_up, moe_w_down):
    cos, sin = rope_cos_sin(positions)
    h = x
    k_nope = k_rope = v = None
    for layer in range(DEPTH):
        if layer < N_A_LAYERS:
            a = layer
            mix = mamba2_mixer(h, ssm_w_in[a], ssm_conv_w[a], ssm_conv_b[a], ssm_dt_bias[a],
                               ssm_a_log[a], ssm_d[a], ssm_norm_g[a], ssm_w_out[a])
        else:
            bi = layer - N_A_LAYERS
            if bi == 0:
                k_nope, k_rope, v = mla_shared_kv(h, mla_w_kv_a, mla_kv_norm_g, mla_w_kv_b, cos, sin)
            mix = mla_attention(h, k_nope, k_rope, v, mla_w_q_a[bi], mla_q_norm_g[bi],
                                mla_w_q_b[bi], mla_w_o[bi], cos, sin)
        h = layer_norm(DN_ALPHA * h + mix, ln_g[layer, 0], ln_b[layer, 0])
        c = layer // 2
        if layer % 2 == 0:
            ffn = swiglu(h, ffn_w_gate[c], ffn_w_up[c], ffn_w_down[c])
        else:
            ffn = moe_swiglu(h, moe_w_router[c], moe_b_router[c], moe_w_gate[c],
                             moe_w_up[c], moe_w_down[c])
        h = layer_norm(DN_ALPHA * h + ffn, ln_g[layer, 1], ln_b[layer, 1])
    return h


_drawn_inputs = setup_inputs


def setup_inputs(seed=0):
    import zlib

    import numpy as np

    out = dict(_drawn_inputs(seed))
    spreads = {}
    factors = {'ssm_conv_b': 4.399,
     'ssm_norm_g': 6.613,
     'mla_kv_norm_g': 8.0,
     'mla_q_norm_g': 8.0,
     'moe_b_router': 3.912}
    for name, (base, spread) in spreads.items():
        noise = np.random.default_rng([zlib.crc32(name.encode()), seed]).standard_normal(out[name].shape)
        drawn = base * np.exp(spread * noise) if base else spread * noise
        out[name] = __import__('jax').numpy.asarray(drawn.astype(out[name].dtype))
    for name, factor in factors.items():
        out[name] = (out[name] * factor).astype(out[name].dtype)
    return out
```

```python
import math
from contextlib import ExitStack

import concourse.bass as bass
from concourse import mybir

F32 = mybir.dt.float32
I32 = mybir.dt.int32
U32 = mybir.dt.uint32
ALU = mybir.AluOpType
ACT = mybir.ActivationFunctionType
AX = mybir.AxisListType

P = 128
SEQ, D = 256, 1024
NT = SEQ // P
KD = D // P
ALPHA = (2.0 * 2) ** 0.25
LN_EPS, RMS_EPS = 1e-5, 1e-6
DI, HD, NG, NS = 2048, 64, 4, 128
NH = DI // HD
HG = NH // NG
XBC = DI + 2 * NG * NS
NM = XBC // P
MX = DI // P
GW = DI // NG
AH, NOPE, ROPE, VD, QL, KVL = 8, 128, 64, 128, 384, 256
HR = ROPE // 2
SCALE = (NOPE + ROPE) ** -0.5
FF, NE, TOPK = 2816, 8, 2
FC = 256
NC = FF // FC
MAX_EXTRA = SEQ * TOPK // (P + 1)
NTAB = NE + MAX_EXTRA + 1
SLOT, NSLOT = 2 * KD * FC + 2 * D, 4
XC = SLOT // KD
MB = XC // P
NL_XBC, NL_Z, NL_WO = XBC // XC, DI // GW, 4
NL_FFN0 = NL_XBC + NL_Z + NL_WO
NL_KVQ = NL_FFN0 + NC
NL_MOE = NL_KVQ + 5
USED_WO = NL_WO
USED_FFN = USED_WO + NC
USED_MLA = USED_FFN + 2
NEG = -1.0e30
TWO_PI_1, TWO_PI_2 = 6.28125, 2029.0 / 2 ** 20
TWO_PI_3 = 2 * math.pi - TWO_PI_1 - TWO_PI_2
MAGIC = 1.5 * 2 ** 23
PI_IN = 3.1415925


class Count:

    def __init__(self):
        self.n, self.extra = 0, None

    def up(self, by=1):
        self.n += by
        return self.value()

    def value(self):
        return self.n if self.extra is None else self.extra + self.n


def build_kernel(nc, d, out):
    ctx = ExitStack()
    with ctx:
        def sb(name, shape, dt=F32):
            return ctx.enter_context(nc.sbuf_tensor(name, shape, dt))

        def sems(names):
            return [ctx.enter_context(nc.semaphore(n)) for n in names.split()]

        ring = sb("ring", [P, NSLOT, SLOT])
        h_tok = sb("h_tok", [P, NT, D])
        h_T = sb("h_T", [P, KD, SEQ])
        ln_gb = sb("ln_gb", [P, 2 * D])
        ident, tri, stri, ones = (sb(n, [P, P]) for n in ("ident", "tri", "stri", "ones"))
        slot_iota = sb("slot_iota", [P, P])
        causal_add = sb("causal_add", [P, 2 * P])
        before = sb("before", [P, NE, NE])
        neg_half = sb("neg_half", [P, 2])
        conv_wb = sb("conv_wb", [P, NM, 5])
        gains = sb("gains", [P, MX + 2 + 3])
        rows = sb("rows", [P, 3 * NH + NE + HR])
        w_dt = sb("w_dt", [P, KD, NH])
        w_rt = sb("w_rt", [P, KD, NE])
        pos_i = sb("pos_i", [P, NT], I32)
        dt_bias, a_log, d_skip = (rows[:, k * NH:(k + 1) * NH] for k in range(3))
        b_rt = rows[:, 3 * NH:3 * NH + NE]
        inv_freq = rows[:, 3 * NH + NE:]
        NJ = 2 * NG + 4 * NT + NT
        pow_in_t, pow_out_t = sb("pow_in_t", [P, NJ, 2]), sb("pow_out_t", [P, NJ, 2])
        bn, mv = sb("bn", [P, 2, 6]), sb("mv", [P, NT, 2])
        sil, hid = sb("sil", [P, 2, FC]), sb("hid", [P, 2, FC])
        hid_T = sb("hid_T", [P, 2, 2, P])
        dt_v, dt_e, dt_s, dt_q, dt_p, dt, la = (
            sb(n, [P, NT * NH]) for n in ("dt_v", "dt_e", "dt_s", "dt_q", "dt_p", "dt", "la"))
        exp_a = sb("exp_a", [P, NH])
        cum, to_end, decay_end, decay_cum = (
            sb("cum", [P, NT * NH]), sb("to_end", [P, NH]), sb("decay_end", [P, NH]), sb("decay_cum", [P, NH]))
        sq_sum = sb("sq_sum", [P, 2 * NG])
        ang, ang_k, ang_r = (sb(n, [P, NT, HR]) for n in ("ang", "ang_k", "ang_r"))
        ang_c = sb("ang_c", [P, NT, HR])
        pos_f = sb("pos_f", [P, NT])
        sin_t, cos_t = sb("sin_t", [P, NT, HR]), sb("cos_t", [P, NT, HR])
        kq_ss = sb("kq_ss", [P, NT, 2])
        mx, negm, psum_row, rinv = (sb(n, [P, AH * NT]) for n in ("mx", "negm", "psum_row", "rinv"))
        logits, top_v = sb("logits", [P, NT, NE]), sb("top_v", [P, NT, NE])
        top_i, top_f = sb("top_i", [P, NT, NE], U32), sb("top_f", [P, NT, 2])
        one_hot = sb("one_hot", [P, 2, NT, NE])
        gap, gap_e, den, w_top = sb("gap", [P, NT]), sb("gap_e", [P, NT]), sb("den", [P, NT]), sb("w_top", [P, 2, NT])
        chosen, gates, posm = sb("chosen", [P, NT, NE]), sb("gates", [P, NT, NE]), sb("posm", [P, NT, NE])
        chosen_sum = sb("chosen_sum", [P, NE])
        over, rank, sel = sb("over", [P, NE]), sb("rank", [P, NE]), sb("sel", [P, MAX_EXTRA, NE])
        rank_in = sb("rank_in", [P, NE, NE])
        sel_in = sb("sel_in", [P, NT, NE])
        ctl_f, ctl = sb("ctl_f", [P, 4]), sb("ctl", [P, 4], I32)
        slot_tab, gate_tab = sb("slot_tab", [P, NT, NTAB]), sb("gate_tab", [P, NT, NTAB])

        WORK = 17408
        work = sb("work", [P, WORK])
        used = [0]

        def carve(*shape):
            n = math.prod(shape)
            v = work[:, used[0]:used[0] + n]
            used[0] += n
            assert used[0] <= WORK, used
            names = "abcd"[:len(shape)]
            if len(shape) > 1:
                v = v.rearrange(f"p ({' '.join(names)}) -> p {' '.join(names)}", **dict(zip(names, shape)))
            return v

        xbc_T = carve(NM, SEQ)
        z_gate = carve(NT, NG, GW)
        cb_mask = carve(NT * NG, P)
        x_skip, x_dt = carve(2, GW), carve(2, GW)
        x_end, state = carve(GW), carve(2, GW)
        b_tok = hid_T[:].rearrange("p a b c -> p (a b) c")
        decay = carve(2, 4, P)
        mix_T = carve(2, 4, P)
        y_tmp = carve(GW)
        conv_acc = x_skip.rearrange("p a (b c) -> p (a b) c", c=SEQ)[:, 0:2, :]
        y_sq = sil[:].rearrange("p a b -> p (a b)")
        used[0] = 0
        ckv_n, q_n = carve(NT, KVL), carve(NT, QL)
        k_rope, k_rot = carve(NT, ROPE), carve(NT, ROPE)
        ckv_T, q_T = carve(2, SEQ), carve(3, SEQ)
        kn_T, qn_T = carve(AH, SEQ), carve(AH, SEQ)
        v_tok = carve(NT, AH * VD)
        q_rot = carve(NT, AH * ROPE)
        rot_a, rot_b = carve(AH * HR), carve(AH * HR)
        qr_T, kr_T = carve(AH, SEQ), carve(SEQ)
        o_T = carve(AH, SEQ)
        prob, prob_T = carve(4, SEQ), carve(2, NT, P)
        sq_junk = carve(QL)
        used[0] = 0
        moe_acc = carve(NT, D)
        xe_T = carve(KD, P)
        y_e = carve(2, 512)
        pick, pick_g = carve(NT, P), carve(NT, P)
        scat = carve(NT, P)

        ps = ctx.enter_context(nc.psum_tensor("ps", [P, 8, 512], F32))

        ring_full = sems("ring_full0 ring_full1 ring_full2 ring_full3")
        (x_in, xt_in, small_in, wdt_in, gb_in, out_done) = sems("x_in xt_in small_in wdt_in gb_in out_done")
        (slots_used, consts) = sems("slots_used consts")
        (dve_step, act_step) = sems("dve_step act_step")
        (dt_mm, dt_abs, dt_exp, la_ready, cum_mm, cum_ready, decays) = sems(
            "dt_mm dt_abs dt_exp la_ready cum_mm cum_ready decays")
        (xbc_mm, conv_done, xbc_done, z_mm, z_done) = sems("xbc_mm conv_done xbc_done z_mm z_done")
        (btr_mm, b_done, cb_mm, cb_done) = sems("btr_mm b_done cb_mm cb_done")
        (xs_tr, x_done, bc_mm, relu_done, dec_done, mix_done) = sems(
            "xs_tr x_done bc_mm relu_done dec_done mix_done")
        (st_mm, st_done, yd_mm, yoff_mm, y_done, sq_done, yn_done, yt_mm, yt_done) = sems(
            "st_mm st_done yd_mm yoff_mm y_done sq_done yn_done yt_mm yt_done")
        (pow_go, pow_ok, ln_done, ln_tr, hT_done) = sems("pow_go pow_ok ln_done ln_tr hT_done")
        (ang_done, trig_done) = sems("ang_done trig_done")
        (f_gu, f_silu, f_hid, f_tr, f_hT) = sems("f_gu f_silu f_hid f_tr f_hT")
        (kq_mm, kq_sq, kq_done, kr_done, kq_tr, kqT_done) = sems("kq_mm kq_sq kq_done kr_done kq_tr kqT_done")
        (nope_mm, nope_done, v_mm, v_done, qr_mm, qrot_done, qr_tr, qrT_done) = sems(
            "nope_mm nope_done v_mm v_done qr_mm qrot_done qr_tr qrT_done")
        (sc_mm, max_done, exp_done, prob_done, prob_tr, probT_done, o_mm, o_done) = sems(
            "sc_mm max_done exp_done prob_done prob_tr probT_done o_mm o_done")
        (rt_mm, gap_done, gap_exp, chosen_done, pos_mm, route_done) = sems(
            "rt_mm gap_done gap_exp chosen_done pos_mm route_done")
        (m_pick, m_gat, m_xeA, m_xeV, m_gu, m_silu, m_hid, m_tr, m_hT, m_yec, m_sc, m_acc, m_str, m_scat) = sems(
            "m_pick m_gat m_xeA m_xeV m_gu m_silu m_hid m_tr m_hT m_yec m_sc m_acc m_str m_scat")
        moe_zero, = sems("moe_zero")

        block = ctx.enter_context(nc.Block())

        def slot(n):
            return ring[:, n % NSLOT, :]

        def full(n):
            return ring_full[n % NSLOT], 16 * (n // NSLOT + 1)

        def freed(n):
            if n < NL_XBC:
                return xbc_mm, MB * (n + 1)
            if n < NL_XBC + NL_Z:
                return z_mm, NT * (n - NL_XBC + 1)
            if n < NL_KVQ:
                return slots_used, n - NL_XBC - NL_Z + 1
            if n < NL_KVQ + 3:
                return (kq_mm, v_mm, qr_mm)[n - NL_KVQ], NT
            return slots_used, USED_FFN + n - NL_KVQ - 2

        LOADS_BEFORE = NL_MOE // NSLOT
        assert NL_MOE % NSLOT == 0
        PER_ITEM = [len(range(s, NC, NSLOT)) for s in range(NSLOT)]

        def full_moe(i, c):
            s = c % NSLOT
            return ring_full[s], (i * PER_ITEM[s] + (LOADS_BEFORE + c // NSLOT + 1)) * 16

        @block.sync
        def _(sp):
            sp.dma_start(h_T[:], d["x_T"]).then_inc(xt_in, 16)
            sp.dma_start(w_dt[:], d["w_dt"]).then_inc(wdt_in, 16)

            def load(n, src):
                if n >= NSLOT:
                    sp.wait_ge(*freed(n - NSLOT))
                sp.dma_start(slot(n)[:, 0:src.shape[1]], src).then_inc(ring_full[n % NSLOT], 16)

            for q in range(NL_XBC):
                load(q, d["w_xbc"][q])
            sp.dma_start(conv_wb[:], d["conv_wb"]).then_inc(small_in, 16)
            sp.dma_start(rows[:], d["rows"].partition_broadcast(P)).then_inc(small_in, 16)
            sp.dma_start(gains[:], d["gains"]).then_inc(small_in, 16)
            sp.dma_start(pos_i[:], d["pos"]).then_inc(small_in, 16)
            sp.dma_start(w_rt[:], d["w_rt"]).then_inc(small_in, 16)
            sp.dma_start(h_tok[:], d["x_tok"]).then_inc(x_in, 16)
            sp.dma_start(ln_gb[:], d["ln_gb"][0].partition_broadcast(P)).then_inc(gb_in, 16)
            for g in range(NL_Z):
                load(NL_XBC + g, d["w_z"][g])
            for q in range(NL_WO):
                load(NL_XBC + NL_Z + q, d["w_out"][q])
            for c in range(NC):
                load(NL_FFN0 + c, d["w_ffn"][c])
                if c == 4:
                    sp.wait_ge(ln_done, NT)
                    sp.dma_start(ln_gb[:], d["ln_gb"][1].partition_broadcast(P)).then_inc(gb_in, 16)
            load(NL_KVQ, d["w_kvq"])
            load(NL_KVQ + 1, d["w_kvb"])
            load(NL_KVQ + 2, d["w_qb"])
            sp.wait_ge(ln_done, 2 * NT)
            sp.dma_start(ln_gb[:], d["ln_gb"][2].partition_broadcast(P)).then_inc(gb_in, 16)
            load(NL_KVQ + 3, d["w_o"][0])
            load(NL_KVQ + 4, d["w_o"][1])

            def load_item(i, e, first=False):
                for c in range(NC):
                    if c >= NSLOT:
                        sp.wait_ge(slots_used, i * NC + (USED_MLA + c - NSLOT + 1))
                    elif first:
                        sp.wait_ge(*freed(NL_MOE + c - NSLOT))
                    else:
                        last = c + NSLOT * ((NC - 1 - c) // NSLOT)
                        sp.wait_ge(slots_used, i * NC + (USED_MLA - NC + last + 1))
                    sp.dma_start(slot(c)[:], d["w_moe"][c][bass.ds(e, 1), :, :].rearrange("o p n -> (o p) n"))\
                        .then_inc(ring_full[c % NSLOT], 16)

            load_item(0, 0, first=True)
            with sp.Fori(1, NE) as i:
                load_item(i, i)
            sp.wait_ge(ln_done, 3 * NT)
            sp.dma_start(ln_gb[:], d["ln_gb"][3].partition_broadcast(P)).then_inc(gb_in, 16)
            sp.wait_ge(route_done, 1)
            n_extra = sp.value_load(ctl[0:1, 0:1], min_val=0, max_val=MAX_EXTRA)
            with sp.If(n_extra > 0):
                with sp.Fori(0, n_extra) as k:
                    e = sp.value_load(ctl[0:1, bass.ds(k + 1, 1)], min_val=0, max_val=NE - 1)
                    load_item(k + NE, e)
            for t in range(NT):
                sp.wait_ge(ln_done, 3 * NT + t + 1)
                sp.dma_start(out[t * P:(t + 1) * P, :], h_tok[:, t, :]).then_inc(out_done, 16)
            sp.wait_ge(out_done, 16 * NT)

        @block.gpsimd
        def _(pool):
            g = nc.gpsimd
            g.memset(ident[:], 0.0).then_inc(consts, 1)
            g.memset(tri[:], 1.0).then_inc(consts, 1)
            g.memset(stri[:], 1.0).then_inc(consts, 1)
            g.memset(ones[:], 1.0).then_inc(consts, 1)
            g.memset(causal_add[:], 0.0).then_inc(consts, 1)
            g.memset(before[:], 1.0).then_inc(consts, 1)
            g.memset(neg_half[:], -0.5).then_inc(consts, 1)
            g.memset(pow_in_t[:], 1.0).then_inc(consts, 1)
            g.memset(slot_tab[:], -1.0).then_inc(consts, 1)
            g.memset(gate_tab[:], 0.0).then_inc(consts, 1)
            g.iota(slot_iota[:], [[1, P]], base=0, channel_multiplier=0,
                   allow_small_or_imprecise_dtypes=True).then_inc(consts, 1)
            pool.wait_ge(consts, 11)
            g.affine_select(out=ident[:], in_=ident[:], compare_op=ALU.not_equal, fill=1.0, base=0,
                            pattern=[[-1, P]], channel_multiplier=1).then_inc(consts, 1)
            g.affine_select(out=tri[:], in_=tri[:], compare_op=ALU.is_ge, fill=0.0, base=0,
                            pattern=[[1, P]], channel_multiplier=-1).then_inc(consts, 1)
            g.affine_select(out=stri[:], in_=stri[:], compare_op=ALU.is_gt, fill=0.0, base=0,
                            pattern=[[1, P]], channel_multiplier=-1).then_inc(consts, 1)
            g.affine_select(out=causal_add[:, P:], in_=causal_add[:, P:], compare_op=ALU.is_ge, fill=NEG, base=0,
                            pattern=[[-1, P]], channel_multiplier=1).then_inc(consts, 1)
            g.affine_select(out=before[:], in_=before[:], compare_op=ALU.is_gt, fill=0.0, base=0,
                            pattern=[[1, NE], [-1, NE]], channel_multiplier=0).then_inc(consts, 1)
            with pool.Fori(0, NJ) as j:
                pool.wait_ge(pow_go, j + 1)
                g.tensor_tensor(pow_out_t[:, bass.ds(j, 1), :], pow_in_t[:, bass.ds(j, 1), :],
                                neg_half[:, :].unsqueeze(1), ALU.pow).then_inc(pow_ok, 1)

        CONSTS = 16

        @block.tensor
        def _(pe):
            mm, tr = nc.tensor.matmul, nc.tensor.transpose

            def group(outp, pairs):
                for k, (a, b) in enumerate(pairs):
                    last = mm(outp, a, b, start=(k == 0), stop=(k == len(pairs) - 1))
                return last

            def tok(t):
                return slice(t * P, (t + 1) * P)

            pe.wait_ge(xt_in, 16)
            pe.wait_ge(wdt_in, 16)
            for t in range(NT):
                last = group(ps[:, 4, t * NH:(t + 1) * NH], [(h_T[:, k, tok(t)], w_dt[:, k, :]) for k in range(KD)])
            last.then_inc(dt_mm, 1)

            for m in range(NM):
                q, j = divmod(m, MB)
                if j == 0:
                    pe.wait_ge(*full(q))
                if m >= 4:
                    pe.wait_ge(conv_done, m - 3)
                w = slot(q).rearrange("p (k c) -> p k c", k=KD)
                last = group(ps[:, m % 4, 0:SEQ], [(w[:, k, j * P:(j + 1) * P], h_T[:, k, :]) for k in range(KD)])
                last.then_inc(xbc_mm, 1)
                if m == 7:
                    pe.wait_ge(consts, CONSTS)
                    pe.wait_ge(la_ready, 1)
                    mm(ps[:, 5, 0:NT * NH], tri[:], la[:], start=True, stop=True)
                    mm(ps[:, 5, NT * NH:2 * NT * NH], ones[:], la[:], start=True, stop=True).then_inc(cum_mm, 1)

            def z_step(u):
                g, t = divmod(u, NT)
                n = NL_XBC + g
                if t == 0:
                    pe.wait_ge(*full(n))
                if u == 0:
                    pe.wait_ge(cum_ready, 1)
                elif u == 1:
                    pe.wait_ge(cb_done, 1)
                else:
                    pe.wait_ge(z_done, u - 1)
                w = slot(n)[:, 0:KD * GW].rearrange("p (k c) -> p k c", k=KD)
                group(ps[:, 5 if u % 2 == 0 else 3, :], [(h_T[:, k, tok(t)], w[:, k, :]) for k in range(KD)])\
                    .then_inc(z_mm, 1)

            pe.wait_ge(xbc_done, NM)
            pe.wait_ge(dt_abs, 1)
            for g in range(NG):
                last = tr(ps[:, 4, g * P:(g + 1) * P], xbc_T[:, MX + g, 0:P], ident[:])
            last.then_inc(btr_mm, 1)
            for t in range(NT):
                for g in range(NG):
                    last = mm(ps[:, 2 + t, g * P:(g + 1) * P], xbc_T[:, MX + g, tok(t)],
                              xbc_T[:, MX + NG + g, tok(t)], start=True, stop=True)
            last.then_inc(cb_mm, 1)

            def ssd_front(u):
                g, t = divmod(u, NT)
                if u >= 1:
                    pe.wait_ge(x_done, u)
                for j in range(4):
                    last = tr(ps[:, 0, j * P:(j + 1) * P], xbc_T[:, g * 4 + j, tok(t)], ident[:])
                last.then_inc(xs_tr, 1)
                for b in range(2):
                    if u >= 1:
                        pe.wait_ge(relu_done, 2 * u + b - 1)
                    for j in range(4):
                        h = t * NH + g * HG + b * 4 + j
                        last = mm(ps[:, 6 + b, j * P:(j + 1) * P], la[:, h:h + 1].broadcast_to([P, P]), tri[:],
                                  start=True, stop=True)
                    last.then_inc(bc_mm, 1)

            def y_back(u):
                pe.wait_ge(yn_done, u + 1)
                if u == 0:
                    pe.wait_ge(cb_done, 1)
                else:
                    pe.wait_ge(yt_done, u)
                g, t = divmod(u, NT)
                for j in range(4):
                    last = tr(ps[:, 2, j * P:(j + 1) * P], z_gate[:, t, g, j * P:(j + 1) * P], ident[:])
                last.then_inc(yt_mm, 1)

            NU = NG * NT
            z_step(0)
            ssd_front(0)
            for u in range(NU):
                g, t = divmod(u, NT)
                if u + 1 < NU:
                    z_step(u + 1)
                    ssd_front(u + 1)
                if t == 0:
                    pe.wait_ge(b_done, 1)
                    pe.wait_ge(x_done, u + 1)
                    if u >= 1:
                        pe.wait_ge(y_done, u)
                    mm(ps[:, 1, :], b_tok[:, g, :], x_end[:], start=True, stop=True).then_inc(st_mm, 1)
                else:
                    pe.wait_ge(st_done, g + 1)
                    mm(ps[:, 1, :], xbc_T[:, MX + NG + g, tok(t)], state[:, g % 2, :], start=True, stop=True)\
                        .then_inc(yoff_mm, 1)
                if u >= 1:
                    pe.wait_ge(y_done, u)
                for b in range(2):
                    pe.wait_ge(mix_done, 2 * u + b + 1)
                    for j in range(4):
                        c = (b * 4 + j) * HD
                        last = mm(ps[:, 4, c:c + HD], mix_T[:, b, j, :], x_dt[:, u % 2, c:c + HD],
                                  start=True, stop=True)
                last.then_inc(yd_mm, 1)
                if u >= 1:
                    y_back(u - 1)
            y_back(NU - 1)

            pe.wait_ge(yt_done, NU)
            pe.wait_ge(z_done, NU)
            for q in range(NL_WO):
                n = NL_XBC + NL_Z + q
                pe.wait_ge(*full(n))
                w = slot(n)[:, 0:4 * D].rearrange("p (k c) -> p k c", k=4)
                for j in range(4):
                    k = 4 * q + j
                    for t in range(NT):
                        for f in range(2):
                            last = mm(ps[:, 4 + 2 * t + f, :], xbc_T[:, k, tok(t)], w[:, j, f * 512:(f + 1) * 512],
                                      start=(k == 0), stop=(k == MX - 1))
                last.then_inc(slots_used, 1)

            def to_channel_major(t, ln, bank):
                pe.wait_ge(ln_done, ln * NT + t + 1)
                for k in range(KD):
                    last = tr(ps[:, bank + 2 * t + k // 4, (k % 4) * P:(k % 4 + 1) * P],
                              h_tok[:, t, k * P:(k + 1) * P], ident[:])
                last.then_inc(ln_tr, 1)

            for t in range(NT):
                to_channel_major(t, 0, 0)
            steps = [(c, t) for c in range(NC) for t in range(NT)]

            def gate_up(s):
                c, t = steps[s]
                n = NL_FFN0 + c
                if t == 0:
                    pe.wait_ge(*full(n))
                if s < NT:
                    pe.wait_ge(hT_done, s + 1)
                if s >= 2:
                    pe.wait_ge(f_hid, s - 1)
                w = slot(n)[:, 0:2 * KD * FC].rearrange("p (k c) -> p k c", k=KD)
                group(ps[:, 4 + s % 2, :], [(h_T[:, k, tok(t)], w[:, k, :]) for k in range(KD)]).then_inc(f_gu, 1)

            gate_up(0)
            for s, (c, t) in enumerate(steps):
                if s + 1 < len(steps):
                    gate_up(s + 1)
                pe.wait_ge(f_hid, s + 1)
                for j in range(2):
                    last = tr(ps[:, 6 + s % 2, j * P:(j + 1) * P], hid[:, s % 2, j * P:(j + 1) * P], ident[:])
                last.then_inc(f_tr, 1)
                pe.wait_ge(f_hT, s + 1)
                w = slot(NL_FFN0 + c)[:, 2 * KD * FC:].rearrange("p (j c) -> p j c", j=2)
                for j in range(2):
                    for f in range(2):
                        last = mm(ps[:, 2 * t + f, :], hid_T[:, s % 2, j, :], w[:, j, f * 512:(f + 1) * 512],
                                  start=(c == 0 and j == 0), stop=(c == NC - 1 and j == 1))
                if t == NT - 1:
                    last.then_inc(slots_used, 1)
            for t in range(NT):
                to_channel_major(t, 1, 4)
            n = NL_KVQ
            KQ = KVL + ROPE + QL
            pe.wait_ge(*full(n))
            w = slot(n)[:, 0:KD * KQ].rearrange("p (k c) -> p k c", k=KD)
            for t in range(NT):
                pe.wait_ge(hT_done, NT + t + 1)
                group(ps[:, 2 * t, 0:KVL + ROPE], [(h_T[:, k, tok(t)], w[:, k, 0:KVL + ROPE]) for k in range(KD)])
                group(ps[:, 2 * t + 1, 0:QL], [(h_T[:, k, tok(t)], w[:, k, KVL + ROPE:]) for k in range(KD)])\
                    .then_inc(kq_mm, 1)
            for t in range(NT):
                pe.wait_ge(kq_done, t + 1)
                for j in range(2):
                    tr(ps[:, 4 + 2 * t, j * P:(j + 1) * P], ckv_n[:, t, j * P:(j + 1) * P], ident[:])
                tr(ps[0:ROPE, 4 + 2 * t, 2 * P:3 * P], k_rot[:, t, :], ident[:])
                for j in range(3):
                    last = tr(ps[:, 5 + 2 * t, j * P:(j + 1) * P], q_n[:, t, j * P:(j + 1) * P], ident[:])
                last.then_inc(kq_tr, 1)
            pe.wait_ge(kqT_done, NT)
            pe.wait_ge(*full(NL_KVQ + 1))
            pe.wait_ge(*full(NL_KVQ + 2))
            wk = slot(NL_KVQ + 1)[:, 0:2 * AH * (NOPE + VD)].rearrange("p (k c) -> p k c", k=2)
            wq = slot(NL_KVQ + 2)[:, 0:3 * AH * (NOPE + ROPE)].rearrange("p (k c) -> p k c", k=3)
            for h in range(AH):
                if h >= 4:
                    pe.wait_ge(nope_done, h - 3)
                group(ps[:, h % 4, 0:SEQ], [(wk[:, k, h * NOPE:(h + 1) * NOPE], ckv_T[:, k, :]) for k in range(2)])
                group(ps[:, h % 4, SEQ:2 * SEQ], [(wq[:, k, h * NOPE:(h + 1) * NOPE], q_T[:, k, :])
                                                  for k in range(3)]).then_inc(nope_mm, 1)
            for t in range(NT):
                for f in range(2):
                    last = group(ps[:, 4 + 2 * t + f, :],
                                 [(ckv_T[:, k, tok(t)], wk[:, k, AH * NOPE + f * 512:AH * NOPE + (f + 1) * 512])
                                  for k in range(2)])
                last.then_inc(v_mm, 1)
            pe.wait_ge(nope_done, AH)
            for t in range(NT):
                group(ps[:, t, :], [(q_T[:, k, tok(t)], wq[:, k, AH * NOPE:]) for k in range(3)]).then_inc(qr_mm, 1)
            for t in range(NT):
                pe.wait_ge(qrot_done, t + 1)
                pe.wait_ge(v_done, t + 1)
                for h in range(AH):
                    last = tr(ps[0:ROPE, 4 + 2 * t + h // 4, (h % 4) * P:(h % 4 + 1) * P],
                              q_rot[:, t, h * ROPE:(h + 1) * ROPE], ident[:])
                last.then_inc(qr_tr, 1)

            NA = AH * NT

            def scores(a):
                h, t = divmod(a, NT)
                if a >= 2:
                    pe.wait_ge(max_done, a - 1)
                nk = (t + 1) * P
                mm(ps[:, a % 2, 0:nk], qn_T[:, h, tok(t)], kn_T[:, h, 0:nk], start=True, stop=False)
                mm(ps[:, a % 2, 0:nk], qr_T[0:ROPE, h, tok(t)], kr_T[0:ROPE, 0:nk], start=False, stop=True)\
                    .then_inc(sc_mm, 1)

            pe.wait_ge(qrT_done, NT)
            scores(0)
            scores(1)
            for a in range(NA):
                h, t = divmod(a, NT)
                pe.wait_ge(prob_done, a + 1)
                for j in range(t + 1):
                    last = tr(ps[:, 2 + a % 2, j * P:(j + 1) * P], prob[:, a % 4, j * P:(j + 1) * P], ident[:])
                last.then_inc(prob_tr, 1)
                if a + 2 < NA:
                    scores(a + 2)
                pe.wait_ge(probT_done, a + 1)
                if a >= 2:
                    pe.wait_ge(o_done, a - 1)
                group(ps[:, 4 + a % 2, 0:P], [(v_tok[:, j, h * VD:(h + 1) * VD], prob_T[:, a % 2, j, :])
                                              for j in range(t + 1)]).then_inc(o_mm, 1)
            pe.wait_ge(o_done, NA)
            for q in range(2):
                n = NL_KVQ + 3 + q
                pe.wait_ge(*full(n))
                w = slot(n)[:, 0:4 * D].rearrange("p (k c) -> p k c", k=4)
                for j in range(4):
                    h = 4 * q + j
                    for t in range(NT):
                        for f in range(2):
                            last = mm(ps[:, 4 + 2 * t + f, :], o_T[:, h, tok(t)], w[:, j, f * 512:(f + 1) * 512],
                                      start=(h == 0), stop=(h == AH - 1))
                last.then_inc(slots_used, 1)
            for t in range(NT):
                to_channel_major(t, 2, 0)
            for t in range(NT):
                pe.wait_ge(hT_done, 2 * NT + t + 1)
                last = group(ps[:, 4, t * NE:(t + 1) * NE], [(h_T[:, k, tok(t)], w_rt[:, k, :]) for k in range(KD)])
            last.then_inc(rt_mm, 1)
            pe.wait_ge(chosen_done, 1)
            mm(ps[:, 5, 0:NE], stri[:], chosen[:, 0, :], start=True, stop=True)
            group(ps[:, 5, NE:2 * NE], [(stri[:], chosen[:, 1, :]), (ones[:], chosen[:, 0, :])])
            mm(ps[:, 5, 2 * NE:3 * NE], ones[:], chosen_sum[:], start=True, stop=True).then_inc(pos_mm, 1)

            def gather(i):
                pe.wait_ge(m_pick, i + 1)
                for k in range(KD):
                    last = group(ps[:, 2 + k // 4, (k % 4) * P:(k % 4 + 1) * P],
                                 [(h_tok[:, t, k * P:(k + 1) * P], pick[:, t, :]) for t in range(NT)])
                last.then_inc(m_gat, 1)

            def scatter(i):
                pe.wait_ge(m_yec, i)
                pe.wait_ge(m_scat, i)
                for j in range(4):
                    t, f = divmod(j, 2)
                    if j >= 2:
                        pe.wait_ge(m_acc, i * 4 + (j - 1))
                    mm(ps[:, 2 + j % 2, :], scat[:, t, :], y_e[:, f, :], start=True, stop=True).then_inc(m_sc, 1)

            gather(0)
            n_extra = pe.value_load(ctl[0:1, 0:1], min_val=0, max_val=MAX_EXTRA)
            n_items = pe.snap(n_extra + NE)
            pe.wait_ge(moe_zero, 3)
            with pe.Fori(0, n_items) as i:
                def gate_up_moe(s):
                    pe.wait_ge(*full_moe(i, s))
                    if s >= 2:
                        pe.wait_ge(m_hid, i * NC + (s - 1))
                    w = slot(s)[:, 0:2 * KD * FC].rearrange("p (k c) -> p k c", k=KD)
                    group(ps[:, 4 + s % 2, :], [(xe_T[:, k, :], w[:, k, :]) for k in range(KD)]).then_inc(m_gu, 1)

                def down_moe(s):
                    pe.wait_ge(m_hid, i * NC + (s + 1))
                    for j in range(2):
                        last = tr(ps[:, 6 + s % 2, j * P:(j + 1) * P], hid[:, s % 2, j * P:(j + 1) * P], ident[:])
                    last.then_inc(m_tr, 1)
                    pe.wait_ge(m_hT, i * NC + (s + 1))
                    if s == 0:
                        pe.wait_ge(m_yec, i)
                    w = slot(s)[:, 2 * KD * FC:].rearrange("p (j c) -> p j c", j=2)
                    for j in range(2):
                        for f in range(2):
                            last = mm(ps[:, f, :], hid_T[:, s % 2, j, :], w[:, j, f * 512:(f + 1) * 512],
                                      start=(s == 0 and j == 0), stop=(s == NC - 1 and j == 1))
                    last.then_inc(slots_used, 1)

                pe.wait_ge(m_xeA, i + 1)
                pe.wait_ge(m_xeV, i + 1)
                gate_up_moe(0)
                scatter(i)
                pe.wait_ge(m_acc, i * 4 + 4)
                for t in range(NT):
                    last = tr(ps[:, 2, t * P:(t + 1) * P], pick_g[:, t, :], ident[:])
                last.then_inc(m_str, 1)
                for s in range(NC - 1):
                    gate_up_moe(s + 1)
                    down_moe(s)
                pe.wait_ge(m_scat, i + 1)
                gather(i + 1)
                down_moe(NC - 1)
            scatter(n_items)

        @block.scalar
        def _(act):
            A = nc.scalar.activation
            act.wait_ge(small_in, 16 * 5)
            A(exp_a[:], a_log, ACT.Exp).then_inc(dt_exp, 1)
            act.wait_ge(dt_abs, 1)
            A(dt_e[:], dt_s[:], ACT.Exp).then_inc(dt_exp, 1)
            for m in range(NM):
                act.wait_ge(conv_done, m + 1)
                A(xbc_T[:, m, :], conv_acc[:, m % 2, :], ACT.Silu).then_inc(xbc_done, 1)
                if m == 1:
                    act.wait_ge(ang_done, 2)
                    A(sin_t[:], ang_r[:], ACT.Sin).then_inc(trig_done, 1)
                    A(cos_t[:], ang_c[:], ACT.Sin).then_inc(trig_done, 1)
            act.wait_ge(cum_ready, 1)
            A(decay_end[:], to_end[:], ACT.Exp).then_inc(decays, 1)
            A(decay_cum[:], cum[:, NH:], ACT.Exp).then_inc(decays, 1)
            def z_silu(u):
                g, t = divmod(u, NT)
                act.wait_ge(z_mm, u + 1)
                A(z_gate[:, t, g, :], ps[:, 5 if u % 2 == 0 else 3, :], ACT.Silu).then_inc(z_done, 1)

            def head_decays(u):
                g, t = divmod(u, NT)
                for b in range(2):
                    act.wait_ge(bc_mm, 2 * u + b + 1)
                    if u >= 1:
                        act.wait_ge(mix_done, 2 * u + b - 1)
                    for j in range(4):
                        h = t * NH + g * HG + b * 4 + j
                        last = A(decay[:, b, j, :], ps[:, 6 + b, j * P:(j + 1) * P], ACT.Relu,
                                 bias=cum[:, h:h + 1], scale=-1.0)
                    last.then_inc(relu_done, 1)
                for b in range(2):
                    act.wait_ge(relu_done, 2 * u + b + 1)
                    A(decay[:, b, :, :], decay[:, b, :, :], ACT.Exp, scale=-1.0).then_inc(dec_done, 1)

            def y_square(u):
                g, t = divmod(u, NT)
                act.wait_ge(y_done, u + 1)
                if u >= 1:
                    act.wait_ge(sq_done, u)
                A(y_sq, z_gate[:, t, g, :], ACT.Square, accum_out=sq_sum[:, u:u + 1]).then_inc(sq_done, 1)

            def y_channel_major(u):
                g, t = divmod(u, NT)
                act.wait_ge(yt_mm, u + 1)
                for j in range(4):
                    m = g * 4 + j
                    last = A(xbc_T[:, m, t * P:(t + 1) * P], ps[:, 2, j * P:(j + 1) * P], ACT.Copy,
                             scale=gains[:, m:m + 1])
                last.then_inc(yt_done, 1)

            NU = NG * NT
            act.wait_ge(btr_mm, 1)
            A(b_tok, ps[:, 4, :].rearrange("p (g c) -> p g c", g=NG), ACT.Copy).then_inc(b_done, 1)
            z_silu(0)
            head_decays(0)
            for u in range(NU):
                g, t = divmod(u, NT)
                if u + 1 < NU:
                    z_silu(u + 1)
                if t == 0:
                    act.wait_ge(st_mm, g + 1)
                    A(state[:, g % 2, :], ps[:, 1, :], ACT.Copy).then_inc(st_done, 1)
                if u + 1 < NU:
                    head_decays(u + 1)
                y_square(u)
                if u >= 1:
                    y_channel_major(u - 1)
            y_channel_major(NU - 1)

            def evacuate_h(t, ln, bank):
                act.wait_ge(ln_tr, ln * NT + t + 1)
                for b in range(2):
                    last = A(h_T[:, 4 * b:4 * b + 4, t * P:(t + 1) * P],
                             ps[:, bank + 2 * t + b, :].rearrange("p (k c) -> p k c", k=4), ACT.Copy)
                last.then_inc(hT_done, 1)

            for t in range(NT):
                evacuate_h(t, 0, 0)
            def hid_transposed(s):
                act.wait_ge(f_tr, s + 1)
                A(hid_T[:, s % 2, :, :], ps[:, 6 + s % 2, 0:2 * P].rearrange("p (j c) -> p j c", j=2), ACT.Copy)\
                    .then_inc(f_hT, 1)

            for s in range(NC * NT):
                act.wait_ge(f_gu, s + 1)
                A(sil[:, s % 2, :], ps[:, 4 + s % 2, 0:FC], ACT.Silu).then_inc(f_silu, 1)
                if s >= 1:
                    hid_transposed(s - 1)
            hid_transposed(NC * NT - 1)
            for t in range(NT):
                evacuate_h(t, 1, 4)
            for t in range(NT):
                act.wait_ge(kq_mm, t + 1)
                if t:
                    act.wait_ge(kq_sq, 2 * t)
                A(sq_junk[:, 0:KVL], ps[:, 2 * t, 0:KVL], ACT.Square, accum_out=kq_ss[:, t, 0:1]).then_inc(kq_sq, 1)
                act.wait_ge(kq_sq, 2 * t + 1)
                A(sq_junk[:, 0:QL], ps[:, 2 * t + 1, 0:QL], ACT.Square, accum_out=kq_ss[:, t, 1:2]).then_inc(kq_sq, 1)
            for t in range(NT):
                act.wait_ge(kq_tr, t + 1)
                s_ = slice(t * P, (t + 1) * P)
                for j in range(2):
                    A(ckv_T[:, j, s_], ps[:, 4 + 2 * t, j * P:(j + 1) * P], ACT.Copy, scale=gains[:, MX + j:MX + j + 1])
                A(kr_T[0:ROPE, s_], ps[0:ROPE, 4 + 2 * t, 2 * P:3 * P], ACT.Copy)
                for j in range(3):
                    last = A(q_T[:, j, s_], ps[:, 5 + 2 * t, j * P:(j + 1) * P], ACT.Copy,
                             scale=gains[:, MX + 2 + j:MX + 3 + j])
                last.then_inc(kqT_done, 1)
            for h in range(AH):
                act.wait_ge(nope_mm, h + 1)
                A(kn_T[:, h, :], ps[:, h % 4, 0:SEQ], ACT.Copy)
                A(qn_T[:, h, :], ps[:, h % 4, SEQ:], ACT.Copy).then_inc(nope_done, 1)
            for t in range(NT):
                act.wait_ge(qr_tr, t + 1)
                for b in range(2):
                    last = A(qr_T[0:ROPE, 4 * b:4 * b + 4, t * P:(t + 1) * P],
                             ps[0:ROPE, 4 + 2 * t + b, :].rearrange("p (h c) -> p h c", h=4), ACT.Copy)
                last.then_inc(qrT_done, 1)

            def softmax_exp(a):
                nk = (a % NT + 1) * P
                act.wait_ge(max_done, a + 1)
                A(prob[:, a % 4, 0:nk], prob[:, a % 4, 0:nk], ACT.Exp, bias=negm[:, a:a + 1], scale=SCALE,
                  accum_out=psum_row[:, a:a + 1]).then_inc(exp_done, 1)

            softmax_exp(0)
            for a in range(AH * NT):
                if a + 1 < AH * NT:
                    softmax_exp(a + 1)
                act.wait_ge(prob_tr, a + 1)
                if a >= 2:
                    act.wait_ge(o_mm, a - 1)
                nk = a % NT + 1
                A(prob_T[:, a % 2, 0:nk, :], ps[:, 2 + a % 2, 0:nk * P].rearrange("p (j c) -> p j c", j=nk), ACT.Copy)\
                    .then_inc(probT_done, 1)
            for t in range(NT):
                evacuate_h(t, 2, 0)
            act.wait_ge(gap_done, 1)
            A(gap_e[:], gap[:], ACT.Exp).then_inc(gap_exp, 1)

            def expert_rows(i):
                act.wait_ge(m_gat, i + 1)
                A(xe_T[:, 0:4, :], ps[:, 2, :].rearrange("p (k c) -> p k c", k=4), ACT.Copy).then_inc(m_xeA, 1)

            expert_rows(0)
            act.wait_ge(route_done, 1)
            n_extra = act.value_load(ctl[0:1, 0:1], min_val=0, max_val=MAX_EXTRA)
            n_items = act.snap(n_extra + NE)
            with act.Fori(0, n_items) as i:
                def silu_moe(s):
                    act.wait_ge(m_gu, i * NC + (s + 1))
                    A(sil[:, s % 2, :], ps[:, 4 + s % 2, 0:FC], ACT.Silu).then_inc(m_silu, 1)

                def hid_T_moe(s):
                    act.wait_ge(m_tr, i * NC + (s + 1))
                    A(hid_T[:, s % 2, :, :], ps[:, 6 + s % 2, 0:2 * P].rearrange("p (j c) -> p j c", j=2), ACT.Copy)\
                        .then_inc(m_hT, 1)

                silu_moe(0)
                act.wait_ge(m_str, i + 1)
                A(scat[:], ps[:, 2, 0:2 * P].rearrange("p (t c) -> p t c", t=NT), ACT.Copy).then_inc(m_scat, 1)
                for s in range(NC - 1):
                    silu_moe(s + 1)
                    hid_T_moe(s)
                expert_rows(i + 1)
                hid_T_moe(NC - 1)

        @block.vector
        def _(dve):
            V = nc.vector
            TS, TT, STT = V.tensor_scalar, V.tensor_tensor, V.scalar_tensor_tensor
            chain = Count()

            def step(ins):
                ins.then_inc(dve_step, 1)
                dve.wait_ge(dve_step, chain.up())

            def heads(ap, n=HG, w=HD):
                return ap.unsqueeze(2).broadcast_to([P, n, w])

            def by_head(ap, n=HG):
                return ap.rearrange("p (h w) -> p h w", h=n)

            dve.wait_ge(small_in, 16 * 5)
            dve.wait_ge(dt_mm, 1)
            step(TT(dt_v[:].rearrange("p (t h) -> p t h", t=NT), ps[:, 4, 0:NT * NH].rearrange("p (t h) -> p t h", t=NT),
                    dt_bias.unsqueeze(1).broadcast_to([P, NT, NH]), ALU.add))
            STT(dt_s[:], dt_v[:], -1.0, dt_v[:], ALU.mult, ALU.min).then_inc(dt_abs, 1)
            dve.wait_ge(dt_exp, 2)
            step(TS(dt_q[:], dt_e[:], 2.0, None, ALU.add))
            step(V.reciprocal(dt_q[:], dt_q[:]))
            step(TT(dt_s[:], dt_e[:], dt_q[:], ALU.mult))
            step(TT(dt_q[:], dt_s[:], dt_s[:], ALU.mult))
            step(TS(dt_p[:], dt_q[:], 1.0 / 17, None, ALU.mult))
            for k in (15, 13, 11, 9, 7, 5, 3):
                step(STT(dt_p[:], dt_p[:], 1.0 / k, dt_q[:], ALU.add, ALU.mult))
            step(STT(dt_p[:], dt_p[:], 1.0, dt_s[:], ALU.add, ALU.mult))
            step(TS(dt_v[:], dt_v[:], 0.0, None, ALU.max))
            step(STT(dt[:], dt_p[:], 2.0, dt_v[:], ALU.mult, ALU.add))
            STT(la[:].rearrange("p (t h) -> p t h", t=NT), dt[:].rearrange("p (t h) -> p t h", t=NT), -1.0,
                exp_a[:].unsqueeze(1).broadcast_to([P, NT, NH]), ALU.mult, ALU.mult).then_inc(la_ready, 1)

            def rope_angles():
                step(V.tensor_copy(pos_f[:], pos_i[:]))
                step(TT(ang[:], pos_f[:].unsqueeze(2).broadcast_to([P, NT, HR]),
                        inv_freq.unsqueeze(1).broadcast_to([P, NT, HR]), ALU.mult))
                for quarter, dst in ((0.0, ang_r), (0.25, ang_c)):
                    step(TS(ang_k[:], ang[:], 1 / (2 * math.pi), quarter, ALU.mult, ALU.add))
                    step(TS(ang_k[:], ang_k[:], MAGIC, None, ALU.add))
                    step(TS(ang_k[:], ang_k[:], MAGIC, None, ALU.subtract))
                    step(STT(dst[:], ang_k[:], -TWO_PI_1, ang[:], ALU.mult, ALU.add))
                    step(STT(dst[:], ang_k[:], -TWO_PI_2, dst[:], ALU.mult, ALU.add))
                    step(STT(dst[:], ang_k[:], -TWO_PI_3, dst[:], ALU.mult, ALU.add))
                    step(TS(dst[:], dst[:], quarter * 2 * math.pi, PI_IN, ALU.add, ALU.min))
                    TS(dst[:], dst[:], -PI_IN, None, ALU.max).then_inc(ang_done, 1)

            for m in range(NM):
                dve.wait_ge(xbc_mm, m + 1)
                if m >= 2:
                    dve.wait_ge(xbc_done, m - 1)
                acc, src = conv_acc[:, m % 2, :], ps[:, m % 4, 0:SEQ]
                step(TS(acc, src, conv_wb[:, m, 3:4], conv_wb[:, m, 4:5], ALU.mult, ALU.add))
                for b in (1, 2, 3):
                    ins = STT(acc[:, b:], src[:, 0:SEQ - b], conv_wb[:, m, 3 - b:4 - b], acc[:, b:], ALU.mult, ALU.add)
                    if b < 3:
                        step(ins)
                ins.then_inc(conv_done, 1)
                if m == 1:
                    rope_angles()
                if m == 9:
                    dve.wait_ge(cum_mm, 1)
                    step(V.tensor_copy(cum[:], ps[:, 5, 0:NT * NH]))
                    TT(to_end[:], ps[:, 5, NT * NH:NT * NH + NH], cum[:, 0:NH], ALU.subtract).then_inc(cum_ready, 1)
            dve.wait_ge(cb_mm, 1)
            for t in range(NT):
                last = TT(cb_mask[:, t * NG:(t + 1) * NG, :], ps[:, 2 + t, :].rearrange("p (g c) -> p g c", g=NG),
                          tri[:].unsqueeze(1).broadcast_to([P, NG, P]), ALU.mult)
            last.then_inc(cb_done, 1)
            dve.wait_ge(decays, 2)

            def scaled_x(u):
                g, t = divmod(u, NT)
                hs = slice(g * HG, (g + 1) * HG)
                dve.wait_ge(xs_tr, u + 1)
                if u >= 2:
                    dve.wait_ge(yd_mm, u - 1)
                TT(by_head(x_skip[:, u % 2, :]), by_head(ps[:, 0, :]), heads(d_skip[:, hs]), ALU.mult)
                ins = TT(by_head(x_dt[:, u % 2, :]), by_head(ps[:, 0, :]),
                         heads(dt[:, t * NH + g * HG:t * NH + (g + 1) * HG]), ALU.mult)
                if t == 0:
                    step(ins)
                    ins = TT(by_head(x_end[:]), by_head(x_dt[:, u % 2, :]), heads(decay_end[:, hs]), ALU.mult)
                ins.then_inc(x_done, 1)

            NU = NG * NT
            scaled_x(0)
            for u in range(NU):
                g, t = divmod(u, NT)
                for b in range(2):
                    dve.wait_ge(dec_done, 2 * u + b + 1)
                    if u >= 1:
                        dve.wait_ge(yd_mm, u)
                    TT(mix_T[:, b, :, :], decay[:, b, :, :],
                       cb_mask[:, t * NG + g:t * NG + g + 1, :].broadcast_to([P, 4, P]), ALU.mult).then_inc(mix_done, 1)
                if u + 1 < NU:
                    scaled_x(u + 1)
                dve.wait_ge(yd_mm, u + 1)
                skip = x_skip[:, u % 2, :]
                step(TT(skip, ps[:, 4, :], skip, ALU.add))
                if t == 1:
                    dve.wait_ge(yoff_mm, g + 1)
                    step(TT(by_head(y_tmp[:]), by_head(ps[:, 1, :]), heads(decay_cum[:, g * HG:(g + 1) * HG]), ALU.mult))
                    step(TT(skip, skip, y_tmp[:], ALU.add))
                dve.wait_ge(z_done, u + 1)
                y = z_gate[:, t, g, :]
                TT(y, y, skip, ALU.mult).then_inc(y_done, 1)
                dve.wait_ge(sq_done, u + 1)
                TS(pow_in_t[:, u, 0:1], sq_sum[:, u:u + 1], 1.0 / GW, LN_EPS, ALU.mult, ALU.add).then_inc(pow_go, 1)
                dve.wait_ge(pow_ok, u + 1)
                TS(y, y, pow_out_t[:, u, 0:1], None, ALU.mult).then_inc(yn_done, 1)

            jobs = Count()
            jobs.n = NU

            def layer_norm(ln, added):
                job = jobs.n
                jobs.up(NT)
                for t in range(NT):
                    if added:
                        for f in range(2):
                            hs = h_tok[:, t, f * 512:(f + 1) * 512]
                            ins = STT(hs, hs, ALPHA, added(t, f), ALU.mult, ALU.add)
                            step(ins)
                    src = h_tok if added else moe_acc
                    for f in range(2):
                        ins = V.bn_stats(bn[:, f, :], src[:, t, f * 512:(f + 1) * 512])
                        if f:
                            step(ins)
                    step(V.bn_aggr(mv[:, t, :], bn[:]))
                    TS(pow_in_t[:, job + t, 0:1], mv[:, t, 1:2], LN_EPS, None, ALU.add).then_inc(pow_go, 1)
                dve.wait_ge(gb_in, 16 * (ln + 1))
                for t in range(NT):
                    hs = h_tok[:, t, :]
                    dve.wait_ge(pow_ok, job + t + 1)
                    step(TS(hs, (h_tok if added else moe_acc)[:, t, :], mv[:, t, 0:1], pow_out_t[:, job + t, 0:1],
                            ALU.subtract, ALU.mult))
                    step(TT(hs, hs, ln_gb[:, 0:D], ALU.mult))
                    TT(hs, hs, ln_gb[:, D:], ALU.add).then_inc(ln_done, 1)

            dve.wait_ge(x_in, 16)
            dve.wait_ge(slots_used, USED_WO)
            layer_norm(0, lambda t, f: ps[:, 4 + 2 * t + f, :])
            for s in range(NC * NT):
                dve.wait_ge(f_silu, s + 1)
                TT(hid[:, s % 2, :], sil[:, s % 2, :], ps[:, 4 + s % 2, FC:], ALU.mult).then_inc(f_hid, 1)
            dve.wait_ge(slots_used, USED_FFN)
            layer_norm(1, lambda t, f: ps[:, 2 * t + f, :])
            def rotate(dst, src, t, n):
                x = src.rearrange("p (h c) -> p h c", h=n)
                y = dst.rearrange("p (h c) -> p h c", h=n)
                c = cos_t[:, t:t + 1, :].broadcast_to([P, n, HR])
                s = sin_t[:, t:t + 1, :].broadcast_to([P, n, HR])
                ra = rot_a[:, 0:n * HR].rearrange("p (h c) -> p h c", h=n)
                rb = rot_b[:, 0:n * HR].rearrange("p (h c) -> p h c", h=n)
                TT(ra, x[:, :, 0:HR], c, ALU.mult)
                step(TT(rb, x[:, :, HR:], s, ALU.mult))
                step(TT(y[:, :, 0:HR], ra, rb, ALU.subtract))
                TT(ra, x[:, :, HR:], c, ALU.mult)
                step(TT(rb, x[:, :, 0:HR], s, ALU.mult))
                return TT(y[:, :, HR:], ra, rb, ALU.add)

            dve.wait_ge(trig_done, 2)
            job = jobs.n
            jobs.up(NT)
            for t in range(NT):
                dve.wait_ge(kq_sq, 2 * t + 2)
                TS(pow_in_t[:, job + t, 0:1], kq_ss[:, t, 0:1], 1.0 / KVL, RMS_EPS, ALU.mult, ALU.add)
                TS(pow_in_t[:, job + t, 1:2], kq_ss[:, t, 1:2], 1.0 / QL, RMS_EPS, ALU.mult, ALU.add).then_inc(pow_go, 1)
                step(rotate(k_rot[:, t, :], ps[:, 2 * t, KVL:KVL + ROPE], t, 1))
                dve.wait_ge(pow_ok, job + t + 1)
                TS(ckv_n[:, t, :], ps[:, 2 * t, 0:KVL], pow_out_t[:, job + t, 0:1], None, ALU.mult)
                TS(q_n[:, t, :], ps[:, 2 * t + 1, 0:QL], pow_out_t[:, job + t, 1:2], None, ALU.mult).then_inc(kq_done, 1)
            for t in range(NT):
                dve.wait_ge(v_mm, t + 1)
                for f in range(2):
                    last = V.tensor_copy(v_tok[:, t, f * 512:(f + 1) * 512], ps[:, 4 + 2 * t + f, :])
                last.then_inc(v_done, 1)
            for t in range(NT):
                dve.wait_ge(qr_mm, t + 1)
                ins = rotate(q_rot[:, t, :], ps[:, t, :], t, AH)
                ins.then_inc(qrot_done, 1)
                dve.wait_ge(qrot_done, t + 1)

            NA = AH * NT

            def masked_max(a):
                t = a % NT
                nk = (t + 1) * P
                dve.wait_ge(sc_mm, a + 1)
                if a >= 4:
                    dve.wait_ge(prob_tr, a - 3)
                step(V.tensor_tensor_reduce(out=prob[:, a % 4, 0:nk], in0=ps[:, a % 2, 0:nk],
                                            in1=causal_add[:, 2 * P - nk:], scale=1.0, scalar=NEG * 2,
                                            op0=ALU.add, op1=ALU.max, accum_out=mx[:, a:a + 1]))
                TS(negm[:, a:a + 1], mx[:, a:a + 1], -SCALE, None, ALU.mult).then_inc(max_done, 1)

            def out_T(a):
                h, t = divmod(a, NT)
                dve.wait_ge(o_mm, a + 1)
                V.tensor_copy(o_T[:, h, t * P:(t + 1) * P], ps[:, 4 + a % 2, 0:P]).then_inc(o_done, 1)

            masked_max(0)
            for a in range(NA):
                if a + 1 < NA:
                    masked_max(a + 1)
                nk = (a % NT + 1) * P
                dve.wait_ge(exp_done, a + 1)
                step(V.reciprocal(rinv[:, a:a + 1], psum_row[:, a:a + 1]))
                TS(prob[:, a % 4, 0:nk], prob[:, a % 4, 0:nk], rinv[:, a:a + 1], None, ALU.mult).then_inc(prob_done, 1)
                if a >= 1:
                    out_T(a - 1)
            out_T(NA - 1)
            dve.wait_ge(slots_used, USED_MLA)
            layer_norm(2, lambda t, f: ps[:, 4 + 2 * t + f, :])
            V.memset(scat[:], 0.0).then_inc(moe_zero, 1)
            V.memset(y_e[:], 0.0).then_inc(moe_zero, 1)
            dve.wait_ge(ln_done, 3 * NT)
            TS(moe_acc[:], h_tok[:], ALPHA, None, ALU.mult).then_inc(moe_zero, 1)

            dve.wait_ge(rt_mm, 1)
            step(TT(logits[:], ps[:, 4, 0:NT * NE].rearrange("p (t e) -> p t e", t=NT),
                    b_rt.unsqueeze(1).broadcast_to([P, NT, NE]), ALU.add))
            for t in range(NT):
                step(V.max(top_v[:, t, :], logits[:, t, :]))
                step(V.max_index(top_i[:, t, :], top_v[:, t, :], logits[:, t, :]))
            step(V.tensor_copy(top_f[:], top_i[:, :, 0:2]))
            TT(gap[:], top_v[:, :, 1], top_v[:, :, 0], ALU.subtract).then_inc(gap_done, 1)
            for k in range(2):
                for t in range(NT):
                    ins = TS(one_hot[:, k, t, :], slot_iota[:, 0:NE], top_f[:, t, k:k + 1], None, ALU.is_equal)
            step(ins)
            step(TT(chosen[:], one_hot[:, 0, :, :], one_hot[:, 1, :, :], ALU.add))
            TT(chosen_sum[:], chosen[:, 0, :], chosen[:, 1, :], ALU.add).then_inc(chosen_done, 1)
            dve.wait_ge(gap_exp, 1)
            step(TS(den[:], gap_e[:], 1.0, None, ALU.add))
            step(V.reciprocal(w_top[:, 0, :], den[:]))
            step(TT(w_top[:, 1, :], gap_e[:], w_top[:, 0, :], ALU.mult))
            for t in range(NT):
                step(TS(gates[:, t, :], one_hot[:, 0, t, :], w_top[:, 0, t:t + 1], None, ALU.mult))
                step(STT(gates[:, t, :], one_hot[:, 1, t, :], w_top[:, 1, t:t + 1], gates[:, t, :], ALU.mult, ALU.add))
            dve.wait_ge(pos_mm, 1)
            step(STT(posm[:], ps[:, 5, 0:NT * NE].rearrange("p (t e) -> p t e", t=NT), 1.0, chosen[:], ALU.add, ALU.mult))
            step(TS(posm[:], posm[:], -1.0, None, ALU.add))
            dve.wait_ge(consts, CONSTS)
            V.tensor_copy(slot_tab[:, :, 0:NE], posm[:])
            V.tensor_copy(gate_tab[:, :, 0:NE], gates[:])
            step(TS(over[:], ps[:, 5, 2 * NE:3 * NE], float(P), None, ALU.is_gt))
            step(TT(rank_in[:], before[:], over[:].unsqueeze(1).broadcast_to([P, NE, NE]), ALU.mult))
            step(V.tensor_reduce(rank[:], rank_in[:], axis=AX.X, op=ALU.add))
            V.tensor_reduce(ctl_f[:, 0:1], over[:], axis=AX.X, op=ALU.add)
            for k in range(MAX_EXTRA):
                step(STT(sel[:, k, :], rank[:], float(k), over[:], ALU.is_equal, ALU.mult))
                step(TT(rank_in[:, 0, :], sel[:, k, :], slot_iota[:, 0:NE], ALU.mult))
                step(V.tensor_reduce(ctl_f[:, k + 1:k + 2], rank_in[:, 0, :], axis=AX.X, op=ALU.add))
                s = sel[:, k, :].unsqueeze(1).broadcast_to([P, NT, NE])
                step(STT(sel_in[:], posm[:], -float(P), s, ALU.add, ALU.mult))
                step(V.tensor_reduce(slot_tab[:, :, NE + k], sel_in[:], axis=AX.X, op=ALU.add))
                step(TT(sel_in[:], gates[:], s, ALU.mult))
                step(V.tensor_reduce(gate_tab[:, :, NE + k], sel_in[:], axis=AX.X, op=ALU.add))
            V.tensor_copy(ctl[:], ctl_f[:]).then_inc(route_done, 1)

            def picks(i):
                for t in range(NT):
                    TS(pick[:, t, :], slot_iota[:], slot_tab[:, t, bass.ds(i, 1)], None, ALU.is_equal)
                for t in range(NT):
                    ins = TS(pick_g[:, t, :], slot_iota[:], slot_tab[:, t, bass.ds(i, 1)],
                             gate_tab[:, t, bass.ds(i, 1)], ALU.is_equal, ALU.mult)
                ins.then_inc(m_pick, 1)

            def expert_rows(i):
                dve.wait_ge(m_gat, i + 1)
                V.tensor_copy(xe_T[:, 4:8, :], ps[:, 3, :].rearrange("p (k c) -> p k c", k=4)).then_inc(m_xeV, 1)

            def accumulate(i):
                for j in range(4):
                    t, f = divmod(j, 2)
                    dve.wait_ge(m_sc, i * 4 + (j + 1))
                    a = moe_acc[:, t, f * 512:(f + 1) * 512]
                    TT(a, ps[:, 2 + j % 2, :], a, ALU.add).then_inc(m_acc, 1)

            dve.wait_ge(route_done, 1)
            picks(0)
            expert_rows(0)
            n_extra = dve.value_load(ctl[0:1, 0:1], min_val=0, max_val=MAX_EXTRA)
            n_items = dve.snap(n_extra + NE)
            dve.wait_ge(moe_zero, 3)
            with dve.Fori(0, n_items) as i:
                def hidden(s):
                    dve.wait_ge(m_silu, i * NC + (s + 1))
                    TT(hid[:, s % 2, :], sil[:, s % 2, :], ps[:, 4 + s % 2, FC:], ALU.mult).then_inc(m_hid, 1)

                hidden(0)
                accumulate(i)
                dve.wait_ge(m_str, i + 1)
                picks(i + 1)
                for s in range(1, NC):
                    hidden(s)
                expert_rows(i + 1)
                dve.wait_ge(slots_used, i * NC + (USED_MLA + NC))
                for f in range(2):
                    ins = V.tensor_copy(y_e[:, f, :], ps[:, f, :])
                ins.then_inc(m_yec, 1)
            accumulate(n_items)
            dve.wait_ge(m_acc, n_items * 4 + 4)
            layer_norm(3, None)


def kernel(**inputs):
    import numpy as np
    import concourse.bacc as bacc
    from concourse.bass_utils import run_bass_kernel_spmd

    a = {k: np.asarray(v) for k, v in inputs.items()}
    rows_first = lambda w, k: np.ascontiguousarray(w.reshape(k, P, -1).transpose(1, 0, 2))

    def swiglu_chunks(gate, up, down):
        lead = gate.shape[:-2]
        gu = np.stack([w.reshape(*lead, KD, P, NC, FC) for w in (gate, up)], axis=-2)
        n = len(lead)
        gu = gu.transpose(n + 2, *range(n), n + 1, n, n + 3, n + 4).reshape(NC, *lead, P, 2 * KD * FC)
        dn = down.reshape(*lead, NC, 2, P, D)
        dn = dn.transpose(n, *range(n), n + 2, n + 1, n + 3).reshape(NC, *lead, P, 2 * D)
        return np.ascontiguousarray(np.concatenate([gu, dn], axis=-1))

    x = a["x"][0]
    w_in = a["ssm_w_in"][0]
    w_xbc = w_in[:, DI:DI + XBC].reshape(KD, P, NL_XBC, XC).transpose(2, 1, 0, 3).reshape(NL_XBC, P, KD * XC)
    w_z = w_in[:, 0:DI].reshape(KD, P, NG, GW).transpose(2, 1, 0, 3).reshape(NG, P, KD * GW)
    kvb = a["mla_w_kv_b"].reshape(KVL, AH, NOPE + VD)
    kvb = np.concatenate([kvb[:, :, :NOPE].reshape(KVL, -1), kvb[:, :, NOPE:].reshape(KVL, -1)], axis=1)
    qb = a["mla_w_q_b"][0].reshape(QL, AH, NOPE + ROPE)
    qb = np.concatenate([qb[:, :, :NOPE].reshape(QL, -1), qb[:, :, NOPE:].reshape(QL, -1)], axis=1)
    kvq = np.concatenate([a["mla_w_kv_a"], a["mla_w_q_a"][0]], axis=1)
    conv = np.concatenate([a["ssm_conv_w"][0], a["ssm_conv_b"]], axis=0)
    arrays = {
        "x_tok": x.reshape(NT, P, D).transpose(1, 0, 2),
        "x_T": x.T.reshape(KD, P, SEQ).transpose(1, 0, 2),
        "w_dt": w_in[:, DI + XBC:].reshape(KD, P, NH).transpose(1, 0, 2),
        "w_rt": a["moe_w_router"][0].reshape(KD, P, NE).transpose(1, 0, 2),
        "w_xbc": w_xbc, "w_z": w_z,
        "w_out": a["ssm_w_out"][0].reshape(NL_WO, 4, P, D).transpose(0, 2, 1, 3).reshape(NL_WO, P, 4 * D),
        "w_ffn": swiglu_chunks(a["ffn_w_gate"][0], a["ffn_w_up"][0], a["ffn_w_down"][0]),
        "w_kvq": rows_first(kvq, KD).reshape(P, -1),
        "w_kvb": rows_first(kvb, 2).reshape(P, -1),
        "w_qb": rows_first(qb, 3).reshape(P, -1),
        "w_o": a["mla_w_o"][0].reshape(2, 4, P, D).transpose(0, 2, 1, 3).reshape(2, P, 4 * D),
        "w_moe": swiglu_chunks(a["moe_w_gate"][0], a["moe_w_up"][0], a["moe_w_down"][0]),
        "conv_wb": conv.reshape(5, NM, P).transpose(2, 1, 0),
        "gains": np.concatenate([a["ssm_norm_g"].reshape(MX, P), a["mla_kv_norm_g"].reshape(2, P),
                                 a["mla_q_norm_g"].reshape(3, P)], axis=0).T,
        "rows": np.concatenate([a["ssm_dt_bias"][0], a["ssm_a_log"][0], a["ssm_d"][0], a["moe_b_router"][0],
                                np.array([10000.0 ** (-2.0 * k / ROPE) for k in range(HR)], np.float32)]),
        "ln_gb": np.stack([a["ln_g"].reshape(4, D), a["ln_b"].reshape(4, D)], axis=1).reshape(4, 2 * D),
        "pos": a["positions"].reshape(NT, P).T,
    }
    arrays = {k: np.ascontiguousarray(v) for k, v in arrays.items()}
    nc = bacc.Bacc("TRN2", target_bir_lowering=False, num_devices=1)
    d = {k: nc.dram_tensor(f"{k}_dram", v.shape, mybir.dt.from_np(v.dtype), kind="ExternalInput").ap()
         for k, v in arrays.items()}
    out = nc.dram_tensor("out", (SEQ, D), F32, kind="ExternalOutput").ap()
    build_kernel(nc, d, out)
    r = run_bass_kernel_spmd(nc, [{f"{k}_dram": v for k, v in arrays.items()}], core_ids=[0])
    return r.results[0]["out"].reshape(1, SEQ, D)
```

```python
import math
from contextlib import ExitStack

import concourse.bass as bass
from concourse import mybir

F32 = mybir.dt.float32
F32R = mybir.dt.float32r
I32 = mybir.dt.int32
U32 = mybir.dt.uint32
ALU = mybir.AluOpType
ACT = mybir.ActivationFunctionType
AX = mybir.AxisListType

P = 128
SEQ, D = 256, 1024
NT = SEQ // P
KD = D // P
ALPHA = (2.0 * 2) ** 0.25
LN_EPS, RMS_EPS = 1e-5, 1e-6
DI, HD, NG, NS = 2048, 64, 4, 128
NH = DI // HD
HG = NH // NG
XBC = DI + 2 * NG * NS
NM = XBC // P
MX = DI // P
GW = DI // NG
AH, NOPE, ROPE, VD, QL, KVL = 8, 128, 64, 128, 384, 256
HR = ROPE // 2
SCALE = (NOPE + ROPE) ** -0.5
FF, NE, TOPK = 2816, 8, 2
FC = 256
NC = FF // FC
MAX_EXTRA = SEQ * TOPK // (P + 1)
NTAB = NE + MAX_EXTRA + 1
UW, NRAW, NPART = 1024, 11, 6
GU, DN = 2 * KD * FC // UW, 2 * D // UW
ITEM = NC * (GU + DN)
assert ITEM % NRAW == 0 and ITEM % NPART == 0
R_Z = NM
R_WO = R_Z + NG * KD * GW // UW
R_FFN = R_WO + MX
R_KVQ = R_FFN + ITEM
R_KVB = R_KVQ + KD
R_QB = R_KVB + 4
R_O = R_QB + 5
R_MOE = R_O + AH
S_Z = NM
S_FFN = S_Z + NG * KD * GW // UW
S_KVQ = S_FFN + ITEM
S_MOE = S_KVQ + KD
D_WO, D_O = MX, MX + AH
NEG = -1.0e30
TWO_PI_1, TWO_PI_2 = 6.28125, 2029.0 / 2 ** 20
TWO_PI_3 = 2 * math.pi - TWO_PI_1 - TWO_PI_2
MAGIC = 1.5 * 2 ** 23
PI_IN = 3.1415925


class Count:

    def __init__(self):
        self.n, self.extra = 0, None

    def up(self, by=1):
        self.n += by
        return self.value()

    def value(self):
        return self.n if self.extra is None else self.extra + self.n


def build_kernel(nc, d, out):
    ctx = ExitStack()
    with ctx:
        def sb(name, shape, dt=F32):
            return ctx.enter_context(nc.sbuf_tensor(name, shape, dt))

        def sems(names):
            return [ctx.enter_context(nc.semaphore(n)) for n in names.split()]

        raw = sb("raw", [P, NRAW, UW])
        w_hi, w_lo = sb("w_hi", [P, NPART, UW], F32R), sb("w_lo", [P, NPART, UW], F32R)
        h_tok = sb("h_tok", [P, NT, D])
        h_hi, h_lo = sb("h_hi", [P, KD, SEQ], F32R), sb("h_lo", [P, KD, SEQ], F32R)
        ln_gb = sb("ln_gb", [P, 2 * D])
        ident, tri, stri, ones = (sb(n, [P, P]) for n in ("ident", "tri", "stri", "ones"))
        slot_iota = sb("slot_iota", [P, P])
        causal_add = sb("causal_add", [P, 2 * P])
        before = sb("before", [P, NE, NE])
        neg_half = sb("neg_half", [P, 2])
        conv_wb = sb("conv_wb", [P, NM, 5])
        gains = sb("gains", [P, MX + 2 + 3])
        rows = sb("rows", [P, 3 * NH + NE + HR])
        wrt_hi, wrt_lo = sb("wrt_hi", [P, KD, NE], F32R), sb("wrt_lo", [P, KD, NE], F32R)
        pos_i = sb("pos_i", [P, NT], I32)
        dt_bias, a_log, d_skip = (rows[:, k * NH:(k + 1) * NH] for k in range(3))
        b_rt = rows[:, 3 * NH:3 * NH + NE]
        inv_freq = rows[:, 3 * NH + NE:]
        NJ = 2 * NG + 4 * NT + NT
        pow_in_t, pow_out_t = sb("pow_in_t", [P, NJ, 2]), sb("pow_out_t", [P, NJ, 2])
        bn, mv = sb("bn", [P, 2, 6]), sb("mv", [P, NT, 2])
        sil, hid = sb("sil", [P, 2, FC]), sb("hid", [P, 2, FC])
        hid_hi, hid_lo = sb("hid_hi", [P, 2, 2, P], F32R), sb("hid_lo", [P, 2, 2, P], F32R)
        wdt_hi, wdt_lo = (v[:].rearrange("p a b c -> p (a b c)")[:, 0:KD * NH].rearrange("p (k n) -> p k n", k=KD)
                          for v in (hid_hi, hid_lo))
        dt, la = sb("dt", [P, NT * NH]), sb("la", [P, NT * NH])
        exp_a = sb("exp_a", [P, NH])
        cum, to_end, decay_end, decay_cum = (
            sb("cum", [P, NT * NH]), sb("to_end", [P, NH]), sb("decay_end", [P, NH]), sb("decay_cum", [P, NH]))
        sq_sum = sb("sq_sum", [P, 2 * NG])
        ang_r, ang_c = sb("ang_r", [P, NT, HR]), sb("ang_c", [P, NT, HR])
        pos_f = sb("pos_f", [P, NT])
        sin_t, cos_t = sb("sin_t", [P, NT, HR]), sb("cos_t", [P, NT, HR])
        kq_ss = sb("kq_ss", [P, NT, 2])
        mx, negm, psum_row, rinv = (sb(n, [P, AH * NT]) for n in ("mx", "negm", "psum_row", "rinv"))
        logits, top_v = sb("logits", [P, NT, NE]), sb("top_v", [P, NT, NE])
        top_i, top_f = sb("top_i", [P, NT, NE], U32), sb("top_f", [P, NT, 2])
        one_hot = sb("one_hot", [P, 2, NT, NE])
        gap, gap_e, den, w_top = sb("gap", [P, NT]), sb("gap_e", [P, NT]), sb("den", [P, NT]), sb("w_top", [P, 2, NT])
        chosen, gates, posm = sb("chosen", [P, NT, NE]), sb("gates", [P, NT, NE]), sb("posm", [P, NT, NE])
        chosen_sum = sb("chosen_sum", [P, NE])
        over, rank, sel = sb("over", [P, NE]), sb("rank", [P, NE]), sb("sel", [P, MAX_EXTRA, NE])
        rank_in = sb("rank_in", [P, NE, NE])
        sel_in = sb("sel_in", [P, NT, NE])
        ctl_f, ctl = sb("ctl_f", [P, 4]), sb("ctl", [P, 4], I32)
        slot_tab, gate_tab = sb("slot_tab", [P, NT, NTAB]), sb("gate_tab", [P, NT, NTAB])

        WORK = 16896
        work = sb("work", [P, WORK])
        used = [0]

        def carve(*shape):
            n = math.prod(shape)
            v = work[:, used[0]:used[0] + n]
            used[0] += n
            assert used[0] <= WORK, used
            names = "abcd"[:len(shape)]
            if len(shape) > 1:
                v = v.rearrange(f"p ({' '.join(names)}) -> p {' '.join(names)}", **dict(zip(names, shape)))
            return v

        xbc_T = carve(NM, SEQ)
        z_gate = carve(NT, NG, GW)
        used[0] -= NT * NG * GW
        x_T, w_dt, w_rt = carve(KD, SEQ), carve(KD, NH), carve(KD, NE)
        used[0] = NM * SEQ + NT * NG * GW
        cb_mask = carve(NT * NG, P)
        used[0] -= NT * NG * P
        dt_v, dt_e, dt_s, dt_q, dt_p = (carve(NT * NH) for _ in range(5))
        ang, ang_k = carve(NT, HR), carve(NT, HR)
        used[0] = NM * SEQ + NT * NG * GW + NT * NG * P
        x_skip, x_dt = carve(2, GW), carve(2, GW)
        x_end, state, b_tok = carve(GW), carve(GW), carve(NG, P)
        decay = carve(2, 4, P)
        mix_T = carve(2, 4, P)
        y_tmp = hid[:].rearrange("p a b -> p (a b)")
        conv_acc = x_skip.rearrange("p a (b c) -> p (a b) c", c=SEQ)[:, 0:2, :]
        y_sq = sil[:].rearrange("p a b -> p (a b)")
        used[0] = 0
        ckv_n, q_n = carve(NT, KVL), carve(NT, QL)
        k_rope, k_rot = carve(NT, ROPE), carve(NT, ROPE)
        ckv_T, q_T = carve(2, SEQ), carve(3, SEQ)
        kn_T, qn_T = carve(AH, SEQ), carve(AH, SEQ)
        v_tok = carve(NT, AH * VD)
        q_rot = carve(NT, AH * ROPE)
        rot_a, rot_b = carve(AH * HR), carve(AH * HR)
        qr_T, kr_T = carve(AH, SEQ), carve(SEQ)
        o_T = carve(AH, SEQ)
        prob, prob_T = carve(4, SEQ), carve(2, NT, P)
        sq_junk = carve(QL)
        used[0] = 0
        moe_acc = carve(NT, D)
        y_e = carve(2, 512)
        pick, pick_g = carve(NT, P), carve(NT, P)
        scat = carve(NT, P)

        ps = ctx.enter_context(nc.psum_tensor("ps", [P, 8, 512], F32))

        raw_full = sems(" ".join(f"raw_full{n}" for n in range(NRAW)))
        (x_in, xt_in, small_in, wdt_in, wrt_in, gb_in, out_done) = sems(
            "x_in xt_in small_in wdt_in wrt_in gb_in out_done")
        (hi_done, lo_pool, lo_done, parts_used, direct_used, consts) = sems(
            "hi_done lo_pool lo_done parts_used direct_used consts")
        (small_hi, small_lo, h_hi_done) = sems("small_hi small_lo h_hi_done")
        (dve_step, act_step) = sems("dve_step act_step")
        (dt_mm, dt_abs, dt_exp, la_ready, cum_mm, cum_ready, decays) = sems(
            "dt_mm dt_abs dt_exp la_ready cum_mm cum_ready decays")
        (conv_done, xbc_done, z_done) = sems("conv_done xbc_done z_done")
        (btr_mm, b_done, cb_mm, cb_done) = sems("btr_mm b_done cb_mm cb_done")
        (xs_tr, x_done, bc_mm, relu_done, dec_done, mix_done) = sems(
            "xs_tr x_done bc_mm relu_done dec_done mix_done")
        (st_mm, st_done, yd_mm, yoff_mm, y_done, sq_done, yn_done, yt_mm, yt_done) = sems(
            "st_mm st_done yd_mm yoff_mm y_done sq_done yn_done yt_mm yt_done")
        (pow_go, pow_ok, ln_done, ln_tr, hT_done) = sems("pow_go pow_ok ln_done ln_tr hT_done")
        (ang_done, trig_done) = sems("ang_done trig_done")
        (f_gu0, f_silu, f_hid, f_tr, f_hT, f_hThi) = sems("f_gu0 f_silu f_hid f_tr f_hT f_hThi")
        (kq_sq, kq_done, kr_done, kq_tr, kqT_done) = sems("kq_sq kq_done kr_done kq_tr kqT_done")
        (nope_mm, nope_done, v_mm, v_done, qr_mm, qrot_done, qr_tr, qrT_done) = sems(
            "nope_mm nope_done v_mm v_done qr_mm qrot_done qr_tr qrT_done")
        (sc_mm, max_done, exp_done, prob_done, prob_tr, probT_done, o_mm, o_done) = sems(
            "sc_mm max_done exp_done prob_done prob_tr probT_done o_mm o_done")
        (rt_mm, gap_done, gap_exp, chosen_done, pos_mm, route_done) = sems(
            "rt_mm gap_done gap_exp chosen_done pos_mm route_done")
        (m_pick, m_gat, m_xehi, m_xe, m_silu, m_hid, m_tr, m_hThi, m_hT, m_yec, m_sc, m_acc, m_str, m_scat) = sems(
            "m_pick m_gat m_xehi m_xe m_silu m_hid m_tr m_hThi m_hT m_yec m_sc m_acc m_str m_scat")
        moe_zero, = sems("moe_zero")

        block = ctx.enter_context(nc.Block())
        NSMALL = 4

        KQ = KVL + ROPE + QL

        def unit(n):
            return raw[:, n % NRAW, :]

        def full(n):
            return raw_full[n % NRAW], 16 * (n // NRAW + 1)

        def freed(n):
            if n < R_Z:
                return lo_pool, n + 1
            if n < R_WO:
                return lo_done, n - R_Z + 1
            if n < R_FFN:
                return direct_used, n - R_WO + 1
            if n < R_KVB:
                return lo_done, n - R_Z - MX + 1
            if n < R_QB:
                return v_mm, NT
            if n < R_O:
                return qr_mm, NT
            return direct_used, D_WO + n - R_O + 1

        ORDER = [("gu", 0, j) for j in range(GU)]
        for c in range(1, NC):
            ORDER += [("gu", c, j) for j in range(GU)] + [("dn", c - 1, j) for j in range(DN)]
        ORDER += [("dn", NC - 1, j) for j in range(DN)]
        AT = {u: r for r, u in enumerate(ORDER)}
        LO0 = S_MOE - S_Z

        def full_moe(i, r):
            p = (R_MOE + r) % NRAW
            before_item = len(range(p, R_MOE, NRAW)) + len([x for x in range(r) if (R_MOE + x) % NRAW == p])
            return raw_full[p], (i * (ITEM // NRAW) + (before_item + 1)) * 16

        @block.sync
        def _(sp):
            def load(n, src):
                if n >= NRAW:
                    sp.wait_ge(*freed(n - NRAW))
                sp.dma_start(unit(n)[:, 0:src.shape[1]], src).then_inc(raw_full[n % NRAW], 16)

            def gain_bias(ln):
                if ln:
                    sp.wait_ge(ln_done, ln * NT)
                sp.dma_start(ln_gb[:], d["ln_gb"][ln].partition_broadcast(P)).then_inc(gb_in, 16)

            for k in range(0, KD, 4):
                sp.dma_start(x_T[:, k:k + 4, :], d["x_T"][:, k:k + 4, :]).then_inc(xt_in, 16)
            load(0, d["w_xbc"][0])
            sp.dma_start(w_dt, d["w_dt"]).then_inc(wdt_in, 16)
            for m in range(1, 4):
                load(m, d["w_xbc"][m])
            sp.dma_start(conv_wb[:], d["conv_wb"]).then_inc(small_in, 16)
            sp.dma_start(rows[:], d["rows"].partition_broadcast(P)).then_inc(small_in, 16)
            sp.dma_start(gains[:], d["gains"]).then_inc(small_in, 16)
            sp.dma_start(pos_i[:], d["pos"]).then_inc(small_in, 16)
            sp.dma_start(w_rt, d["w_rt"]).then_inc(wrt_in, 16)
            for m in range(4, NM):
                load(m, d["w_xbc"][m])
                if m == NRAW - 1:
                    sp.dma_start(h_tok[:], d["x_tok"]).then_inc(x_in, 16)
                    gain_bias(0)
            for u in range(R_WO - R_Z):
                load(R_Z + u, d["w_z"][u])
            for u in range(MX):
                load(R_WO + u, d["w_out"][u])
            for c in range(NC):
                for j in range(GU):
                    load(R_FFN + c * (GU + DN) + j, d["w_ffn_gu"][c][j])
                for j in range(DN):
                    load(R_FFN + c * (GU + DN) + GU + j, d["w_ffn_dn"][c][j])
                if c == 4:
                    gain_bias(1)
            for k in range(KD):
                load(R_KVQ + k, d["w_kvq"][k])
            for u in range(4):
                load(R_KVB + u, d["w_kvb"][u])
            for u in range(3):
                load(R_QB + u, d["w_qb"][u])
            for u in range(2):
                load(R_QB + 3 + u, d["w_qr"][u][:, 0:(2 - u) * AH * ROPE])
            gain_bias(2)
            for h in range(AH):
                load(R_O + h, d["w_o"][h])

            def load_item(i, e, first=False):
                for r, (kind, c, j) in enumerate(ORDER):
                    if first and r < NRAW:
                        sp.wait_ge(*freed(R_MOE + r - NRAW))
                    else:
                        sp.wait_ge(lo_done, i * ITEM + (LO0 + r - NRAW + 1))
                    sp.dma_start(unit(R_MOE + r), d["w_moe_" + kind][c][j][bass.ds(e, 1), :, :]
                                 .rearrange("o p n -> (o p) n")).then_inc(raw_full[(R_MOE + r) % NRAW], 16)

            load_item(0, 0, first=True)
            with sp.Fori(1, NE) as i:
                load_item(i, i)
            gain_bias(3)
            sp.wait_ge(route_done, 1)
            n_extra = sp.value_load(ctl[0:1, 0:1], min_val=0, max_val=MAX_EXTRA)
            with sp.If(n_extra > 0):
                with sp.Fori(0, n_extra) as k:
                    e = sp.value_load(ctl[0:1, bass.ds(k + 1, 1)], min_val=0, max_val=NE - 1)
                    load_item(k + NE, e)
            for t in range(NT):
                sp.wait_ge(ln_done, 3 * NT + t + 1)
                sp.dma_start(out[t * P:(t + 1) * P, :], h_tok[:, t, :]).then_inc(out_done, 16)
            sp.wait_ge(out_done, 16 * NT)

        @block.gpsimd
        def _(pool):
            g = nc.gpsimd
            g.memset(ident[:], 0.0).then_inc(consts, 1)
            g.memset(tri[:], 1.0).then_inc(consts, 1)
            g.memset(stri[:], 1.0).then_inc(consts, 1)
            g.memset(ones[:], 1.0).then_inc(consts, 1)
            g.memset(causal_add[:], 0.0).then_inc(consts, 1)
            g.memset(before[:], 1.0).then_inc(consts, 1)
            g.memset(neg_half[:], -0.5).then_inc(consts, 1)
            g.memset(pow_in_t[:], 1.0).then_inc(consts, 1)
            g.memset(slot_tab[:], -1.0).then_inc(consts, 1)
            g.memset(gate_tab[:], 0.0).then_inc(consts, 1)
            g.iota(slot_iota[:], [[1, P]], base=0, channel_multiplier=0,
                   allow_small_or_imprecise_dtypes=True).then_inc(consts, 1)
            pool.wait_ge(consts, 11)
            g.affine_select(out=ident[:], in_=ident[:], compare_op=ALU.not_equal, fill=1.0, base=0,
                            pattern=[[-1, P]], channel_multiplier=1).then_inc(consts, 1)
            g.affine_select(out=tri[:], in_=tri[:], compare_op=ALU.is_ge, fill=0.0, base=0,
                            pattern=[[1, P]], channel_multiplier=-1).then_inc(consts, 1)
            g.affine_select(out=stri[:], in_=stri[:], compare_op=ALU.is_gt, fill=0.0, base=0,
                            pattern=[[1, P]], channel_multiplier=-1).then_inc(consts, 1)
            g.affine_select(out=causal_add[:, P:], in_=causal_add[:, P:], compare_op=ALU.is_ge, fill=NEG, base=0,
                            pattern=[[-1, P]], channel_multiplier=1).then_inc(consts, 1)
            g.affine_select(out=before[:], in_=before[:], compare_op=ALU.is_gt, fill=0.0, base=0,
                            pattern=[[1, NE], [-1, NE]], channel_multiplier=0).then_inc(consts, 1)
            for q in range(NM):
                pool.wait_ge(hi_done, q + 1)
                g.tensor_tensor(w_lo[:, q % NPART, :], unit(q), w_hi[:, q % NPART, :].bitcast(F32), ALU.subtract)\
                    .then_inc(lo_pool, 1)
            with pool.Fori(0, NJ) as j:
                pool.wait_ge(pow_go, j + 1)
                g.tensor_tensor(pow_out_t[:, bass.ds(j, 1), :], pow_in_t[:, bass.ds(j, 1), :],
                                neg_half[:, :].unsqueeze(1), ALU.pow).then_inc(pow_ok, 1)

        CONSTS = 16

        @block.tensor
        def _(pe):
            mm, tr = nc.tensor.matmul, nc.tensor.transpose

            def group(outp, pairs):
                for k, (a, b) in enumerate(pairs):
                    last = mm(outp, a, b, start=(k == 0), stop=(k == len(pairs) - 1))
                return last

            def tok(t):
                return slice(t * P, (t + 1) * P)

            def three(outp, a, b, first, last):
                mm(outp, a[0], b[0], start=first, stop=False)
                mm(outp, a[0], b[1], start=False, stop=False)
                return mm(outp, a[1], b[0], start=False, stop=last)

            def part(q, c0, c1):
                return w_hi[:, q % NPART, c0:c1], w_lo[:, q % NPART, c0:c1]

            def rows_of(k, cols):
                return h_hi[:, k, cols], h_lo[:, k, cols]

            def split_in(q):
                if q < S_Z:
                    pe.wait_ge(lo_pool, q + 1)
                else:
                    pe.wait_ge(lo_done, q - S_Z + 1)

            pe.wait_ge(h_hi_done, 2)
            pe.wait_ge(hT_done, 2)
            pe.wait_ge(small_lo, 1)
            for t in range(NT):
                for k in range(KD):
                    last = three(ps[:, 4, t * NH:(t + 1) * NH], rows_of(k, tok(t)), (wdt_hi[:, k, :], wdt_lo[:, k, :]),
                                 k == 0, k == KD - 1)
            last.then_inc(dt_mm, 1)

            for m in range(NM):
                split_in(m)
                if m >= 4:
                    pe.wait_ge(conv_done, m - 3)
                for k in range(KD):
                    last = three(ps[:, m % 4, 0:SEQ], part(m, k * P, (k + 1) * P), rows_of(k, slice(0, SEQ)),
                                 k == 0, k == KD - 1)
                last.then_inc(parts_used, 1)
                if m == 7:
                    pe.wait_ge(consts, CONSTS)
                    pe.wait_ge(la_ready, 1)
                    mm(ps[:, 5, 0:NT * NH], tri[:], la[:], start=True, stop=True)
                    mm(ps[:, 5, NT * NH:2 * NT * NH], ones[:], la[:], start=True, stop=True).then_inc(cum_mm, 1)

            def z_step(u):
                g, half = divmod(u, 2)
                if u == 0:
                    pe.wait_ge(cum_ready, 1)
                    pe.wait_ge(cb_done, 1)
                elif half == 0:
                    pe.wait_ge(z_done, NT * g)
                for j in (2 * half, 2 * half + 1):
                    q = S_Z + 4 * g + j
                    split_in(q)
                    for k in (2 * j, 2 * j + 1):
                        for t in range(NT):
                            last = three(ps[:, 5 - 2 * t, :], rows_of(k, tok(t)), part(q, k % 2 * GW, (k % 2 + 1) * GW),
                                         k == 0, k == KD - 1)
                    last.then_inc(parts_used, 1)

            pe.wait_ge(xbc_done, NM)
            pe.wait_ge(dt_abs, 1)
            for g in range(NG):
                last = tr(ps[:, 4, g * P:(g + 1) * P], xbc_T[:, MX + g, 0:P], ident[:])
            last.then_inc(btr_mm, 1)
            for t in range(NT):
                for g in range(NG):
                    last = mm(ps[:, 2 + t, g * P:(g + 1) * P], xbc_T[:, MX + g, tok(t)],
                              xbc_T[:, MX + NG + g, tok(t)], start=True, stop=True)
            last.then_inc(cb_mm, 1)

            def ssd_front(u):
                g, t = divmod(u, NT)
                if u >= 1:
                    pe.wait_ge(x_done, u)
                for j in range(4):
                    last = tr(ps[:, 0, j * P:(j + 1) * P], xbc_T[:, g * 4 + j, tok(t)], ident[:])
                last.then_inc(xs_tr, 1)
                for b in range(2):
                    if u >= 1:
                        pe.wait_ge(relu_done, 2 * u + b - 1)
                    for j in range(4):
                        h = t * NH + g * HG + b * 4 + j
                        last = mm(ps[:, 6 + b, j * P:(j + 1) * P], la[:, h:h + 1].broadcast_to([P, P]), tri[:],
                                  start=True, stop=True)
                    last.then_inc(bc_mm, 1)

            def y_back(u):
                pe.wait_ge(yn_done, u + 1)
                if u == 0:
                    pe.wait_ge(cb_done, 1)
                else:
                    pe.wait_ge(yt_done, u)
                g, t = divmod(u, NT)
                for j in range(4):
                    last = tr(ps[:, 2, j * P:(j + 1) * P], z_gate[:, t, g, j * P:(j + 1) * P], ident[:])
                last.then_inc(yt_mm, 1)

            NU = NG * NT
            ssd_front(0)
            z_step(0)
            z_step(1)
            for u in range(NU):
                g, t = divmod(u, NT)
                if u + 1 < NU:
                    ssd_front(u + 1)
                if u + 2 < NU:
                    z_step(u + 2)
                if t == 0:
                    pe.wait_ge(b_done, 1)
                    pe.wait_ge(x_done, u + 1)
                    if u >= 1:
                        pe.wait_ge(y_done, u)
                    mm(ps[:, 1, :], b_tok[:, g, :], x_end[:], start=True, stop=True).then_inc(st_mm, 1)
                else:
                    pe.wait_ge(st_done, g + 1)
                    mm(ps[:, 1, :], xbc_T[:, MX + NG + g, tok(t)], state, start=True, stop=True)\
                        .then_inc(yoff_mm, 1)
                if u >= 1:
                    pe.wait_ge(y_done, u)
                for b in range(2):
                    pe.wait_ge(mix_done, 2 * u + b + 1)
                    for j in range(4):
                        c = (b * 4 + j) * HD
                        last = mm(ps[:, 4, c:c + HD], mix_T[:, b, j, :], x_dt[:, u % 2, c:c + HD],
                                  start=True, stop=True)
                last.then_inc(yd_mm, 1)
                if u >= 1:
                    y_back(u - 1)
            y_back(NU - 1)

            pe.wait_ge(yt_done, NU)
            pe.wait_ge(z_done, NU)
            for k in range(MX):
                pe.wait_ge(*full(R_WO + k))
                for t in range(NT):
                    for f in range(2):
                        last = mm(ps[:, 4 + 2 * t + f, :], xbc_T[:, k, tok(t)], unit(R_WO + k)[:, f * 512:(f + 1) * 512],
                                  start=(k == 0), stop=(k == MX - 1))
                last.then_inc(direct_used, 1)

            def to_channel_major(t, ln, bank):
                pe.wait_ge(ln_done, ln * NT + t + 1)
                for k in range(KD):
                    last = tr(ps[:, bank + 2 * t + k // 4, (k % 4) * P:(k % 4 + 1) * P],
                              h_tok[:, t, k * P:(k + 1) * P], ident[:])
                last.then_inc(ln_tr, 1)

            for t in range(NT):
                to_channel_major(t, 0, 0)
            steps = [(c, t) for c in range(NC) for t in range(NT)]

            def gate_up(s, j):
                c, t = steps[s]
                q = S_FFN + c * (GU + DN) + j
                if s < NT and j == 0:
                    pe.wait_ge(hT_done, 2 + 2 * (s + 1))
                if t == 0:
                    split_in(q)
                if s >= 2 and j == 0:
                    pe.wait_ge(f_hid, s - 1)
                for k in (2 * j, 2 * j + 1):
                    last = three(ps[:, 4 + s % 2, :], rows_of(k, tok(t)), part(q, k % 2 * 512, (k % 2 + 1) * 512),
                                 k == 0, k == KD - 1)
                if t == NT - 1:
                    last.then_inc(parts_used, 1)
                elif j == GU - 1:
                    last.then_inc(f_gu0, 1)

            for j in range(GU):
                gate_up(0, j)
            for s, (c, t) in enumerate(steps):
                if s + 1 < len(steps):
                    gate_up(s + 1, 0)
                pe.wait_ge(f_hid, s + 1)
                for j in range(2):
                    last = tr(ps[:, 6 + s % 2, j * P:(j + 1) * P], hid[:, s % 2, j * P:(j + 1) * P], ident[:])
                last.then_inc(f_tr, 1)
                if s + 1 < len(steps):
                    for j in range(1, GU):
                        gate_up(s + 1, j)
                pe.wait_ge(f_hT, s + 1)
                for j in range(DN):
                    q = S_FFN + c * (GU + DN) + GU + j
                    if t == 0:
                        split_in(q)
                    for f in range(2):
                        last = three(ps[:, 2 * t + f, :], (hid_hi[:, s % 2, j, :], hid_lo[:, s % 2, j, :]),
                                     part(q, f * 512, (f + 1) * 512), c == 0 and j == 0, c == NC - 1 and j == DN - 1)
                    if t == NT - 1:
                        last.then_inc(parts_used, 1)
            for t in range(NT):
                to_channel_major(t, 1, 4)
            pe.wait_ge(hT_done, 2 + 4 * NT)
            for k in range(KD):
                q = S_KVQ + k
                split_in(q)
                for t in range(NT):
                    three(ps[:, 2 * t, 0:KVL + ROPE], rows_of(k, tok(t)), part(q, 0, KVL + ROPE), k == 0, k == KD - 1)
                    last = three(ps[:, 2 * t + 1, 0:QL], rows_of(k, tok(t)), part(q, KVL + ROPE, KQ), k == 0, k == KD - 1)
                last.then_inc(parts_used, 1)
            for t in range(NT):
                pe.wait_ge(kq_done, t + 1)
                for j in range(2):
                    tr(ps[:, 4 + 2 * t, j * P:(j + 1) * P], ckv_n[:, t, j * P:(j + 1) * P], ident[:])
                tr(ps[0:ROPE, 4 + 2 * t, 2 * P:3 * P], k_rot[:, t, :], ident[:])
                for j in range(3):
                    last = tr(ps[:, 5 + 2 * t, j * P:(j + 1) * P], q_n[:, t, j * P:(j + 1) * P], ident[:])
                last.then_inc(kq_tr, 1)
            pe.wait_ge(kqT_done, NT)
            for u in range(9):
                pe.wait_ge(*full(R_KVB + u))
            wk = [unit(R_KVB + k) for k in range(2)]
            wv = [unit(R_KVB + 2 + k) for k in range(2)]
            wq = [unit(R_QB + k) for k in range(3)]
            wr = [unit(R_QB + 3)[:, 0:AH * ROPE], unit(R_QB + 3)[:, AH * ROPE:], unit(R_QB + 4)[:, 0:AH * ROPE]]
            for h in range(AH):
                if h >= 4:
                    pe.wait_ge(nope_done, h - 3)
                group(ps[:, h % 4, 0:SEQ], [(wk[k][:, h * NOPE:(h + 1) * NOPE], ckv_T[:, k, :]) for k in range(2)])
                group(ps[:, h % 4, SEQ:2 * SEQ], [(wq[k][:, h * NOPE:(h + 1) * NOPE], q_T[:, k, :])
                                                  for k in range(3)]).then_inc(nope_mm, 1)
            for t in range(NT):
                for f in range(2):
                    last = group(ps[:, 4 + 2 * t + f, :],
                                 [(ckv_T[:, k, tok(t)], wv[k][:, f * 512:(f + 1) * 512]) for k in range(2)])
                last.then_inc(v_mm, 1)
            pe.wait_ge(nope_done, AH)
            for t in range(NT):
                group(ps[:, t, :], [(q_T[:, k, tok(t)], wr[k]) for k in range(3)]).then_inc(qr_mm, 1)
            for t in range(NT):
                pe.wait_ge(qrot_done, t + 1)
                pe.wait_ge(v_done, t + 1)
                for h in range(AH):
                    last = tr(ps[0:ROPE, 4 + 2 * t + h // 4, (h % 4) * P:(h % 4 + 1) * P],
                              q_rot[:, t, h * ROPE:(h + 1) * ROPE], ident[:])
                last.then_inc(qr_tr, 1)

            NA = AH * NT

            def scores(a):
                h, t = divmod(a, NT)
                if a >= 2:
                    pe.wait_ge(max_done, a - 1)
                nk = (t + 1) * P
                mm(ps[:, a % 2, 0:nk], qn_T[:, h, tok(t)], kn_T[:, h, 0:nk], start=True, stop=False)
                mm(ps[:, a % 2, 0:nk], qr_T[0:ROPE, h, tok(t)], kr_T[0:ROPE, 0:nk], start=False, stop=True)\
                    .then_inc(sc_mm, 1)

            pe.wait_ge(qrT_done, NT)
            scores(0)
            scores(1)
            for a in range(NA):
                h, t = divmod(a, NT)
                pe.wait_ge(prob_done, a + 1)
                for j in range(t + 1):
                    last = tr(ps[:, 2 + a % 2, j * P:(j + 1) * P], prob[:, a % 4, j * P:(j + 1) * P], ident[:])
                last.then_inc(prob_tr, 1)
                if a + 2 < NA:
                    scores(a + 2)
                pe.wait_ge(probT_done, a + 1)
                if a >= 2:
                    pe.wait_ge(o_done, a - 1)
                group(ps[:, 4 + a % 2, 0:P], [(v_tok[:, j, h * VD:(h + 1) * VD], prob_T[:, a % 2, j, :])
                                              for j in range(t + 1)]).then_inc(o_mm, 1)
            pe.wait_ge(o_done, NA)
            for h in range(AH):
                pe.wait_ge(*full(R_O + h))
                for t in range(NT):
                    for f in range(2):
                        last = mm(ps[:, 4 + 2 * t + f, :], o_T[:, h, tok(t)], unit(R_O + h)[:, f * 512:(f + 1) * 512],
                                  start=(h == 0), stop=(h == AH - 1))
                last.then_inc(direct_used, 1)
            for t in range(NT):
                to_channel_major(t, 2, 0)
            for t in range(NT):
                pe.wait_ge(hT_done, 2 + 4 * NT + 2 * (t + 1))
                for k in range(KD):
                    last = three(ps[:, 4, t * NE:(t + 1) * NE], rows_of(k, tok(t)), (wrt_hi[:, k, :], wrt_lo[:, k, :]),
                                 k == 0, k == KD - 1)
            last.then_inc(rt_mm, 1)
            pe.wait_ge(chosen_done, 1)
            mm(ps[:, 5, 0:NE], stri[:], chosen[:, 0, :], start=True, stop=True)
            group(ps[:, 5, NE:2 * NE], [(stri[:], chosen[:, 1, :]), (ones[:], chosen[:, 0, :])])
            mm(ps[:, 5, 2 * NE:3 * NE], ones[:], chosen_sum[:], start=True, stop=True).then_inc(pos_mm, 1)

            def gather(i):
                pe.wait_ge(m_pick, i + 1)
                for k in range(KD):
                    last = group(ps[:, 2 + k // 4, (k % 4) * P:(k % 4 + 1) * P],
                                 [(h_tok[:, t, k * P:(k + 1) * P], pick[:, t, :]) for t in range(NT)])
                last.then_inc(m_gat, 1)

            def scatter(i):
                pe.wait_ge(m_yec, i + 1)
                pe.wait_ge(m_scat, i + 1)
                for j in range(4):
                    t, f = divmod(j, 2)
                    if j >= 2:
                        pe.wait_ge(m_acc, i * 4 + (j - 1))
                    mm(ps[:, 2 + j % 2, :], scat[:, t, :], y_e[:, f, :], start=True, stop=True).then_inc(m_sc, 1)

            gather(0)
            n_extra = pe.value_load(ctl[0:1, 0:1], min_val=0, max_val=MAX_EXTRA)
            n_items = pe.snap(n_extra + NE)
            with pe.Fori(0, n_items) as i:
                def split_moe(r):
                    pe.wait_ge(lo_done, i * ITEM + (LO0 + r + 1))

                def gate_up_moe(s, j):
                    r = AT["gu", s, j]
                    split_moe(r)
                    if s >= 2 and j == 0:
                        pe.wait_ge(m_hid, i * NC + (s - 1))
                    for k in (2 * j, 2 * j + 1):
                        last = three(ps[:, 4 + s % 2, :], rows_of(k, slice(0, P)),
                                     part(r, k % 2 * 512, (k % 2 + 1) * 512), k == 0, k == KD - 1)
                    last.then_inc(parts_used, 1)

                def hid_transpose_moe(s):
                    pe.wait_ge(m_hid, i * NC + (s + 1))
                    for j in range(2):
                        last = tr(ps[:, 6 + s % 2, j * P:(j + 1) * P], hid[:, s % 2, j * P:(j + 1) * P], ident[:])
                    last.then_inc(m_tr, 1)

                def down_moe(s):
                    pe.wait_ge(m_hT, i * NC + (s + 1))
                    for j in range(DN):
                        r = AT["dn", s, j]
                        split_moe(r)
                        for f in range(2):
                            last = three(ps[:, f, :], (hid_hi[:, s % 2, j, :], hid_lo[:, s % 2, j, :]),
                                         part(r, f * 512, (f + 1) * 512), s == 0 and j == 0,
                                         s == NC - 1 and j == DN - 1)
                        last.then_inc(parts_used, 1)

                pe.wait_ge(m_xe, i * 2 + 2)
                for j in range(GU):
                    gate_up_moe(0, j)
                scatter(i)
                pe.wait_ge(m_acc, i * 4 + 4)
                for t in range(NT):
                    last = tr(ps[:, 2, t * P:(t + 1) * P], pick_g[:, t, :], ident[:])
                last.then_inc(m_str, 1)
                for s in range(NC - 1):
                    gate_up_moe(s + 1, 0)
                    hid_transpose_moe(s)
                    for j in range(1, GU):
                        gate_up_moe(s + 1, j)
                    down_moe(s)
                pe.wait_ge(m_scat, i + 2)
                gather(i + 1)
                hid_transpose_moe(NC - 1)
                down_moe(NC - 1)
            scatter(n_items)

        @block.scalar
        def _(act):
            A = nc.scalar.activation

            def high(n, q, width=UW):
                act.wait_ge(*full(n))
                if q >= NPART:
                    act.wait_ge(parts_used, q - NPART + 1)
                A(w_hi[:, q % NPART, 0:width], unit(n)[:, 0:width], ACT.Copy).then_inc(hi_done, 1)

            act.wait_ge(xt_in, 16 * 2)
            for j in range(2):
                A(h_hi[:, 4 * j:4 * j + 4, :], x_T[:, 4 * j:4 * j + 4, :], ACT.Copy).then_inc(h_hi_done, 1)
            act.wait_ge(wdt_in, 16)
            A(wdt_hi[:], w_dt, ACT.Copy).then_inc(small_hi, 1)
            for q in range(4):
                high(q, q)
            act.wait_ge(wrt_in, 16)
            A(wrt_hi[:], w_rt, ACT.Copy).then_inc(small_hi, 1)
            act.wait_ge(small_in, 16 * NSMALL)
            A(exp_a[:], a_log, ACT.Exp).then_inc(dt_exp, 1)
            act.wait_ge(dt_abs, 1)
            A(dt_e[:], dt_s[:], ACT.Exp).then_inc(dt_exp, 1)
            high(4, 4)
            high(5, 5)
            for m in range(NM):
                high(m + NPART, m + NPART)
                act.wait_ge(conv_done, m + 1)
                A(xbc_T[:, m, :], conv_acc[:, m % 2, :], ACT.Silu).then_inc(xbc_done, 1)
                if m == 1:
                    act.wait_ge(ang_done, 2)
                    A(sin_t[:], ang_r[:], ACT.Sin).then_inc(trig_done, 1)
                    A(cos_t[:], ang_c[:], ACT.Sin).then_inc(trig_done, 1)
            act.wait_ge(cum_ready, 1)
            A(decay_end[:], to_end[:], ACT.Exp).then_inc(decays, 1)
            A(decay_cum[:], cum[:, NH:], ACT.Exp).then_inc(decays, 1)
            def z_silu(u):
                g, t = divmod(u, NT)
                if t == 0:
                    act.wait_ge(parts_used, S_Z + 4 * (g + 1))
                A(z_gate[:, t, g, :], ps[:, 5 - 2 * t, :], ACT.Silu).then_inc(z_done, 1)

            def head_decays(u):
                g, t = divmod(u, NT)
                for b in range(2):
                    act.wait_ge(bc_mm, 2 * u + b + 1)
                    if u >= 1:
                        act.wait_ge(mix_done, 2 * u + b - 1)
                    for j in range(4):
                        h = t * NH + g * HG + b * 4 + j
                        last = A(decay[:, b, j, :], ps[:, 6 + b, j * P:(j + 1) * P], ACT.Relu,
                                 bias=cum[:, h:h + 1], scale=-1.0)
                    last.then_inc(relu_done, 1)
                for b in range(2):
                    act.wait_ge(relu_done, 2 * u + b + 1)
                    A(decay[:, b, :, :], decay[:, b, :, :], ACT.Exp, scale=-1.0).then_inc(dec_done, 1)

            def y_square(u):
                g, t = divmod(u, NT)
                act.wait_ge(y_done, u + 1)
                if u >= 1:
                    act.wait_ge(sq_done, u)
                A(y_sq, z_gate[:, t, g, :], ACT.Square, accum_out=sq_sum[:, u:u + 1]).then_inc(sq_done, 1)

            def y_channel_major(u):
                g, t = divmod(u, NT)
                act.wait_ge(yt_mm, u + 1)
                for j in range(4):
                    m = g * 4 + j
                    last = A(xbc_T[:, m, t * P:(t + 1) * P], ps[:, 2, j * P:(j + 1) * P], ACT.Copy,
                             scale=gains[:, m:m + 1])
                last.then_inc(yt_done, 1)

            NU = NG * NT
            act.wait_ge(btr_mm, 1)
            A(b_tok, ps[:, 4, :].rearrange("p (g c) -> p g c", g=NG), ACT.Copy).then_inc(b_done, 1)
            head_decays(0)
            for z in range(NPART, NPART + 4):
                high(R_Z + z, S_Z + z)
            z_silu(0)
            z_silu(1)
            for u in range(NU):
                g, t = divmod(u, NT)
                if t == 0 and u > 0:
                    z_silu(u)
                    z_silu(u + 1)
                if t == 0:
                    act.wait_ge(st_mm, g + 1)
                    A(state, ps[:, 1, :], ACT.Copy).then_inc(st_done, 1)
                if u + 1 < NU:
                    head_decays(u + 1)
                for z in (2 * u + NPART + 4, 2 * u + NPART + 5):
                    if S_Z + z < S_FFN:
                        high(R_Z + z, S_Z + z)
                y_square(u)
                if u >= 1:
                    y_channel_major(u - 1)
            y_channel_major(NU - 1)

            def h_high(t, ln, bank):
                act.wait_ge(ln_tr, ln * NT + t + 1)
                for b in range(2):
                    A(h_hi[:, 4 * b:4 * b + 4, t * P:(t + 1) * P],
                      ps[:, bank + 2 * t + b, :].rearrange("p (k c) -> p k c", k=4), ACT.Copy).then_inc(h_hi_done, 1)

            for r in range(NPART):
                high(R_FFN + r, S_FFN + r)
            for t in range(NT):
                h_high(t, 0, 0)

            def silu(s):
                c, t = divmod(s, NT)
                if t == 0:
                    act.wait_ge(f_gu0, c + 1)
                else:
                    act.wait_ge(parts_used, S_FFN + c * (GU + DN) + GU)
                A(sil[:, s % 2, :], ps[:, 4 + s % 2, 0:FC], ACT.Silu).then_inc(f_silu, 1)

            def hid_high(s):
                act.wait_ge(f_tr, s + 1)
                A(hid_hi[:, s % 2, :, :], ps[:, 6 + s % 2, 0:2 * P].rearrange("p (j c) -> p j c", j=2), ACT.Copy)\
                    .then_inc(f_hThi, 1)

            def high_next(c, j):
                r = (c + 1) * (GU + DN) + j
                high(R_FFN + r, S_FFN + r, UW if c + 1 < NC else KQ)

            silu(0)
            for c in range(NC):
                high_next(c, 0)
                hid_high(2 * c)
                high_next(c, 1)
                high_next(c, 2)
                silu(2 * c + 1)
                high_next(c, 3)
                hid_high(2 * c + 1)
                if c + 1 < NC:
                    silu(2 * c + 2)
                high_next(c, 4)
                high_next(c, 5)
            for t in range(NT):
                h_high(t, 1, 4)
            for k in range(NPART, KD):
                high(R_KVQ + k, S_KVQ + k, KQ)
            for t in range(NT):
                if t == 0:
                    act.wait_ge(parts_used, S_KVQ + KD)
                else:
                    act.wait_ge(kq_sq, 2 * t)
                A(sq_junk[:, 0:KVL], ps[:, 2 * t, 0:KVL], ACT.Square, accum_out=kq_ss[:, t, 0:1]).then_inc(kq_sq, 1)
                act.wait_ge(kq_sq, 2 * t + 1)
                A(sq_junk[:, 0:QL], ps[:, 2 * t + 1, 0:QL], ACT.Square, accum_out=kq_ss[:, t, 1:2]).then_inc(kq_sq, 1)
            for t in range(NT):
                act.wait_ge(kq_tr, t + 1)
                s_ = slice(t * P, (t + 1) * P)
                for j in range(2):
                    A(ckv_T[:, j, s_], ps[:, 4 + 2 * t, j * P:(j + 1) * P], ACT.Copy, scale=gains[:, MX + j:MX + j + 1])
                A(kr_T[0:ROPE, s_], ps[0:ROPE, 4 + 2 * t, 2 * P:3 * P], ACT.Copy)
                for j in range(3):
                    last = A(q_T[:, j, s_], ps[:, 5 + 2 * t, j * P:(j + 1) * P], ACT.Copy,
                             scale=gains[:, MX + 2 + j:MX + 3 + j])
                last.then_inc(kqT_done, 1)
            for h in range(AH):
                act.wait_ge(nope_mm, h + 1)
                A(kn_T[:, h, :], ps[:, h % 4, 0:SEQ], ACT.Copy)
                A(qn_T[:, h, :], ps[:, h % 4, SEQ:], ACT.Copy).then_inc(nope_done, 1)
            for t in range(NT):
                act.wait_ge(qr_tr, t + 1)
                for b in range(2):
                    last = A(qr_T[0:ROPE, 4 * b:4 * b + 4, t * P:(t + 1) * P],
                             ps[0:ROPE, 4 + 2 * t + b, :].rearrange("p (h c) -> p h c", h=4), ACT.Copy)
                last.then_inc(qrT_done, 1)

            def softmax_exp(a):
                nk = (a % NT + 1) * P
                act.wait_ge(max_done, a + 1)
                A(prob[:, a % 4, 0:nk], prob[:, a % 4, 0:nk], ACT.Exp, bias=negm[:, a:a + 1], scale=SCALE,
                  accum_out=psum_row[:, a:a + 1]).then_inc(exp_done, 1)

            softmax_exp(0)
            for a in range(AH * NT):
                if a + 1 < AH * NT:
                    softmax_exp(a + 1)
                act.wait_ge(prob_tr, a + 1)
                if a >= 2:
                    act.wait_ge(o_mm, a - 1)
                nk = a % NT + 1
                A(prob_T[:, a % 2, 0:nk, :], ps[:, 2 + a % 2, 0:nk * P].rearrange("p (j c) -> p j c", j=nk), ACT.Copy)\
                    .then_inc(probT_done, 1)
            for t in range(NT):
                h_high(t, 2, 0)
            act.wait_ge(gap_done, 1)
            A(gap_e[:], gap[:], ACT.Exp).then_inc(gap_exp, 1)

            def expert_rows_high(i):
                act.wait_ge(m_gat, i + 1)
                for b in range(2):
                    A(h_hi[:, 4 * b:4 * b + 4, 0:P], ps[:, 2 + b, :].rearrange("p (k c) -> p k c", k=4), ACT.Copy)\
                        .then_inc(m_xehi, 1)

            expert_rows_high(0)
            act.wait_ge(route_done, 1)
            n_extra = act.value_load(ctl[0:1, 0:1], min_val=0, max_val=MAX_EXTRA)
            n_items = act.snap(n_extra + NE)
            with act.Fori(0, n_items) as i:
                def high_moe(r):
                    sem, n = full_moe(i, r)
                    act.wait_ge(sem, n)
                    act.wait_ge(parts_used, i * ITEM + (S_MOE + r - NPART + 1))
                    A(w_hi[:, r % NPART, :], unit(R_MOE + r), ACT.Copy).then_inc(hi_done, 1)

                def silu_moe(s):
                    act.wait_ge(parts_used, i * ITEM + (S_MOE + AT["gu", s, GU - 1] + 1))
                    A(sil[:, s % 2, :], ps[:, 4 + s % 2, 0:FC], ACT.Silu).then_inc(m_silu, 1)

                def hid_high_moe(s):
                    act.wait_ge(m_tr, i * NC + (s + 1))
                    A(hid_hi[:, s % 2, :, :], ps[:, 6 + s % 2, 0:2 * P].rearrange("p (j c) -> p j c", j=2), ACT.Copy)\
                        .then_inc(m_hThi, 1)

                for r in range(NPART + 2):
                    high_moe(r)
                silu_moe(0)
                high_moe(NPART + 2)
                high_moe(NPART + 3)
                act.wait_ge(m_str, i + 1)
                A(scat[:], ps[:, 2, 0:2 * P].rearrange("p (t c) -> p t c", t=NT), ACT.Copy).then_inc(m_scat, 1)
                for s in range(NC - 1):
                    nxt = range(AT["gu", s + 1, 0] + NPART, min(AT["gu", s + 1, 0] + NPART + GU + DN, ITEM))
                    high_moe(nxt[0])
                    hid_high_moe(s)
                    high_moe(nxt[1])
                    for r in nxt[2:3]:
                        high_moe(r)
                    silu_moe(s + 1)
                    for r in nxt[3:]:
                        high_moe(r)
                expert_rows_high(i + 1)
                hid_high_moe(NC - 1)

        @block.vector
        def _(dve):
            V = nc.vector
            TS, TT, STT = V.tensor_scalar, V.tensor_tensor, V.scalar_tensor_tensor
            chain = Count()

            def step(ins):
                ins.then_inc(dve_step, 1)
                dve.wait_ge(dve_step, chain.up())

            def heads(ap, n=HG, w=HD):
                return ap.unsqueeze(2).broadcast_to([P, n, w])

            def by_head(ap, n=HG):
                return ap.rearrange("p (h w) -> p h w", h=n)

            def low(n, q, width=UW):
                dve.wait_ge(hi_done, q + 1)
                TT(w_lo[:, q % NPART, 0:width], unit(n)[:, 0:width], w_hi[:, q % NPART, 0:width].bitcast(F32),
                   ALU.subtract).then_inc(lo_done, 1)

            for j in range(2):
                dve.wait_ge(h_hi_done, j + 1)
                k = slice(4 * j, 4 * j + 4)
                TT(h_lo[:, k, :], x_T[:, k, :], h_hi[:, k, :].bitcast(F32), ALU.subtract).then_inc(hT_done, 1)
            dve.wait_ge(small_hi, 1)
            TT(wdt_lo[:], w_dt, wdt_hi[:].bitcast(F32), ALU.subtract).then_inc(small_lo, 1)
            dve.wait_ge(small_hi, 2)
            TT(wrt_lo[:], w_rt, wrt_hi[:].bitcast(F32), ALU.subtract).then_inc(small_lo, 1)
            dve.wait_ge(small_in, 16 * NSMALL)
            dve.wait_ge(dt_mm, 1)
            step(TT(dt_v[:].rearrange("p (t h) -> p t h", t=NT), ps[:, 4, 0:NT * NH].rearrange("p (t h) -> p t h", t=NT),
                    dt_bias.unsqueeze(1).broadcast_to([P, NT, NH]), ALU.add))
            STT(dt_s[:], dt_v[:], -1.0, dt_v[:], ALU.mult, ALU.min).then_inc(dt_abs, 1)
            dve.wait_ge(dt_exp, 2)
            step(TS(dt_q[:], dt_e[:], 2.0, None, ALU.add))
            step(V.reciprocal(dt_q[:], dt_q[:]))
            step(TT(dt_s[:], dt_e[:], dt_q[:], ALU.mult))
            step(TT(dt_q[:], dt_s[:], dt_s[:], ALU.mult))
            step(TS(dt_p[:], dt_q[:], 1.0 / 17, None, ALU.mult))
            for k in (15, 13, 11, 9, 7, 5, 3):
                step(STT(dt_p[:], dt_p[:], 1.0 / k, dt_q[:], ALU.add, ALU.mult))
            step(STT(dt_p[:], dt_p[:], 1.0, dt_s[:], ALU.add, ALU.mult))
            step(TS(dt_v[:], dt_v[:], 0.0, None, ALU.max))
            step(STT(dt[:], dt_p[:], 2.0, dt_v[:], ALU.mult, ALU.add))
            STT(la[:].rearrange("p (t h) -> p t h", t=NT), dt[:].rearrange("p (t h) -> p t h", t=NT), -1.0,
                exp_a[:].unsqueeze(1).broadcast_to([P, NT, NH]), ALU.mult, ALU.mult).then_inc(la_ready, 1)

            def rope_angles():
                step(V.tensor_copy(pos_f[:], pos_i[:]))
                step(TT(ang[:], pos_f[:].unsqueeze(2).broadcast_to([P, NT, HR]),
                        inv_freq.unsqueeze(1).broadcast_to([P, NT, HR]), ALU.mult))
                for quarter, dst in ((0.0, ang_r), (0.25, ang_c)):
                    step(TS(ang_k[:], ang[:], 1 / (2 * math.pi), quarter, ALU.mult, ALU.add))
                    step(TS(ang_k[:], ang_k[:], MAGIC, None, ALU.add))
                    step(TS(ang_k[:], ang_k[:], MAGIC, None, ALU.subtract))
                    step(STT(dst[:], ang_k[:], -TWO_PI_1, ang[:], ALU.mult, ALU.add))
                    step(STT(dst[:], ang_k[:], -TWO_PI_2, dst[:], ALU.mult, ALU.add))
                    step(STT(dst[:], ang_k[:], -TWO_PI_3, dst[:], ALU.mult, ALU.add))
                    step(TS(dst[:], dst[:], quarter * 2 * math.pi, PI_IN, ALU.add, ALU.min))
                    TS(dst[:], dst[:], -PI_IN, None, ALU.max).then_inc(ang_done, 1)

            for m in range(NM):
                dve.wait_ge(parts_used, m + 1)
                if m >= 2:
                    dve.wait_ge(xbc_done, m - 1)
                acc, src = conv_acc[:, m % 2, :], ps[:, m % 4, 0:SEQ]
                step(TS(acc, src, conv_wb[:, m, 3:4], conv_wb[:, m, 4:5], ALU.mult, ALU.add))
                for b in (1, 2, 3):
                    ins = STT(acc[:, b:], src[:, 0:SEQ - b], conv_wb[:, m, 3 - b:4 - b], acc[:, b:], ALU.mult, ALU.add)
                    if b < 3:
                        step(ins)
                ins.then_inc(conv_done, 1)
                if m + NPART >= NM:
                    low(m + NPART, m + NPART)
                if m == 1:
                    rope_angles()
                if m == 9:
                    dve.wait_ge(cum_mm, 1)
                    step(V.tensor_copy(cum[:], ps[:, 5, 0:NT * NH]))
                    TT(to_end[:], ps[:, 5, NT * NH:NT * NH + NH], cum[:, 0:NH], ALU.subtract).then_inc(cum_ready, 1)
            dve.wait_ge(cb_mm, 1)
            for t in range(NT):
                last = TT(cb_mask[:, t * NG:(t + 1) * NG, :], ps[:, 2 + t, :].rearrange("p (g c) -> p g c", g=NG),
                          tri[:].unsqueeze(1).broadcast_to([P, NG, P]), ALU.mult)
            last.then_inc(cb_done, 1)
            dve.wait_ge(decays, 2)

            def scaled_x(u):
                g, t = divmod(u, NT)
                hs = slice(g * HG, (g + 1) * HG)
                dve.wait_ge(xs_tr, u + 1)
                if u >= 2:
                    dve.wait_ge(yd_mm, u - 1)
                TT(by_head(x_skip[:, u % 2, :]), by_head(ps[:, 0, :]), heads(d_skip[:, hs]), ALU.mult)
                ins = TT(by_head(x_dt[:, u % 2, :]), by_head(ps[:, 0, :]),
                         heads(dt[:, t * NH + g * HG:t * NH + (g + 1) * HG]), ALU.mult)
                if t == 0:
                    step(ins)
                    ins = TT(by_head(x_end[:]), by_head(x_dt[:, u % 2, :]), heads(decay_end[:, hs]), ALU.mult)
                ins.then_inc(x_done, 1)

            NU = NG * NT
            scaled_x(0)
            for u in range(NU):
                g, t = divmod(u, NT)
                for b in range(2):
                    dve.wait_ge(dec_done, 2 * u + b + 1)
                    if u >= 1:
                        dve.wait_ge(yd_mm, u)
                    TT(mix_T[:, b, :, :], decay[:, b, :, :],
                       cb_mask[:, t * NG + g:t * NG + g + 1, :].broadcast_to([P, 4, P]), ALU.mult).then_inc(mix_done, 1)
                for z in (2 * u + NPART, 2 * u + NPART + 1):
                    if S_Z + z < S_FFN:
                        low(R_Z + z, S_Z + z)
                if u + 1 < NU:
                    scaled_x(u + 1)
                dve.wait_ge(yd_mm, u + 1)
                skip = x_skip[:, u % 2, :]
                step(TT(skip, ps[:, 4, :], skip, ALU.add))
                if t == 1:
                    dve.wait_ge(yoff_mm, g + 1)
                    step(TT(by_head(y_tmp[:]), by_head(ps[:, 1, :]), heads(decay_cum[:, g * HG:(g + 1) * HG]), ALU.mult))
                    step(TT(skip, skip, y_tmp[:], ALU.add))
                dve.wait_ge(z_done, u + 1)
                y = z_gate[:, t, g, :]
                TT(y, y, skip, ALU.mult).then_inc(y_done, 1)
                dve.wait_ge(sq_done, u + 1)
                TS(pow_in_t[:, u, 0:1], sq_sum[:, u:u + 1], 1.0 / GW, LN_EPS, ALU.mult, ALU.add).then_inc(pow_go, 1)
                dve.wait_ge(pow_ok, u + 1)
                TS(y, y, pow_out_t[:, u, 0:1], None, ALU.mult).then_inc(yn_done, 1)

            jobs = Count()
            jobs.n = NU

            def layer_norm(ln, added):
                job = jobs.n
                jobs.up(NT)
                for t in range(NT):
                    if added:
                        for f in range(2):
                            hs = h_tok[:, t, f * 512:(f + 1) * 512]
                            ins = STT(hs, hs, ALPHA, added(t, f), ALU.mult, ALU.add)
                            step(ins)
                    src = h_tok if added else moe_acc
                    for f in range(2):
                        ins = V.bn_stats(bn[:, f, :], src[:, t, f * 512:(f + 1) * 512])
                        if f:
                            step(ins)
                    step(V.bn_aggr(mv[:, t, :], bn[:]))
                    TS(pow_in_t[:, job + t, 0:1], mv[:, t, 1:2], LN_EPS, None, ALU.add).then_inc(pow_go, 1)
                dve.wait_ge(gb_in, 16 * (ln + 1))
                for t in range(NT):
                    hs = h_tok[:, t, :]
                    dve.wait_ge(pow_ok, job + t + 1)
                    step(TS(hs, (h_tok if added else moe_acc)[:, t, :], mv[:, t, 0:1], pow_out_t[:, job + t, 0:1],
                            ALU.subtract, ALU.mult))
                    step(TT(hs, hs, ln_gb[:, 0:D], ALU.mult))
                    TT(hs, hs, ln_gb[:, D:], ALU.add).then_inc(ln_done, 1)

            dve.wait_ge(x_in, 16)
            for r in range(NPART):
                low(R_FFN + r, S_FFN + r)
            dve.wait_ge(direct_used, D_WO)
            layer_norm(0, lambda t, f: ps[:, 4 + 2 * t + f, :])

            def h_low(t, ln, bank):
                for b in range(2):
                    dve.wait_ge(h_hi_done, 2 + 2 * (ln * NT + t) + b + 1)
                    k, c = slice(4 * b, 4 * b + 4), slice(t * P, (t + 1) * P)
                    TT(h_lo[:, k, c], ps[:, bank + 2 * t + b, :].rearrange("p (k c) -> p k c", k=4),
                       h_hi[:, k, c].bitcast(F32), ALU.subtract).then_inc(hT_done, 1)

            for t in range(NT):
                h_low(t, 0, 0)

            def hidden(s):
                dve.wait_ge(f_silu, s + 1)
                TT(hid[:, s % 2, :], sil[:, s % 2, :], ps[:, 4 + s % 2, FC:], ALU.mult).then_inc(f_hid, 1)

            def hid_low(s):
                dve.wait_ge(f_hThi, s + 1)
                TT(hid_lo[:, s % 2, :, :], ps[:, 6 + s % 2, 0:2 * P].rearrange("p (j c) -> p j c", j=2),
                   hid_hi[:, s % 2, :, :].bitcast(F32), ALU.subtract).then_inc(f_hT, 1)

            def low_next(c, j):
                r = (c + 1) * (GU + DN) + j
                low(R_FFN + r, S_FFN + r, UW if c + 1 < NC else KQ)

            hidden(0)
            for c in range(NC):
                low_next(c, 0)
                hid_low(2 * c)
                low_next(c, 1)
                low_next(c, 2)
                hidden(2 * c + 1)
                low_next(c, 3)
                hid_low(2 * c + 1)
                if c + 1 < NC:
                    hidden(2 * c + 2)
                low_next(c, 4)
                low_next(c, 5)
            dve.wait_ge(parts_used, S_KVQ)
            layer_norm(1, lambda t, f: ps[:, 2 * t + f, :])
            for t in range(NT):
                h_low(t, 1, 4)
            for k in range(NPART, KD):
                low(R_KVQ + k, S_KVQ + k, KQ)

            def rotate(dst, src, t, n):
                x = src.rearrange("p (h c) -> p h c", h=n)
                y = dst.rearrange("p (h c) -> p h c", h=n)
                c = cos_t[:, t:t + 1, :].broadcast_to([P, n, HR])
                s = sin_t[:, t:t + 1, :].broadcast_to([P, n, HR])
                ra = rot_a[:, 0:n * HR].rearrange("p (h c) -> p h c", h=n)
                rb = rot_b[:, 0:n * HR].rearrange("p (h c) -> p h c", h=n)
                TT(ra, x[:, :, 0:HR], c, ALU.mult)
                step(TT(rb, x[:, :, HR:], s, ALU.mult))
                step(TT(y[:, :, 0:HR], ra, rb, ALU.subtract))
                TT(ra, x[:, :, HR:], c, ALU.mult)
                step(TT(rb, x[:, :, 0:HR], s, ALU.mult))
                return TT(y[:, :, HR:], ra, rb, ALU.add)

            dve.wait_ge(trig_done, 2)
            job = jobs.n
            jobs.up(NT)
            for t in range(NT):
                dve.wait_ge(kq_sq, 2 * t + 2)
                TS(pow_in_t[:, job + t, 0:1], kq_ss[:, t, 0:1], 1.0 / KVL, RMS_EPS, ALU.mult, ALU.add)
                TS(pow_in_t[:, job + t, 1:2], kq_ss[:, t, 1:2], 1.0 / QL, RMS_EPS, ALU.mult, ALU.add).then_inc(pow_go, 1)
                step(rotate(k_rot[:, t, :], ps[:, 2 * t, KVL:KVL + ROPE], t, 1))
                dve.wait_ge(pow_ok, job + t + 1)
                TS(ckv_n[:, t, :], ps[:, 2 * t, 0:KVL], pow_out_t[:, job + t, 0:1], None, ALU.mult)
                TS(q_n[:, t, :], ps[:, 2 * t + 1, 0:QL], pow_out_t[:, job + t, 1:2], None, ALU.mult).then_inc(kq_done, 1)
            for t in range(NT):
                dve.wait_ge(v_mm, t + 1)
                for f in range(2):
                    last = V.tensor_copy(v_tok[:, t, f * 512:(f + 1) * 512], ps[:, 4 + 2 * t + f, :])
                last.then_inc(v_done, 1)
            for t in range(NT):
                dve.wait_ge(qr_mm, t + 1)
                ins = rotate(q_rot[:, t, :], ps[:, t, :], t, AH)
                ins.then_inc(qrot_done, 1)
                dve.wait_ge(qrot_done, t + 1)

            NA = AH * NT

            def masked_max(a):
                t = a % NT
                nk = (t + 1) * P
                dve.wait_ge(sc_mm, a + 1)
                if a >= 4:
                    dve.wait_ge(prob_tr, a - 3)
                step(V.tensor_tensor_reduce(out=prob[:, a % 4, 0:nk], in0=ps[:, a % 2, 0:nk],
                                            in1=causal_add[:, 2 * P - nk:], scale=1.0, scalar=NEG * 2,
                                            op0=ALU.add, op1=ALU.max, accum_out=mx[:, a:a + 1]))
                TS(negm[:, a:a + 1], mx[:, a:a + 1], -SCALE, None, ALU.mult).then_inc(max_done, 1)

            def out_T(a):
                h, t = divmod(a, NT)
                dve.wait_ge(o_mm, a + 1)
                V.tensor_copy(o_T[:, h, t * P:(t + 1) * P], ps[:, 4 + a % 2, 0:P]).then_inc(o_done, 1)

            masked_max(0)
            for a in range(NA):
                if a + 1 < NA:
                    masked_max(a + 1)
                nk = (a % NT + 1) * P
                dve.wait_ge(exp_done, a + 1)
                step(V.reciprocal(rinv[:, a:a + 1], psum_row[:, a:a + 1]))
                TS(prob[:, a % 4, 0:nk], prob[:, a % 4, 0:nk], rinv[:, a:a + 1], None, ALU.mult).then_inc(prob_done, 1)
                if a >= 1:
                    out_T(a - 1)
            out_T(NA - 1)
            dve.wait_ge(direct_used, D_O)
            layer_norm(2, lambda t, f: ps[:, 4 + 2 * t + f, :])
            for t in range(NT):
                h_low(t, 2, 0)
            V.memset(scat[:], 0.0).then_inc(m_scat, 1)
            dve.wait_ge(ln_done, 3 * NT)
            TS(moe_acc[:], h_tok[:], ALPHA, None, ALU.mult).then_inc(moe_zero, 1)

            dve.wait_ge(rt_mm, 1)
            step(TT(logits[:], ps[:, 4, 0:NT * NE].rearrange("p (t e) -> p t e", t=NT),
                    b_rt.unsqueeze(1).broadcast_to([P, NT, NE]), ALU.add))
            for t in range(NT):
                step(V.max(top_v[:, t, :], logits[:, t, :]))
                step(V.max_index(top_i[:, t, :], top_v[:, t, :], logits[:, t, :]))
            step(V.tensor_copy(top_f[:], top_i[:, :, 0:2]))
            TT(gap[:], top_v[:, :, 1], top_v[:, :, 0], ALU.subtract).then_inc(gap_done, 1)
            for k in range(2):
                for t in range(NT):
                    ins = TS(one_hot[:, k, t, :], slot_iota[:, 0:NE], top_f[:, t, k:k + 1], None, ALU.is_equal)
            step(ins)
            step(TT(chosen[:], one_hot[:, 0, :, :], one_hot[:, 1, :, :], ALU.add))
            TT(chosen_sum[:], chosen[:, 0, :], chosen[:, 1, :], ALU.add).then_inc(chosen_done, 1)
            dve.wait_ge(gap_exp, 1)
            step(TS(den[:], gap_e[:], 1.0, None, ALU.add))
            step(V.reciprocal(w_top[:, 0, :], den[:]))
            step(TT(w_top[:, 1, :], gap_e[:], w_top[:, 0, :], ALU.mult))
            for t in range(NT):
                step(TS(gates[:, t, :], one_hot[:, 0, t, :], w_top[:, 0, t:t + 1], None, ALU.mult))
                step(STT(gates[:, t, :], one_hot[:, 1, t, :], w_top[:, 1, t:t + 1], gates[:, t, :], ALU.mult, ALU.add))
            dve.wait_ge(pos_mm, 1)
            step(STT(posm[:], ps[:, 5, 0:NT * NE].rearrange("p (t e) -> p t e", t=NT), 1.0, chosen[:], ALU.add, ALU.mult))
            step(TS(posm[:], posm[:], -1.0, None, ALU.add))
            dve.wait_ge(consts, CONSTS)
            V.tensor_copy(slot_tab[:, :, 0:NE], posm[:])
            V.tensor_copy(gate_tab[:, :, 0:NE], gates[:])
            step(TS(over[:], ps[:, 5, 2 * NE:3 * NE], float(P), None, ALU.is_gt))
            step(TT(rank_in[:], before[:], over[:].unsqueeze(1).broadcast_to([P, NE, NE]), ALU.mult))
            step(V.tensor_reduce(rank[:], rank_in[:], axis=AX.X, op=ALU.add))
            V.tensor_reduce(ctl_f[:, 0:1], over[:], axis=AX.X, op=ALU.add)
            for k in range(MAX_EXTRA):
                step(STT(sel[:, k, :], rank[:], float(k), over[:], ALU.is_equal, ALU.mult))
                step(TT(rank_in[:, 0, :], sel[:, k, :], slot_iota[:, 0:NE], ALU.mult))
                step(V.tensor_reduce(ctl_f[:, k + 1:k + 2], rank_in[:, 0, :], axis=AX.X, op=ALU.add))
                s = sel[:, k, :].unsqueeze(1).broadcast_to([P, NT, NE])
                step(STT(sel_in[:], posm[:], -float(P), s, ALU.add, ALU.mult))
                step(V.tensor_reduce(slot_tab[:, :, NE + k], sel_in[:], axis=AX.X, op=ALU.add))
                step(TT(sel_in[:], gates[:], s, ALU.mult))
                step(V.tensor_reduce(gate_tab[:, :, NE + k], sel_in[:], axis=AX.X, op=ALU.add))
            V.tensor_copy(ctl[:], ctl_f[:]).then_inc(route_done, 1)

            def picks(i):
                for t in range(NT):
                    TS(pick[:, t, :], slot_iota[:], slot_tab[:, t, bass.ds(i, 1)], None, ALU.is_equal)
                for t in range(NT):
                    ins = TS(pick_g[:, t, :], slot_iota[:], slot_tab[:, t, bass.ds(i, 1)],
                             gate_tab[:, t, bass.ds(i, 1)], ALU.is_equal, ALU.mult)
                ins.then_inc(m_pick, 1)

            def expert_rows_low(i):
                for b in range(2):
                    dve.wait_ge(m_xehi, 2 * i + (b + 1))
                    k = slice(4 * b, 4 * b + 4)
                    TT(h_lo[:, k, 0:P], ps[:, 2 + b, :].rearrange("p (k c) -> p k c", k=4),
                       h_hi[:, k, 0:P].bitcast(F32), ALU.subtract).then_inc(m_xe, 1)

            def outputs(i):
                dve.wait_ge(parts_used, i * ITEM + S_MOE)
                for f in range(2):
                    ins = V.tensor_copy(y_e[:, f, :], ps[:, f, :])
                ins.then_inc(m_yec, 1)

            def accumulate(i):
                for j in range(4):
                    t, f = divmod(j, 2)
                    dve.wait_ge(m_sc, i * 4 + (j + 1))
                    a = moe_acc[:, t, f * 512:(f + 1) * 512]
                    TT(a, ps[:, 2 + j % 2, :], a, ALU.add).then_inc(m_acc, 1)

            dve.wait_ge(route_done, 1)
            picks(0)
            expert_rows_low(0)
            n_extra = dve.value_load(ctl[0:1, 0:1], min_val=0, max_val=MAX_EXTRA)
            n_items = dve.snap(n_extra + NE)
            dve.wait_ge(moe_zero, 1)
            with dve.Fori(0, n_items) as i:
                def low_moe(r):
                    dve.wait_ge(hi_done, i * ITEM + (S_MOE + r + 1))
                    TT(w_lo[:, r % NPART, :], unit(R_MOE + r), w_hi[:, r % NPART, :].bitcast(F32), ALU.subtract)\
                        .then_inc(lo_done, 1)

                def hidden_moe(s):
                    dve.wait_ge(m_silu, i * NC + (s + 1))
                    TT(hid[:, s % 2, :], sil[:, s % 2, :], ps[:, 4 + s % 2, FC:], ALU.mult).then_inc(m_hid, 1)

                def hid_low_moe(s):
                    dve.wait_ge(m_hThi, i * NC + (s + 1))
                    TT(hid_lo[:, s % 2, :, :], ps[:, 6 + s % 2, 0:2 * P].rearrange("p (j c) -> p j c", j=2),
                       hid_hi[:, s % 2, :, :].bitcast(F32), ALU.subtract).then_inc(m_hT, 1)

                for r in range(4):
                    low_moe(r)
                outputs(i)
                for r in range(4, NPART + 2):
                    low_moe(r)
                hidden_moe(0)
                accumulate(i)
                low_moe(NPART + 2)
                low_moe(NPART + 3)
                dve.wait_ge(m_str, i + 1)
                picks(i + 1)
                for s in range(NC - 1):
                    nxt = range(AT["gu", s + 1, 0] + NPART, min(AT["gu", s + 1, 0] + NPART + GU + DN, ITEM))
                    low_moe(nxt[0])
                    hid_low_moe(s)
                    low_moe(nxt[1])
                    for r in nxt[2:3]:
                        low_moe(r)
                    hidden_moe(s + 1)
                    for r in nxt[3:]:
                        low_moe(r)
                expert_rows_low(i + 1)
                hid_low_moe(NC - 1)
            outputs(n_items)
            accumulate(n_items)
            dve.wait_ge(m_acc, n_items * 4 + 4)
            layer_norm(3, None)


def kernel(**inputs):
    import numpy as np
    import concourse.bacc as bacc
    from concourse.bass_utils import run_bass_kernel_spmd

    a = {k: np.asarray(v) for k, v in inputs.items()}

    def gate_up_units(gate, up):
        n = gate.ndim - 2
        w = np.stack([w.reshape(*w.shape[:n], GU, 2, P, NC, FC) for w in (gate, up)], axis=-2)
        return w.transpose(n + 3, n, *range(n), n + 2, n + 1, n + 4, n + 5).reshape(NC, GU, *gate.shape[:n], P, UW)

    def down_units(down):
        n = down.ndim - 2
        return down.reshape(*down.shape[:n], NC, DN, P, D).transpose(n, n + 1, *range(n), n + 2, n + 3)

    x = a["x"][0]
    w_in = a["ssm_w_in"][0]
    w_xbc = w_in[:, DI:DI + XBC].reshape(KD, P, NM, P).transpose(2, 1, 0, 3).reshape(NM, P, UW)
    w_z = w_in[:, 0:DI].reshape(KD // 2, 2, P, NG, GW).transpose(3, 0, 2, 1, 4).reshape(-1, P, UW)
    kvb = a["mla_w_kv_b"].reshape(KVL, AH, NOPE + VD)
    kvb = np.concatenate([kvb[:, :, :NOPE].reshape(2, P, UW), kvb[:, :, NOPE:].reshape(2, P, UW)], axis=0)
    qb = a["mla_w_q_b"][0].reshape(3, P, AH, NOPE + ROPE)
    w_qr = np.zeros((2, P, UW), np.float32)
    w_qr[0] = qb[0:2, :, :, NOPE:].reshape(2, P, -1).transpose(1, 0, 2).reshape(P, UW)
    w_qr[1, :, 0:AH * ROPE] = qb[2, :, :, NOPE:].reshape(P, -1)
    kvq = np.concatenate([a["mla_w_kv_a"], a["mla_w_q_a"][0]], axis=1)
    conv = np.concatenate([a["ssm_conv_w"][0], a["ssm_conv_b"]], axis=0)
    arrays = {
        "x_tok": x.reshape(NT, P, D).transpose(1, 0, 2),
        "x_T": x.T.reshape(KD, P, SEQ).transpose(1, 0, 2),
        "w_dt": w_in[:, DI + XBC:].reshape(KD, P, NH).transpose(1, 0, 2),
        "w_rt": a["moe_w_router"][0].reshape(KD, P, NE).transpose(1, 0, 2),
        "w_xbc": w_xbc, "w_z": w_z,
        "w_out": a["ssm_w_out"][0].reshape(MX, P, D),
        "w_ffn_gu": gate_up_units(a["ffn_w_gate"][0], a["ffn_w_up"][0]),
        "w_ffn_dn": down_units(a["ffn_w_down"][0]),
        "w_kvq": kvq.reshape(KD, P, -1),
        "w_kvb": kvb,
        "w_qb": qb[:, :, :, :NOPE].reshape(3, P, UW),
        "w_qr": w_qr,
        "w_o": a["mla_w_o"][0].reshape(AH, P, D),
        "w_moe_gu": gate_up_units(a["moe_w_gate"][0], a["moe_w_up"][0]),
        "w_moe_dn": down_units(a["moe_w_down"][0]),
        "conv_wb": conv.reshape(5, NM, P).transpose(2, 1, 0),
        "gains": np.concatenate([a["ssm_norm_g"].reshape(MX, P), a["mla_kv_norm_g"].reshape(2, P),
                                 a["mla_q_norm_g"].reshape(3, P)], axis=0).T,
        "rows": np.concatenate([a["ssm_dt_bias"][0], a["ssm_a_log"][0], a["ssm_d"][0], a["moe_b_router"][0],
                                np.array([10000.0 ** (-2.0 * k / ROPE) for k in range(HR)], np.float32)]),
        "ln_gb": np.stack([a["ln_g"].reshape(4, D), a["ln_b"].reshape(4, D)], axis=1).reshape(4, 2 * D),
        "pos": a["positions"].reshape(NT, P).T,
    }
    arrays = {k: np.ascontiguousarray(v) for k, v in arrays.items()}
    nc = bacc.Bacc("TRN2", target_bir_lowering=False, num_devices=1)
    d = {k: nc.dram_tensor(f"{k}_dram", v.shape, mybir.dt.from_np(v.dtype), kind="ExternalInput").ap()
         for k, v in arrays.items()}
    out = nc.dram_tensor("out", (SEQ, D), F32, kind="ExternalOutput").ap()
    build_kernel(nc, d, out)
    r = run_bass_kernel_spmd(nc, [{f"{k}_dram": v for k, v in arrays.items()}], core_ids=[0])
    return r.results[0]["out"].reshape(1, SEQ, D)
```

```python
import math
from contextlib import ExitStack

import concourse.bass as bass
from concourse import mybir

F32 = mybir.dt.float32
F32R = mybir.dt.float32r
I32 = mybir.dt.int32
U32 = mybir.dt.uint32
ALU = mybir.AluOpType
ACT = mybir.ActivationFunctionType
AX = mybir.AxisListType

P = 128
SEQ, D = 256, 1024
NT = SEQ // P
KD = D // P
ALPHA = (2.0 * 2) ** 0.25
LN_EPS, RMS_EPS = 1e-5, 1e-6
DI, HD, NG, NS = 2048, 64, 4, 128
NH = DI // HD
HG = NH // NG
XBC = DI + 2 * NG * NS
NM = XBC // P
MX = DI // P
GW = DI // NG
AH, NOPE, ROPE, VD, QL, KVL = 8, 128, 64, 128, 384, 256
HR = ROPE // 2
SCALE = (NOPE + ROPE) ** -0.5
FF, NE, TOPK = 2816, 8, 2
FC = 256
NC = FF // FC
MAX_EXTRA = SEQ * TOPK // (P + 1)
NTAB = NE + MAX_EXTRA + 1
UW, NRAW, NPART = 1024, 11, 6
GU, DN = 2 * KD * FC // UW, 2 * D // UW
ITEM = NC * (GU + DN)
assert ITEM % NRAW == 0 and ITEM % NPART == 0
R_Z = NM
R_WO = R_Z + NG * KD * GW // UW
R_FFN = R_WO + MX
R_KVQ = R_FFN + ITEM
R_KVB = R_KVQ + KD
R_QB = R_KVB + 4
R_O = R_QB + 5
R_MOE = R_O + AH
S_Z = NM
S_WO = S_Z + NG * KD * GW // UW
S_FFN = S_WO + MX
S_KVQ = S_FFN + ITEM
S_MOE = S_KVQ + KD
NEG = -1.0e30
TWO_PI_1, TWO_PI_2 = 6.28125, 2029.0 / 2 ** 20
TWO_PI_3 = 2 * math.pi - TWO_PI_1 - TWO_PI_2
MAGIC = 1.5 * 2 ** 23
PI_IN = 3.1415925


class Count:

    def __init__(self):
        self.n, self.extra = 0, None

    def up(self, by=1):
        self.n += by
        return self.value()

    def value(self):
        return self.n if self.extra is None else self.extra + self.n


def build_kernel(nc, d, out):
    ctx = ExitStack()
    with ctx:
        def sb(name, shape, dt=F32):
            return ctx.enter_context(nc.sbuf_tensor(name, shape, dt))

        def sems(names):
            return [ctx.enter_context(nc.semaphore(n)) for n in names.split()]

        raw = sb("raw", [P, NRAW, UW])
        w_hi, w_lo = sb("w_hi", [P, NPART, UW], F32R), sb("w_lo", [P, NPART, UW], F32R)
        h_tok = sb("h_tok", [P, NT, D])
        h_hi, h_lo = sb("h_hi", [P, KD, SEQ], F32R), sb("h_lo", [P, KD, SEQ], F32R)
        ln_gb = sb("ln_gb", [P, 2 * D])
        ident, tri, stri, ones = (sb(n, [P, P]) for n in ("ident", "tri", "stri", "ones"))
        slot_iota = sb("slot_iota", [P, P])
        causal_add = sb("causal_add", [P, 2 * P])
        before = sb("before", [P, NE, NE])
        neg_half = sb("neg_half", [P, 2])
        conv_wb = sb("conv_wb", [P, NM, 5])
        gains = sb("gains", [P, MX + 2 + 3])
        rows = sb("rows", [P, 3 * NH + NE + HR])
        wrt_hi, wrt_lo = sb("wrt_hi", [P, KD, NE], F32R), sb("wrt_lo", [P, KD, NE], F32R)
        pos_i = sb("pos_i", [P, NT], I32)
        dt_bias, a_log, d_skip = (rows[:, k * NH:(k + 1) * NH] for k in range(3))
        b_rt = rows[:, 3 * NH:3 * NH + NE]
        inv_freq = rows[:, 3 * NH + NE:]
        NJ = 2 * NG + 4 * NT + NT
        pow_in_t, pow_out_t = sb("pow_in_t", [P, NJ, 2]), sb("pow_out_t", [P, NJ, 2])
        bn, mv = sb("bn", [P, 2, 6]), sb("mv", [P, NT, 2])
        sil, hid = sb("sil", [P, 2, FC]), sb("hid", [P, 2, FC])
        hid_hi, hid_lo = sb("hid_hi", [P, 2, 2, P], F32R), sb("hid_lo", [P, 2, 2, P], F32R)
        wdt_hi, wdt_lo = (v[:].rearrange("p a b c -> p (a b c)")[:, 0:KD * NH].rearrange("p (k n) -> p k n", k=KD)
                          for v in (hid_hi, hid_lo))
        dt, la = sb("dt", [P, NT * NH]), sb("la", [P, NT * NH])
        exp_a = sb("exp_a", [P, NH])
        cum, to_end, decay_end, decay_cum = (
            sb("cum", [P, NT * NH]), sb("to_end", [P, NH]), sb("decay_end", [P, NH]), sb("decay_cum", [P, NH]))
        sq_sum = sb("sq_sum", [P, 2 * NG])
        ang_r, ang_c = sb("ang_r", [P, NT, HR]), sb("ang_c", [P, NT, HR])
        pos_f = sb("pos_f", [P, NT])
        sin_t, cos_t = sb("sin_t", [P, NT, HR]), sb("cos_t", [P, NT, HR])
        kq_ss = sb("kq_ss", [P, NT, 2])
        mx, negm, psum_row, rinv = (sb(n, [P, AH * NT]) for n in ("mx", "negm", "psum_row", "rinv"))
        logits, top_v = sb("logits", [P, NT, NE]), sb("top_v", [P, NT, NE])
        top_i, top_f = sb("top_i", [P, NT, NE], U32), sb("top_f", [P, NT, 2])
        one_hot = sb("one_hot", [P, 2, NT, NE])
        gap, gap_e, den, w_top = sb("gap", [P, NT]), sb("gap_e", [P, NT]), sb("den", [P, NT]), sb("w_top", [P, 2, NT])
        chosen, gates, posm = sb("chosen", [P, NT, NE]), sb("gates", [P, NT, NE]), sb("posm", [P, NT, NE])
        chosen_sum = sb("chosen_sum", [P, NE])
        over, rank, sel = sb("over", [P, NE]), sb("rank", [P, NE]), sb("sel", [P, MAX_EXTRA, NE])
        rank_in = sb("rank_in", [P, NE, NE])
        sel_in = sb("sel_in", [P, MAX_EXTRA, NE])
        ctl_f, ctl = sb("ctl_f", [P, MAX_EXTRA + 1]), sb("ctl", [P, MAX_EXTRA + 1], I32)
        slot_tab, gate_tab = sb("slot_tab", [P, NT, NTAB]), sb("gate_tab", [P, NT, NTAB])

        WORK = 16896
        with nc.sbuf_tensor("work", [P, WORK], F32) as work:
            pass
        y_hi = sb("y_hi", [P, MX, SEQ], F32R)
        over_bc = sb("over_bc", [P, 2 * NG, SEQ])
        y_lo = sb("y_lo", [P, NT, MX, P], F32R)
        work_end = sb("work_end", [P, WORK - (NM + MX) * SEQ])
        used = [0]

        def carve(*shape):
            n = math.prod(shape)
            v = work[:, used[0]:used[0] + n]
            used[0] += n
            assert used[0] <= WORK, used
            names = "abcd"[:len(shape)]
            if len(shape) > 1:
                v = v.rearrange(f"p ({' '.join(names)}) -> p {' '.join(names)}", **dict(zip(names, shape)))
            return v

        xbc_T = carve(NM, SEQ)
        z_gate = carve(NT, NG, GW)
        used[0] -= NT * NG * GW
        x_T, w_dt, w_rt = carve(KD, SEQ), carve(KD, NH), carve(KD, NE)
        used[0] = NM * SEQ + NT * NG * GW
        cb_mask = carve(NT * NG, P)
        used[0] -= NT * NG * P
        dt_v, dt_e, dt_s, dt_q, dt_p = (carve(NT * NH) for _ in range(5))
        ang, ang_k = carve(NT, HR), carve(NT, HR)
        dt_T = carve(SEQ)
        used[0] = NM * SEQ + NT * NG * GW + NT * NG * P
        x_skip, x_dt = carve(2, GW), carve(2, GW)
        x_end, state, b_tok = carve(GW), carve(GW), carve(NG, P)
        decay = carve(2, 4, P)
        mix_T = carve(2, 4, P)
        y_tmp = hid[:].rearrange("p a b -> p (a b)")
        conv_acc = x_skip.rearrange("p a (b c) -> p (a b) c", c=SEQ)[:, 0:2, :]
        y_sq = sil[:].rearrange("p a b -> p (a b)")
        used[0] = 0
        ckv_n, q_n = carve(NT, KVL), carve(NT, QL)
        k_rot = carve(NT, ROPE)
        ckv_T, q_T = carve(2, SEQ), carve(3, SEQ)
        kn_T, qn_T = carve(AH, SEQ), carve(AH, SEQ)
        v_tok = carve(NT, AH * VD)
        q_rot = carve(NT, AH * ROPE)
        rot_a, rot_b = carve(AH * HR), carve(AH * HR)
        qr_T, kr_T = carve(AH, SEQ), carve(SEQ)
        o_T = carve(AH, SEQ)
        prob, prob_T = carve(4, SEQ), carve(2, NT, P)
        sq_junk = carve(QL)
        used[0] = 0
        moe_acc = carve(NT, D)
        y_e = carve(2, 512)
        pick, pick_g = carve(NT, P), carve(NT, P)
        scat = carve(NT, P)
        logits_T = carve(SEQ)

        ps = ctx.enter_context(nc.psum_tensor("ps", [P, 8, 512], F32))

        raw_full = sems(" ".join(f"raw_full{n}" for n in range(NRAW)))
        (x_in, xt_in0, xt_in1, small_in, wdt_in, wrt_in, gb_in, out_done) = sems(
            "x_in xt_in0 xt_in1 small_in wdt_in wrt_in gb_in out_done")
        (hi_done, lo_pool, lo_done, parts_used, direct_used, consts) = sems(
            "hi_done lo_pool lo_done parts_used direct_used consts")
        (small_hi, small_lo, h_hi_done) = sems("small_hi small_lo h_hi_done")
        dve_step, = sems("dve_step")
        (dt_mmT, dt_T_ready, rt_mmT, rt_T_ready) = sems("dt_mmT dt_T_ready rt_mmT rt_T_ready")
        (dt_mm, dt_abs, dt_exp, la_ready, cum_mm, cum_ready, decays) = sems(
            "dt_mm dt_abs dt_exp la_ready cum_mm cum_ready decays")
        (conv_done, xbc_done, z_done) = sems("conv_done xbc_done z_done")
        (btr_mm, b_done, cb_mm, cb_done) = sems("btr_mm b_done cb_mm cb_done")
        (xs_tr, x_done, bc_mm, relu_done, dec_done, mix_done) = sems(
            "xs_tr x_done bc_mm relu_done dec_done mix_done")
        (st_mm, st_done, yd_mm, yoff_mm, y_done, sq_done, yn_done, yt_mm, yt_hi, yt_done) = sems(
            "st_mm st_done yd_mm yoff_mm y_done sq_done yn_done yt_mm yt_hi yt_done")
        (pow_go, pow_ok, ln_done, ln_tr, hT_done, tile0_mm) = sems("pow_go pow_ok ln_done ln_tr hT_done tile0_mm")
        (ang_done, trig_done) = sems("ang_done trig_done")
        (f_gu0, f_silu, f_hid, f_tr, f_hT, f_hThi) = sems("f_gu0 f_silu f_hid f_tr f_hT f_hThi")
        kq_mm0, = sems("kq_mm0")
        (kq_sq, kq_done, kq_tr, kqT_done) = sems("kq_sq kq_done kq_tr kqT_done")
        (nope_mm, nope_done, v_mm, v_done, qr_mm, qrot_done, qr_tr, qrT_done) = sems(
            "nope_mm nope_done v_mm v_done qr_mm qrot_done qr_tr qrT_done")
        (sc_mm, max_done, exp_done, prob_done, prob_tr, probT_done, o_mm, o_done) = sems(
            "sc_mm max_done exp_done prob_done prob_tr probT_done o_mm o_done")
        (rt_mm, gap_done, gap_exp, chosen_done, pos_mm, route_done) = sems(
            "rt_mm gap_done gap_exp chosen_done pos_mm route_done")
        (m_pick, m_gat, m_xehi, m_xe, m_silu, m_hid, m_tr, m_hThi, m_hT, m_yec, m_sc, m_acc, m_str, m_scat) = sems(
            "m_pick m_gat m_xehi m_xe m_silu m_hid m_tr m_hThi m_hT m_yec m_sc m_acc m_str m_scat")
        moe_zero, = sems("moe_zero")

        block = ctx.enter_context(nc.Block())
        Z_BANKS = (5, 0)
        WO_BANKS = ((5, 0), (6, 7))
        LN_BANKS = (((1, 2), (3, 0)), ((4, 5), (6, 7)), ((0, 1), (2, 3)))
        SCORE_BANKS = (0, 1, 6, 7)
        NSMALL = 4

        KQ = KVL + ROPE + QL

        def unit(n):
            return raw[:, n % NRAW, :]

        def full(n):
            return raw_full[n % NRAW], 16 * (n // NRAW + 1)

        def freed(n):
            if n < R_Z:
                return lo_pool, n + 1
            if n < R_KVB:
                return lo_done, n - R_Z + 1
            if n < R_QB:
                return v_mm, NT
            if n < R_O:
                return qr_mm, NT
            return direct_used, n - R_O + 1

        ORDER = [("gu", 0, j) for j in range(GU)]
        for c in range(1, NC):
            ORDER += [("gu", c, j) for j in range(GU)] + [("dn", c - 1, j) for j in range(DN)]
        ORDER += [("dn", NC - 1, j) for j in range(DN)]
        AT = {u: r for r, u in enumerate(ORDER)}
        EARLY = 4
        LO0 = S_MOE - S_Z

        def full_moe(i, r):
            p = (R_MOE + r) % NRAW
            before_item = len(range(p, R_MOE, NRAW)) + len([x for x in range(r) if (R_MOE + x) % NRAW == p])
            return raw_full[p], (i * (ITEM // NRAW) + (before_item + 1)) * 16

        @block.sync
        def _(sp):
            def load(n, src):
                if n >= NRAW:
                    sp.wait_ge(*freed(n - NRAW))
                sp.dma_start(unit(n)[:, 0:src.shape[1]], src).then_inc(raw_full[n % NRAW], 16)

            def gain_bias(ln):
                if ln:
                    sp.wait_ge(ln_done, 2 * ln * NT)
                sp.dma_start(ln_gb[:], d["ln_gb"][ln].partition_broadcast(P)).then_inc(gb_in, 16)

            sp.dma_start(x_T[:, 0:4, :], d["x_T"][:, 0:4, :]).then_inc(xt_in0, 16)
            sp.dma_start(w_dt, d["w_dt"]).then_inc(wdt_in, 16)
            sp.dma_start(x_T[:, 4:8, :], d["x_T"][:, 4:8, :]).then_inc(xt_in1, 16)
            load(0, d["w_xbc"][0])
            for m in range(1, 4):
                load(m, d["w_xbc"][m])
            sp.dma_start(conv_wb[:], d["conv_wb"]).then_inc(small_in, 16)
            sp.dma_start(rows[:], d["rows"].partition_broadcast(P)).then_inc(small_in, 16)
            sp.dma_start(gains[:], d["gains"]).then_inc(small_in, 16)
            sp.dma_start(pos_i[:], d["pos"]).then_inc(small_in, 16)
            sp.dma_start(w_rt, d["w_rt"]).then_inc(wrt_in, 16)
            for m in range(4, NM):
                load(m, d["w_xbc"][m])
                if m == NRAW - 1:
                    sp.dma_start(h_tok[:], d["x_tok"]).then_inc(x_in, 16)
                    gain_bias(0)
            for u in range(R_WO - R_Z):
                load(R_Z + u, d["w_z"][u])
            for u in range(MX):
                load(R_WO + u, d["w_out"][u])
            for c in range(NC):
                for j in range(GU):
                    load(R_FFN + c * (GU + DN) + j, d["w_ffn_gu"][c][j])
                for j in range(DN):
                    load(R_FFN + c * (GU + DN) + GU + j, d["w_ffn_dn"][c][j])
                if c == 4:
                    gain_bias(1)
            for k in range(KD):
                load(R_KVQ + k, d["w_kvq"][k])
            for u in range(4):
                load(R_KVB + u, d["w_kvb"][u])
            for u in range(3):
                load(R_QB + u, d["w_qb"][u])
            for u in range(2):
                load(R_QB + 3 + u, d["w_qr"][u][:, 0:(2 - u) * AH * ROPE])
            gain_bias(2)
            for h in range(AH):
                load(R_O + h, d["w_o"][h])

            def load_item(i, e, n=ITEM, first=False):
                for r, (kind, c, j) in enumerate(ORDER[0:n]):
                    if first and r < NRAW:
                        sp.wait_ge(*freed(R_MOE + r - NRAW))
                    else:
                        sp.wait_ge(lo_done, i * ITEM + (LO0 + r - NRAW + 1))
                    sp.dma_start(unit(R_MOE + r), d["w_moe_" + kind][c][j][bass.ds(e, 1), :, :]
                                 .rearrange("o p n -> (o p) n")).then_inc(raw_full[(R_MOE + r) % NRAW], 16)

            load_item(0, 0, first=True)
            with sp.Fori(1, NE) as i:
                load_item(i, i)
            gain_bias(3)
            sp.wait_ge(route_done, 1)
            n_extra = sp.value_load(ctl[0:1, 0:1], min_val=0, max_val=MAX_EXTRA)
            n_items = sp.snap(n_extra + NE)
            with sp.If(n_extra > 0):
                with sp.Fori(0, n_extra) as k:
                    e = sp.value_load(ctl[0:1, bass.ds(k + 1, 1)], min_val=0, max_val=NE - 1)
                    load_item(k + NE, e)
            load_item(n_items, 0, n=EARLY)
            for t in range(NT):
                for f in range(2):
                    sp.wait_ge(ln_done, 2 * (3 * NT + t) + f + 1)
                    c = slice(f * 512, (f + 1) * 512)
                    sp.dma_start(out[t * P:(t + 1) * P, c], h_tok[:, t, c]).then_inc(out_done, 16)
            sp.wait_ge(out_done, 16 * 2 * NT)

        @block.gpsimd
        def _(pool):
            g = nc.gpsimd
            g.memset(ident[:], 0.0).then_inc(consts, 1)
            g.memset(tri[:], 1.0).then_inc(consts, 1)
            g.memset(stri[:], 1.0).then_inc(consts, 1)
            g.memset(ones[:], 1.0).then_inc(consts, 1)
            g.memset(causal_add[:], 0.0).then_inc(consts, 1)
            g.memset(before[:], 1.0).then_inc(consts, 1)
            g.memset(neg_half[:], -0.5).then_inc(consts, 1)
            g.memset(pow_in_t[:], 1.0).then_inc(consts, 1)
            g.memset(slot_tab[:], -1.0).then_inc(consts, 1)
            g.memset(gate_tab[:], 0.0).then_inc(consts, 1)
            g.iota(slot_iota[:], [[1, P]], base=0, channel_multiplier=0,
                   allow_small_or_imprecise_dtypes=True).then_inc(consts, 1)
            pool.wait_ge(consts, 11)
            g.affine_select(out=ident[:], in_=ident[:], compare_op=ALU.not_equal, fill=1.0, base=0,
                            pattern=[[-1, P]], channel_multiplier=1).then_inc(consts, 1)
            g.affine_select(out=tri[:], in_=tri[:], compare_op=ALU.is_ge, fill=0.0, base=0,
                            pattern=[[1, P]], channel_multiplier=-1).then_inc(consts, 1)
            g.affine_select(out=stri[:], in_=stri[:], compare_op=ALU.is_gt, fill=0.0, base=0,
                            pattern=[[1, P]], channel_multiplier=-1).then_inc(consts, 1)
            g.affine_select(out=causal_add[:, P:], in_=causal_add[:, P:], compare_op=ALU.is_ge, fill=NEG, base=0,
                            pattern=[[-1, P]], channel_multiplier=1).then_inc(consts, 1)
            g.affine_select(out=before[:], in_=before[:], compare_op=ALU.is_gt, fill=0.0, base=0,
                            pattern=[[1, NE], [-1, NE]], channel_multiplier=0).then_inc(consts, 1)
            for q in range(NM):
                pool.wait_ge(hi_done, q + 1)
                g.tensor_tensor(w_lo[:, q % NPART, :], unit(q), w_hi[:, q % NPART, :].bitcast(F32), ALU.subtract)\
                    .then_inc(lo_pool, 1)
            with pool.Fori(0, NJ) as j:
                pool.wait_ge(pow_go, j + 1)
                g.tensor_tensor(pow_out_t[:, bass.ds(j, 1), :], pow_in_t[:, bass.ds(j, 1), :],
                                neg_half[:, :].unsqueeze(1), ALU.pow).then_inc(pow_ok, 1)

        CONSTS = 16

        @block.tensor
        def _(pe):
            mm, tr = nc.tensor.matmul, nc.tensor.transpose

            def group(outp, pairs):
                for k, (a, b) in enumerate(pairs):
                    last = mm(outp, a, b, start=(k == 0), stop=(k == len(pairs) - 1))
                return last

            def tok(t):
                return slice(t * P, (t + 1) * P)

            def three(outp, a, b, first, last):
                mm(outp, a[0], b[0], start=first, stop=False)
                mm(outp, a[0], b[1], start=False, stop=False)
                return mm(outp, a[1], b[0], start=False, stop=last)

            def part(q, c0, c1):
                return w_hi[:, q % NPART, c0:c1], w_lo[:, q % NPART, c0:c1]

            def rows_of(k, cols):
                return h_hi[:, k, cols], h_lo[:, k, cols]

            def split_in(q):
                if q < S_Z:
                    pe.wait_ge(lo_pool, q + 1)
                else:
                    pe.wait_ge(lo_done, q - S_Z + 1)

            def turned(bank, n, w, halves):
                for k in range(KD):
                    if k % 4 == 0:
                        pe.wait_ge(hT_done, halves - 1 + k // 4)
                    last = three(ps[0:n, bank, 0:SEQ], (w[0][:, k, :], w[1][:, k, :]), rows_of(k, slice(0, SEQ)),
                                 k == 0, k == KD - 1)
                return last

            def turn_back(bank, n, small):
                for t in range(NT):
                    last = tr(ps[:, bank, SEQ + t * n:SEQ + (t + 1) * n], small[0:n, tok(t)], ident[0:n, 0:n])
                return last

            pe.wait_ge(small_lo, 1)
            turned(4, NH, (wdt_hi, wdt_lo), 2).then_inc(dt_mmT, 1)

            for m in range(NM):
                split_in(m)
                if m >= 4:
                    pe.wait_ge(conv_done, m - 3)
                for k in range(KD):
                    last = three(ps[:, m % 4, 0:SEQ], part(m, k * P, (k + 1) * P), rows_of(k, slice(0, SEQ)),
                                 k == 0, k == KD - 1)
                last.then_inc(parts_used, 1)
                if m == 0:
                    pe.wait_ge(consts, CONSTS)
                    pe.wait_ge(dt_T_ready, 1)
                    turn_back(4, NH, dt_T).then_inc(dt_mm, 1)
                if m == 7:
                    pe.wait_ge(consts, CONSTS)
                    pe.wait_ge(la_ready, 1)
                    mm(ps[:, 5, 0:NT * NH], tri[:], la[:], start=True, stop=True)
                    mm(ps[:, 5, NT * NH:2 * NT * NH], ones[:], la[:], start=True, stop=True).then_inc(cum_mm, 1)

            def z_step(u):
                g, half = divmod(u, 2)
                if u == 0:
                    pe.wait_ge(cum_ready, 1)
                    pe.wait_ge(conv_done, NM - 3)
                elif half == 0:
                    pe.wait_ge(z_done, NT * g)
                for j in (2 * half, 2 * half + 1):
                    q = S_Z + 4 * g + j
                    split_in(q)
                    for k in (2 * j, 2 * j + 1):
                        for t in range(NT):
                            last = three(ps[:, Z_BANKS[t], :], rows_of(k, tok(t)), part(q, k % 2 * GW, (k % 2 + 1) * GW),
                                         k == 0, k == KD - 1)
                    last.then_inc(parts_used, 1)

            z_step(0)
            pe.wait_ge(xbc_done, NM)
            pe.wait_ge(dt_abs, 1)
            for g in range(NG):
                last = tr(ps[:, 4, g * P:(g + 1) * P], xbc_T[:, MX + g, 0:P], ident[:])
            last.then_inc(btr_mm, 1)
            for t in range(NT):
                for g in range(NG):
                    last = mm(ps[:, 6 + t, g * P:(g + 1) * P], xbc_T[:, MX + g, tok(t)],
                              xbc_T[:, MX + NG + g, tok(t)], start=True, stop=True)
            last.then_inc(cb_mm, 1)

            def ssd_front(u):
                g, t = divmod(u, NT)
                if u >= 1:
                    pe.wait_ge(x_done, u)
                for j in range(4):
                    last = tr(ps[:, 3, j * P:(j + 1) * P], xbc_T[:, g * 4 + j, tok(t)], ident[:])
                last.then_inc(xs_tr, 1)
                for b in range(2):
                    if u >= 1:
                        pe.wait_ge(relu_done, 2 * u + b - 1)
                    elif b == 0:
                        pe.wait_ge(cb_done, 1)
                    for j in range(4):
                        h = t * NH + g * HG + b * 4 + j
                        last = mm(ps[:, 6 + b, j * P:(j + 1) * P], la[:, h:h + 1].broadcast_to([P, P]), tri[:],
                                  start=True, stop=True)
                    last.then_inc(bc_mm, 1)

            def y_back(u):
                pe.wait_ge(yn_done, u + 1)
                if u >= 1:
                    pe.wait_ge(yt_done, u)
                g, t = divmod(u, NT)
                for j in range(4):
                    last = tr(ps[:, 2, j * P:(j + 1) * P], z_gate[:, t, g, j * P:(j + 1) * P], ident[:])
                last.then_inc(yt_mm, 1)

            def tile_by_tile(k0, nk):
                ahead = 5
                for k in range(k0, nk - ahead):
                    yield k, 0
                    yield k, 1
                for t in range(NT):
                    for k in range(nk - ahead, nk):
                        yield k, t

            FILL = 4

            def mixer_output(k, t):
                pe.wait_ge(yt_done, 2 * (k // 4) + t + 1)
                if k == 0:
                    pe.wait_ge(z_done, NU)
                    if t:
                        pe.wait_ge(relu_done, 2 * NU)
                if t == 0:
                    split_in(S_WO + k)
                for f in range(2):
                    last = three(ps[:, WO_BANKS[t][f], :], (y_hi[:, k, tok(t)], y_lo[:, t, k, :]),
                                 part(S_WO + k, f * 512, (f + 1) * 512), k == 0, k == MX - 1)
                if t == NT - 1:
                    last.then_inc(parts_used, 1)
                elif k == MX - 1:
                    last.then_inc(tile0_mm, 1)

            NU = NG * NT
            ssd_front(0)
            z_step(1)
            for u in range(NU):
                g, t = divmod(u, NT)
                if u + 1 < NU:
                    ssd_front(u + 1)
                if u + 2 < NU:
                    z_step(u + 2)
                if t == 0:
                    pe.wait_ge(b_done, 1)
                    pe.wait_ge(x_done, u + 1)
                    if u >= 1:
                        pe.wait_ge(y_done, u)
                    mm(ps[:, 1, :], b_tok[:, g, :], x_end[:], start=True, stop=True).then_inc(st_mm, 1)
                else:
                    pe.wait_ge(st_done, g + 1)
                    mm(ps[:, 1, :], xbc_T[:, MX + NG + g, tok(t)], state, start=True, stop=True)\
                        .then_inc(yoff_mm, 1)
                if u == NU - 1:
                    for k in range(FILL // 2):
                        mixer_output(k, 0)
                if u >= 1:
                    pe.wait_ge(y_done, u)
                for b in range(2):
                    pe.wait_ge(mix_done, 2 * u + b + 1)
                    for j in range(4):
                        c = (b * 4 + j) * HD
                        last = mm(ps[:, 4, c:c + HD], mix_T[:, b, j, :], x_dt[:, u % 2, c:c + HD],
                                  start=True, stop=True)
                last.then_inc(yd_mm, 1)
                if u >= 1:
                    y_back(u - 1)
            for k in range(FILL // 2, FILL):
                mixer_output(k, 0)

            for k in range(FILL):
                mixer_output(k, 1)
            y_back(NU - 1)
            for k, t in tile_by_tile(FILL, MX):
                mixer_output(k, t)

            def to_channel_major(t, ln):
                for f in range(2):
                    pe.wait_ge(ln_done, 2 * (ln * NT + t) + f + 1)
                    for k in range(4):
                        last = tr(ps[:, LN_BANKS[ln][t][f], k * P:(k + 1) * P],
                                  h_tok[:, t, (4 * f + k) * P:(4 * f + k + 1) * P], ident[:])
                    last.then_inc(ln_tr, 1)

            steps = [(c, t) for c in range(NC) for t in range(NT)]

            def gate_up(s, j):
                c, t = steps[s]
                q = S_FFN + c * (GU + DN) + j
                if s < NT and j % 2 == 0:
                    pe.wait_ge(hT_done, 2 + 2 * s + j // 2 + 1)
                if t == 0:
                    split_in(q)
                if s >= 2 and j == 0:
                    pe.wait_ge(f_hid, s - 1)
                for k in (2 * j, 2 * j + 1):
                    last = three(ps[:, 4 + s % 2, :], rows_of(k, tok(t)), part(q, k % 2 * 512, (k % 2 + 1) * 512),
                                 k == 0, k == KD - 1)
                if t == NT - 1:
                    last.then_inc(parts_used, 1)
                elif j == GU - 1:
                    last.then_inc(f_gu0, 1)

            def down(s):
                c, t = steps[s]
                pe.wait_ge(f_hT, s + 1)
                for j in range(DN):
                    q = S_FFN + c * (GU + DN) + GU + j
                    if t == 0:
                        split_in(q)
                    for f in range(2):
                        last = three(ps[:, 2 * t + f, :], (hid_hi[:, s % 2, j, :], hid_lo[:, s % 2, j, :]),
                                     part(q, f * 512, (f + 1) * 512), c == 0 and j == 0, c == NC - 1 and j == DN - 1)
                    if t == NT - 1:
                        last.then_inc(parts_used, 1)
                if s == len(steps) - NT:
                    last.then_inc(tile0_mm, 1)

            to_channel_major(0, 0)
            for j in range(GU):
                gate_up(0, j)
            to_channel_major(1, 0)
            for s in range(len(steps)):
                if s + 1 < len(steps):
                    gate_up(s + 1, 0)
                pe.wait_ge(f_hid, s + 1)
                for j in range(2):
                    last = tr(ps[:, 6 + s % 2, j * P:(j + 1) * P], hid[:, s % 2, j * P:(j + 1) * P], ident[:])
                last.then_inc(f_tr, 1)
                early = 2 if s + 1 == len(steps) - 1 else GU
                for j in range(1, early):
                    if s + 1 < len(steps):
                        gate_up(s + 1, j)
                down(s)
                for j in range(early, GU):
                    gate_up(s + 1, j)

            def latents(t, ks):
                for k in ks:
                    q = S_KVQ + k
                    if t == 0:
                        split_in(q)
                        if k % 4 == 0:
                            pe.wait_ge(hT_done, 2 + 2 * NT + k // 4 + 1)
                    elif k == 0:
                        pe.wait_ge(hT_done, 2 + 4 * NT)
                    three(ps[:, 2 * t, 0:KVL + ROPE], rows_of(k, tok(t)), part(q, 0, KVL + ROPE), k == 0, k == KD - 1)
                    last = three(ps[:, 2 * t + 1, 0:QL], rows_of(k, tok(t)), part(q, KVL + ROPE, KQ), k == 0, k == KD - 1)
                    if t == NT - 1:
                        last.then_inc(parts_used, 1)
                    elif k == KD - 1:
                        last.then_inc(kq_mm0, 1)

            to_channel_major(0, 1)
            latents(0, range(NPART))
            to_channel_major(1, 1)
            latents(1, range(NPART))
            latents(0, range(NPART, KD))
            latents(1, range(NPART, KD))
            for t in range(NT):
                pe.wait_ge(kq_done, t + 1)
                for j in range(2):
                    tr(ps[:, 4 + 2 * t, j * P:(j + 1) * P], ckv_n[:, t, j * P:(j + 1) * P], ident[:])
                tr(ps[0:ROPE, 4 + 2 * t, 2 * P:3 * P], k_rot[:, t, :], ident[:])
                for j in range(3):
                    last = tr(ps[:, 5 + 2 * t, j * P:(j + 1) * P], q_n[:, t, j * P:(j + 1) * P], ident[:])
                last.then_inc(kq_tr, 1)
            pe.wait_ge(kqT_done, NT)
            for u in range(9):
                pe.wait_ge(*full(R_KVB + u))
            wk = [unit(R_KVB + k) for k in range(2)]
            wv = [unit(R_KVB + 2 + k) for k in range(2)]
            wq = [unit(R_QB + k) for k in range(3)]
            wr = [unit(R_QB + 3)[:, 0:AH * ROPE], unit(R_QB + 3)[:, AH * ROPE:], unit(R_QB + 4)[:, 0:AH * ROPE]]
            for h in range(AH):
                if h >= 4:
                    pe.wait_ge(nope_done, h - 3)
                group(ps[:, h % 4, 0:SEQ], [(wk[k][:, h * NOPE:(h + 1) * NOPE], ckv_T[:, k, :]) for k in range(2)])
                group(ps[:, h % 4, SEQ:2 * SEQ], [(wq[k][:, h * NOPE:(h + 1) * NOPE], q_T[:, k, :])
                                                  for k in range(3)]).then_inc(nope_mm, 1)
            for t in range(NT):
                for f in range(2):
                    last = group(ps[:, 4 + 2 * t + f, :],
                                 [(ckv_T[:, k, tok(t)], wv[k][:, f * 512:(f + 1) * 512]) for k in range(2)])
                last.then_inc(v_mm, 1)
            pe.wait_ge(nope_done, AH)
            for t in range(NT):
                group(ps[:, t, :], [(q_T[:, k, tok(t)], wr[k]) for k in range(3)]).then_inc(qr_mm, 1)
            for t in range(NT):
                pe.wait_ge(qrot_done, t + 1)
                pe.wait_ge(v_done, t + 1)
                for h in range(AH):
                    last = tr(ps[0:ROPE, 4 + 2 * t + h // 4, (h % 4) * P:(h % 4 + 1) * P],
                              q_rot[:, t, h * ROPE:(h + 1) * ROPE], ident[:])
                last.then_inc(qr_tr, 1)

            NA = AH * NT

            def scores(a):
                h, t = divmod(a, NT)
                if a >= 4:
                    pe.wait_ge(max_done, a - 3)
                nk = (t + 1) * P
                mm(ps[:, SCORE_BANKS[a % 4], 0:nk], qn_T[:, h, tok(t)], kn_T[:, h, 0:nk], start=True, stop=False)
                mm(ps[:, SCORE_BANKS[a % 4], 0:nk], qr_T[0:ROPE, h, tok(t)], kr_T[0:ROPE, 0:nk], start=False, stop=True)\
                    .then_inc(sc_mm, 1)

            def weighted_values(a):
                h, t = divmod(a, NT)
                pe.wait_ge(probT_done, a + 1)
                if a >= 2:
                    pe.wait_ge(o_done, a - 1)
                group(ps[:, 4 + a % 2, 0:P], [(v_tok[:, j, h * VD:(h + 1) * VD], prob_T[:, a % 2, j, :])
                                              for j in range(t + 1)]).then_inc(o_mm, 1)

            pe.wait_ge(qrT_done, NT)
            for a in range(4):
                scores(a)
            for a in range(NA):
                t = a % NT
                pe.wait_ge(prob_done, a + 1)
                for j in range(t + 1):
                    last = tr(ps[:, 2 + a % 2, j * P:(j + 1) * P], prob[:, a % 4, j * P:(j + 1) * P], ident[:])
                last.then_inc(prob_tr, 1)
                if a + 4 < NA:
                    scores(a + 4)
                if a >= 1:
                    weighted_values(a - 1)
            weighted_values(NA - 1)
            pe.wait_ge(o_done, NA)
            for h, t in tile_by_tile(0, AH):
                if t == 0:
                    pe.wait_ge(*full(R_O + h))
                for f in range(2):
                    last = mm(ps[:, 4 + 2 * t + f, :], o_T[:, h, tok(t)], unit(R_O + h)[:, f * 512:(f + 1) * 512],
                              start=(h == 0), stop=(h == AH - 1))
                if t == NT - 1:
                    last.then_inc(direct_used, 1)
                elif h == AH - 1:
                    last.then_inc(tile0_mm, 1)
            for t in range(NT):
                to_channel_major(t, 2)
            turned(4, NE, (wrt_hi, wrt_lo), 2 + 6 * NT).then_inc(rt_mmT, 1)
            pe.wait_ge(rt_T_ready, 1)
            turn_back(4, NE, logits_T).then_inc(rt_mm, 1)
            pe.wait_ge(chosen_done, 1)
            mm(ps[:, 5, 0:NE], stri[:], chosen[:, 0, :], start=True, stop=True)
            group(ps[:, 5, NE:2 * NE], [(stri[:], chosen[:, 1, :]), (ones[:], chosen[:, 0, :])])
            mm(ps[:, 5, 2 * NE:3 * NE], ones[:], chosen_sum[:], start=True, stop=True).then_inc(pos_mm, 1)

            def gather(i):
                pe.wait_ge(m_pick, i + 1)
                for k in range(KD):
                    last = group(ps[:, 2 + k // 4, (k % 4) * P:(k % 4 + 1) * P],
                                 [(h_tok[:, t, k * P:(k + 1) * P], pick[:, t, :]) for t in range(NT)])
                last.then_inc(m_gat, 1)

            def scatter(i, t):
                if t == 0:
                    pe.wait_ge(m_yec, i + 1)
                    pe.wait_ge(m_scat, i + 1)
                for j in (2 * t, 2 * t + 1):
                    f = j % 2
                    if j >= 2:
                        pe.wait_ge(m_acc, i * 4 + (j - 1))
                    mm(ps[:, 2 + j % 2, :], scat[:, t, :], y_e[:, f, :], start=True, stop=True).then_inc(m_sc, 1)

            gather(0)
            pe.wait_ge(route_done, 1)
            n_extra = pe.value_load(ctl[0:1, 0:1], min_val=0, max_val=MAX_EXTRA)
            n_items = pe.snap(n_extra + NE)
            with pe.Fori(0, n_items) as i:
                def split_moe(r):
                    pe.wait_ge(lo_done, i * ITEM + (LO0 + r + 1))

                def gate_up_moe(s, j):
                    r = AT["gu", s, j]
                    split_moe(r)
                    if s >= 2 and j == 0:
                        pe.wait_ge(m_hid, i * NC + (s - 1))
                    for k in (2 * j, 2 * j + 1):
                        last = three(ps[:, 4 + s % 2, :], rows_of(k, slice(0, P)),
                                     part(S_MOE + r, k % 2 * 512, (k % 2 + 1) * 512), k == 0, k == KD - 1)
                    last.then_inc(parts_used, 1)

                def hid_transpose_moe(s):
                    pe.wait_ge(m_hid, i * NC + (s + 1))
                    for j in range(2):
                        last = tr(ps[:, 6 + s % 2, j * P:(j + 1) * P], hid[:, s % 2, j * P:(j + 1) * P], ident[:])
                    last.then_inc(m_tr, 1)

                def down_moe(s):
                    pe.wait_ge(m_hT, i * NC + (s + 1))
                    for j in range(DN):
                        r = AT["dn", s, j]
                        split_moe(r)
                        for f in range(2):
                            last = three(ps[:, f, :], (hid_hi[:, s % 2, j, :], hid_lo[:, s % 2, j, :]),
                                         part(S_MOE + r, f * 512, (f + 1) * 512), s == 0 and j == 0,
                                         s == NC - 1 and j == DN - 1)
                        last.then_inc(parts_used, 1)

                pe.wait_ge(m_xe, i * 2 + 2)
                for j in range(GU):
                    gate_up_moe(0, j)
                scatter(i, 0)
                gate_up_moe(1, 0)
                scatter(i, 1)
                gate_up_moe(1, 1)
                pe.wait_ge(m_acc, i * 4 + 4)
                for t in range(NT):
                    last = tr(ps[:, 2, t * P:(t + 1) * P], pick_g[:, t, :], ident[:])
                last.then_inc(m_str, 1)
                for s in range(NC - 1):
                    ahead = 2 if s == 0 else 1
                    if s:
                        gate_up_moe(s + 1, 0)
                    hid_transpose_moe(s)
                    for j in range(ahead, GU):
                        gate_up_moe(s + 1, j)
                    down_moe(s)
                hid_transpose_moe(NC - 1)
                pe.wait_ge(m_scat, i + 2)
                gather(i + 1)
                down_moe(NC - 1)
            for t in range(NT):
                scatter(n_items, t)

        @block.scalar
        def _(act):
            A = nc.scalar.activation

            def high(n, q, width=UW):
                act.wait_ge(*full(n))
                if q >= NPART:
                    act.wait_ge(parts_used, q - NPART + 1)
                A(w_hi[:, q % NPART, 0:width], unit(n)[:, 0:width], ACT.Copy).then_inc(hi_done, 1)

            act.wait_ge(xt_in0, 16)
            A(h_hi[:, 0:4, :], x_T[:, 0:4, :], ACT.Copy).then_inc(h_hi_done, 1)
            act.wait_ge(wdt_in, 16)
            A(wdt_hi[:], w_dt, ACT.Copy).then_inc(small_hi, 1)
            act.wait_ge(xt_in1, 16)
            A(h_hi[:, 4:8, :], x_T[:, 4:8, :], ACT.Copy).then_inc(h_hi_done, 1)
            for q in range(4):
                high(q, q)
            act.wait_ge(wrt_in, 16)
            A(wrt_hi[:], w_rt, ACT.Copy).then_inc(small_hi, 1)
            act.wait_ge(small_in, 16 * NSMALL)
            A(exp_a[:], a_log, ACT.Exp).then_inc(dt_exp, 1)
            act.wait_ge(dt_abs, 1)
            A(dt_e[:], dt_s[:], ACT.Exp).then_inc(dt_exp, 1)
            high(4, 4)
            high(5, 5)
            for m in range(NM):
                high(m + NPART, m + NPART)
                act.wait_ge(conv_done, m + 1)
                A(xbc_T[:, m, :], conv_acc[:, m % 2, :], ACT.Silu).then_inc(xbc_done, 1)
                if m == 8:
                    act.wait_ge(ang_done, 2)
                    A(sin_t[:], ang_r[:], ACT.Sin).then_inc(trig_done, 1)
                    A(cos_t[:], ang_c[:], ACT.Sin).then_inc(trig_done, 1)
            act.wait_ge(cum_ready, 1)
            A(decay_end[:], to_end[:], ACT.Exp).then_inc(decays, 1)
            A(decay_cum[:], cum[:, NH:], ACT.Exp).then_inc(decays, 1)
            def z_silu(u):
                g, t = divmod(u, NT)
                if t == 0:
                    act.wait_ge(parts_used, S_Z + 4 * (g + 1))
                A(z_gate[:, t, g, :], ps[:, Z_BANKS[t], :], ACT.Silu).then_inc(z_done, 1)

            def head_decays(u):
                g, t = divmod(u, NT)
                for b in range(2):
                    act.wait_ge(bc_mm, 2 * u + b + 1)
                    if u >= 1:
                        act.wait_ge(mix_done, 2 * u + b - 1)
                    for j in range(4):
                        h = t * NH + g * HG + b * 4 + j
                        last = A(decay[:, b, j, :], ps[:, 6 + b, j * P:(j + 1) * P], ACT.Relu,
                                 bias=cum[:, h:h + 1], scale=-1.0)
                    last.then_inc(relu_done, 1)
                for b in range(2):
                    act.wait_ge(relu_done, 2 * u + b + 1)
                    A(decay[:, b, :, :], decay[:, b, :, :], ACT.Exp, scale=-1.0).then_inc(dec_done, 1)

            def y_square(u):
                g, t = divmod(u, NT)
                act.wait_ge(y_done, u + 1)
                if u >= 1:
                    act.wait_ge(sq_done, u)
                A(y_sq, z_gate[:, t, g, :], ACT.Square, accum_out=sq_sum[:, u:u + 1]).then_inc(sq_done, 1)

            def y_channel_major(u):
                g, t = divmod(u, NT)
                act.wait_ge(yt_mm, u + 1)
                for j in range(4):
                    m = g * 4 + j
                    last = A(y_hi[:, m, t * P:(t + 1) * P], ps[:, 2, j * P:(j + 1) * P], ACT.Copy,
                             scale=gains[:, m:m + 1])
                last.then_inc(yt_hi, 1)

            NU = NG * NT
            act.wait_ge(btr_mm, 1)
            A(b_tok, ps[:, 4, :].rearrange("p (g c) -> p g c", g=NG), ACT.Copy).then_inc(b_done, 1)
            head_decays(0)
            for z in range(NPART, NPART + 4):
                high(R_Z + z, S_Z + z)
            z_silu(0)
            z_silu(1)
            for u in range(NU):
                g, t = divmod(u, NT)
                if t == 0:
                    act.wait_ge(st_mm, g + 1)
                    A(state, ps[:, 1, :], ACT.Copy).then_inc(st_done, 1)
                if u + 1 < NU:
                    head_decays(u + 1)
                for z in (2 * u + NPART + 4, 2 * u + NPART + 5):
                    if S_Z + z < S_WO:
                        high(R_Z + z, S_Z + z)
                if t == 1 and u + 2 < NU:
                    z_silu(u + 1)
                    z_silu(u + 2)
                y_square(u)
                if u >= 1:
                    y_channel_major(u - 1)
                if NU - 5 <= u < NU - 2:
                    for r in (2 * (u - NU + 5), 2 * (u - NU + 5) + 1):
                        high(R_WO + r, S_WO + r)
            y_channel_major(NU - 1)

            def h_high(t, ln):
                for b in range(2):
                    act.wait_ge(ln_tr, 2 * (ln * NT + t) + b + 1)
                    A(h_hi[:, 4 * b:4 * b + 4, t * P:(t + 1) * P],
                      ps[:, LN_BANKS[ln][t][b], :].rearrange("p (k c) -> p k c", k=4), ACT.Copy).then_inc(h_hi_done, 1)

            for r in range(NPART, MX + NPART):
                high(R_WO + r, S_WO + r)
            for t in range(NT):
                h_high(t, 0)

            def silu(s):
                c, t = divmod(s, NT)
                if t == 0:
                    act.wait_ge(f_gu0, c + 1)
                else:
                    act.wait_ge(parts_used, S_FFN + c * (GU + DN) + GU)
                A(sil[:, s % 2, :], ps[:, 4 + s % 2, 0:FC], ACT.Silu).then_inc(f_silu, 1)

            def hid_high(s):
                act.wait_ge(f_tr, s + 1)
                A(hid_hi[:, s % 2, :, :], ps[:, 6 + s % 2, 0:2 * P].rearrange("p (j c) -> p j c", j=2), ACT.Copy)\
                    .then_inc(f_hThi, 1)

            def high_next(c, j):
                r = (c + 1) * (GU + DN) + j
                high(R_FFN + r, S_FFN + r, UW if c + 1 < NC else KQ)

            silu(0)
            for c in range(NC):
                high_next(c, 0)
                hid_high(2 * c)
                high_next(c, 1)
                high_next(c, 2)
                silu(2 * c + 1)
                high_next(c, 3)
                hid_high(2 * c + 1)
                if c + 1 < NC:
                    silu(2 * c + 2)
                high_next(c, 4)
                high_next(c, 5)
            for t in range(NT):
                h_high(t, 1)
            for k in range(NPART, KD):
                high(R_KVQ + k, S_KVQ + k, KQ)
            for t in range(NT):
                if t == 0:
                    act.wait_ge(kq_mm0, 1)
                else:
                    act.wait_ge(parts_used, S_KVQ + KD)
                    act.wait_ge(kq_sq, 2 * t)
                A(sq_junk[:, 0:KVL], ps[:, 2 * t, 0:KVL], ACT.Square, accum_out=kq_ss[:, t, 0:1]).then_inc(kq_sq, 1)
                act.wait_ge(kq_sq, 2 * t + 1)
                A(sq_junk[:, 0:QL], ps[:, 2 * t + 1, 0:QL], ACT.Square, accum_out=kq_ss[:, t, 1:2]).then_inc(kq_sq, 1)
            for t in range(NT):
                act.wait_ge(kq_tr, t + 1)
                s_ = slice(t * P, (t + 1) * P)
                for j in range(2):
                    A(ckv_T[:, j, s_], ps[:, 4 + 2 * t, j * P:(j + 1) * P], ACT.Copy, scale=gains[:, MX + j:MX + j + 1])
                A(kr_T[0:ROPE, s_], ps[0:ROPE, 4 + 2 * t, 2 * P:3 * P], ACT.Copy)
                for j in range(3):
                    last = A(q_T[:, j, s_], ps[:, 5 + 2 * t, j * P:(j + 1) * P], ACT.Copy,
                             scale=gains[:, MX + 2 + j:MX + 3 + j])
                last.then_inc(kqT_done, 1)
            for h in range(AH):
                act.wait_ge(nope_mm, h + 1)
                A(kn_T[:, h, :], ps[:, h % 4, 0:SEQ], ACT.Copy)
                A(qn_T[:, h, :], ps[:, h % 4, SEQ:], ACT.Copy).then_inc(nope_done, 1)
            for t in range(NT):
                act.wait_ge(qr_tr, t + 1)
                for b in range(2):
                    last = A(qr_T[0:ROPE, 4 * b:4 * b + 4, t * P:(t + 1) * P],
                             ps[0:ROPE, 4 + 2 * t + b, :].rearrange("p (h c) -> p h c", h=4), ACT.Copy)
                last.then_inc(qrT_done, 1)

            def softmax_exp(a):
                nk = (a % NT + 1) * P
                act.wait_ge(max_done, a + 1)
                A(prob[:, a % 4, 0:nk], prob[:, a % 4, 0:nk], ACT.Exp, bias=negm[:, a:a + 1], scale=SCALE,
                  accum_out=psum_row[:, a:a + 1]).then_inc(exp_done, 1)

            def out_T(a):
                h, t = divmod(a, NT)
                act.wait_ge(o_mm, a + 1)
                A(o_T[:, h, t * P:(t + 1) * P], ps[:, 4 + a % 2, 0:P], ACT.Copy).then_inc(o_done, 1)

            softmax_exp(0)
            softmax_exp(1)
            for a in range(AH * NT):
                if a + 2 < AH * NT:
                    softmax_exp(a + 2)
                act.wait_ge(prob_tr, a + 1)
                if a >= 2:
                    act.wait_ge(o_mm, a - 1)
                nk = a % NT + 1
                A(prob_T[:, a % 2, 0:nk, :], ps[:, 2 + a % 2, 0:nk * P].rearrange("p (j c) -> p j c", j=nk), ACT.Copy)\
                    .then_inc(probT_done, 1)
                if a >= 2:
                    out_T(a - 2)
            out_T(AH * NT - 2)
            out_T(AH * NT - 1)
            for r in range(EARLY):
                high(R_MOE + r, S_MOE + r)
            for t in range(NT):
                h_high(t, 2)
            act.wait_ge(gap_done, 1)
            A(gap_e[:], gap[:], ACT.Exp).then_inc(gap_exp, 1)

            def expert_rows_high(i):
                act.wait_ge(m_gat, i + 1)
                for b in range(2):
                    A(h_hi[:, 4 * b:4 * b + 4, 0:P], ps[:, 2 + b, :].rearrange("p (k c) -> p k c", k=4), ACT.Copy)\
                        .then_inc(m_xehi, 1)

            act.wait_ge(route_done, 1)
            n_extra = act.value_load(ctl[0:1, 0:1], min_val=0, max_val=MAX_EXTRA)
            n_items = act.snap(n_extra + NE)
            with act.Fori(0, n_items) as i:
                def high_moe(r):
                    sem, n = full_moe(i, r)
                    act.wait_ge(sem, n)
                    act.wait_ge(parts_used, i * ITEM + (S_MOE + r - NPART + 1))
                    A(w_hi[:, (S_MOE + r) % NPART, :], unit(R_MOE + r), ACT.Copy).then_inc(hi_done, 1)

                def silu_moe(s):
                    act.wait_ge(parts_used, i * ITEM + (S_MOE + AT["gu", s, GU - 1] + 1))
                    A(sil[:, s % 2, :], ps[:, 4 + s % 2, 0:FC], ACT.Silu).then_inc(m_silu, 1)

                def hid_high_moe(s):
                    act.wait_ge(m_tr, i * NC + (s + 1))
                    A(hid_hi[:, s % 2, :, :], ps[:, 6 + s % 2, 0:2 * P].rearrange("p (j c) -> p j c", j=2), ACT.Copy)\
                        .then_inc(m_hThi, 1)

                A(psum_row[:, 0:1], ones[:, 0:1], ACT.Silu)
                expert_rows_high(i)
                for r in range(EARLY, NPART):
                    high_moe(r)
                act.wait_ge(parts_used, i * ITEM + S_MOE)
                for f in range(2):
                    last = A(y_e[:, f, :], ps[:, f, :], ACT.Copy)
                last.then_inc(m_yec, 1)
                for r in range(NPART, NPART + 2):
                    high_moe(r)
                silu_moe(0)
                high_moe(NPART + 2)
                high_moe(NPART + 3)
                act.wait_ge(m_str, i + 1)
                A(scat[:], ps[:, 2, 0:2 * P].rearrange("p (t c) -> p t c", t=NT), ACT.Copy).then_inc(m_scat, 1)
                for s in range(NC - 1):
                    nxt = range(AT["gu", s + 1, 0] + NPART, min(AT["gu", s + 1, 0] + NPART + GU + DN, ITEM + EARLY))
                    high_moe(nxt[0])
                    hid_high_moe(s)
                    high_moe(nxt[1])
                    for r in nxt[2:3]:
                        high_moe(r)
                    silu_moe(s + 1)
                    for r in nxt[3:]:
                        high_moe(r)
                hid_high_moe(NC - 1)
            act.wait_ge(parts_used, n_items * ITEM + S_MOE)
            for f in range(2):
                last = A(y_e[:, f, :], ps[:, f, :], ACT.Copy)
            last.then_inc(m_yec, 1)

        @block.vector
        def _(dve):
            V = nc.vector
            TS, TT, STT = V.tensor_scalar, V.tensor_tensor, V.scalar_tensor_tensor
            chain = Count()

            def step(ins):
                ins.then_inc(dve_step, 1)
                dve.wait_ge(dve_step, chain.up())

            def heads(ap, n=HG, w=HD):
                return ap.unsqueeze(2).broadcast_to([P, n, w])

            def by_head(ap, n=HG):
                return ap.rearrange("p (h w) -> p h w", h=n)

            def low(n, q, width=UW):
                dve.wait_ge(hi_done, q + 1)
                TT(w_lo[:, q % NPART, 0:width], unit(n)[:, 0:width], w_hi[:, q % NPART, 0:width].bitcast(F32),
                   ALU.subtract).then_inc(lo_done, 1)

            for j in range(2):
                dve.wait_ge(h_hi_done, j + 1)
                k = slice(4 * j, 4 * j + 4)
                TT(h_lo[:, k, :], x_T[:, k, :], h_hi[:, k, :].bitcast(F32), ALU.subtract).then_inc(hT_done, 1)
                if j == 0:
                    dve.wait_ge(small_hi, 1)
                    TT(wdt_lo[:], w_dt, wdt_hi[:].bitcast(F32), ALU.subtract).then_inc(small_lo, 1)
            dve.wait_ge(small_hi, 2)
            TT(wrt_lo[:], w_rt, wrt_hi[:].bitcast(F32), ALU.subtract).then_inc(small_lo, 1)
            dve.wait_ge(small_in, 16 * NSMALL)
            dve.wait_ge(dt_mmT, 1)
            V.tensor_copy(dt_T[0:NH, :], ps[0:NH, 4, 0:SEQ]).then_inc(dt_T_ready, 1)
            dve.wait_ge(dt_mm, 1)
            step(TT(dt_v[:].rearrange("p (t h) -> p t h", t=NT), ps[:, 4, SEQ:SEQ + NT * NH].rearrange("p (t h) -> p t h", t=NT),
                    dt_bias.unsqueeze(1).broadcast_to([P, NT, NH]), ALU.add))
            STT(dt_s[:], dt_v[:], -1.0, dt_v[:], ALU.mult, ALU.min).then_inc(dt_abs, 1)
            dve.wait_ge(dt_exp, 2)
            step(TS(dt_q[:], dt_e[:], 2.0, None, ALU.add))
            step(V.reciprocal(dt_q[:], dt_q[:]))
            step(TT(dt_s[:], dt_e[:], dt_q[:], ALU.mult))
            step(TT(dt_q[:], dt_s[:], dt_s[:], ALU.mult))
            step(TS(dt_p[:], dt_q[:], 1.0 / 17, None, ALU.mult))
            for k in (15, 13, 11, 9, 7, 5, 3):
                step(STT(dt_p[:], dt_p[:], 1.0 / k, dt_q[:], ALU.add, ALU.mult))
            step(STT(dt_p[:], dt_p[:], 1.0, dt_s[:], ALU.add, ALU.mult))
            step(TS(dt_v[:], dt_v[:], 0.0, None, ALU.max))
            step(STT(dt[:], dt_p[:], 2.0, dt_v[:], ALU.mult, ALU.add))
            STT(la[:].rearrange("p (t h) -> p t h", t=NT), dt[:].rearrange("p (t h) -> p t h", t=NT), -1.0,
                exp_a[:].unsqueeze(1).broadcast_to([P, NT, NH]), ALU.mult, ALU.mult).then_inc(la_ready, 1)

            def rope_angles(quarter, dst):
                if quarter == 0.0:
                    step(V.tensor_copy(pos_f[:], pos_i[:]))
                    step(TT(ang[:], pos_f[:].unsqueeze(2).broadcast_to([P, NT, HR]),
                            inv_freq.unsqueeze(1).broadcast_to([P, NT, HR]), ALU.mult))
                step(TS(ang_k[:], ang[:], 1 / (2 * math.pi), quarter, ALU.mult, ALU.add))
                step(TS(ang_k[:], ang_k[:], MAGIC, None, ALU.add))
                step(TS(ang_k[:], ang_k[:], MAGIC, None, ALU.subtract))
                step(STT(dst[:], ang_k[:], -TWO_PI_1, ang[:], ALU.mult, ALU.add))
                step(STT(dst[:], ang_k[:], -TWO_PI_2, dst[:], ALU.mult, ALU.add))
                step(STT(dst[:], ang_k[:], -TWO_PI_3, dst[:], ALU.mult, ALU.add))
                step(TS(dst[:], dst[:], quarter * 2 * math.pi, PI_IN, ALU.add, ALU.min))
                TS(dst[:], dst[:], -PI_IN, None, ALU.max).then_inc(ang_done, 1)

            for m in range(NM):
                dve.wait_ge(parts_used, m + 1)
                if m >= 2:
                    dve.wait_ge(xbc_done, m - 1)
                acc, src = conv_acc[:, m % 2, :], ps[:, m % 4, 0:SEQ]
                step(TS(acc, src, conv_wb[:, m, 3:4], conv_wb[:, m, 4:5], ALU.mult, ALU.add))
                for b in (1, 2, 3):
                    ins = STT(acc[:, b:], src[:, 0:SEQ - b], conv_wb[:, m, 3 - b:4 - b], acc[:, b:], ALU.mult, ALU.add)
                    if b < 3:
                        step(ins)
                ins.then_inc(conv_done, 1)
                if m + NPART >= NM:
                    low(m + NPART, m + NPART)
                if m == 3:
                    rope_angles(0.0, ang_r)
                if m == 7:
                    rope_angles(0.25, ang_c)
                if m == 9:
                    dve.wait_ge(cum_mm, 1)
                    step(V.tensor_copy(cum[:], ps[:, 5, 0:NT * NH]))
                    TT(to_end[:], ps[:, 5, NT * NH:NT * NH + NH], cum[:, 0:NH], ALU.subtract).then_inc(cum_ready, 1)
            dve.wait_ge(cb_mm, 1)
            for t in range(NT):
                last = TT(cb_mask[:, t * NG:(t + 1) * NG, :], ps[:, 6 + t, :].rearrange("p (g c) -> p g c", g=NG),
                          tri[:].unsqueeze(1).broadcast_to([P, NG, P]), ALU.mult)
            last.then_inc(cb_done, 1)
            dve.wait_ge(decays, 2)

            def scaled_x(u):
                g, t = divmod(u, NT)
                hs = slice(g * HG, (g + 1) * HG)
                dve.wait_ge(xs_tr, u + 1)
                if u >= 2:
                    dve.wait_ge(yd_mm, u - 1)
                TT(by_head(x_skip[:, u % 2, :]), by_head(ps[:, 3, :]), heads(d_skip[:, hs]), ALU.mult)
                ins = TT(by_head(x_dt[:, u % 2, :]), by_head(ps[:, 3, :]),
                         heads(dt[:, t * NH + g * HG:t * NH + (g + 1) * HG]), ALU.mult)
                if t == 0:
                    step(ins)
                    ins = TT(by_head(x_end[:]), by_head(x_dt[:, u % 2, :]), heads(decay_end[:, hs]), ALU.mult)
                ins.then_inc(x_done, 1)

            def mix(u):
                g, t = divmod(u, NT)
                for b in range(2):
                    dve.wait_ge(dec_done, 2 * u + b + 1)
                    TT(mix_T[:, b, :, :], decay[:, b, :, :],
                       cb_mask[:, t * NG + g:t * NG + g + 1, :].broadcast_to([P, 4, P]), ALU.mult).then_inc(mix_done, 1)

            def y_low(u):
                g, t = divmod(u, NT)
                dve.wait_ge(yt_hi, u + 1)
                for j in range(4):
                    m = g * 4 + j
                    last = STT(y_lo[:, t, m, :], ps[:, 2, j * P:(j + 1) * P], gains[:, m:m + 1],
                               y_hi[:, m, t * P:(t + 1) * P].bitcast(F32), ALU.mult, ALU.subtract)
                last.then_inc(yt_done, 1)

            NU = NG * NT
            scaled_x(0)
            mix(0)
            for z in (NPART, NPART + 1):
                low(R_Z + z, S_Z + z)
            for u in range(NU):
                g, t = divmod(u, NT)
                if u + 1 < NU:
                    scaled_x(u + 1)
                for z in (2 * u + NPART + 2, 2 * u + NPART + 3):
                    if S_Z + z < S_WO:
                        low(R_Z + z, S_Z + z)
                dve.wait_ge(yd_mm, u + 1)
                skip = x_skip[:, u % 2, :]
                step(TT(skip, ps[:, 4, :], skip, ALU.add))
                if t == 1:
                    dve.wait_ge(yoff_mm, g + 1)
                    step(TT(by_head(y_tmp[:]), by_head(ps[:, 1, :]), heads(decay_cum[:, g * HG:(g + 1) * HG]), ALU.mult))
                    step(TT(skip, skip, y_tmp[:], ALU.add))
                dve.wait_ge(z_done, u + 1)
                y = z_gate[:, t, g, :]
                TT(y, y, skip, ALU.mult).then_inc(y_done, 1)
                if u + 1 < NU:
                    mix(u + 1)
                if 1 <= u < NU - 1:
                    y_low(u - 1)
                dve.wait_ge(sq_done, u + 1)
                TS(pow_in_t[:, u, 0:1], sq_sum[:, u:u + 1], 1.0 / GW, LN_EPS, ALU.mult, ALU.add).then_inc(pow_go, 1)
                if u >= NU - 5:
                    low(R_WO + u - NU + 5, S_WO + u - NU + 5)
                dve.wait_ge(pow_ok, u + 1)
                TS(y, y, pow_out_t[:, u, 0:1], None, ALU.mult).then_inc(yn_done, 1)
            y_low(NU - 2)
            y_low(NU - 1)

            J_LN, J_KQ = [NU, NU + NT, NU + 3 * NT, NU + 4 * NT], NU + 2 * NT

            def ln_sums(ln, t, src, added=None):
                for f in range(2):
                    if added:
                        hs = src[:, t, f * 512:(f + 1) * 512]
                        step(STT(hs, hs, ALPHA, added(f), ALU.mult, ALU.add))
                for f in range(2):
                    ins = V.bn_stats(bn[:, f, :], src[:, t, f * 512:(f + 1) * 512])
                step(ins)
                step(V.bn_aggr(mv[:, t, :], bn[:]))
                TS(pow_in_t[:, J_LN[ln] + t, 0:1], mv[:, t, 1:2], LN_EPS, None, ALU.add).then_inc(pow_go, 1)

            def ln_apply(ln, t, src):
                if t == 0:
                    dve.wait_ge(gb_in, 16 * (ln + 1))
                step(STT(h_tok[:, t, :], src[:, t, :], mv[:, t, 0:1], ln_gb[:, 0:D], ALU.subtract, ALU.mult))
                dve.wait_ge(pow_ok, J_LN[ln] + t + 1)
                for f in range(2):
                    hs = h_tok[:, t, f * 512:(f + 1) * 512]
                    STT(hs, hs, pow_out_t[:, J_LN[ln] + t, 0:1], ln_gb[:, D + f * 512:D + (f + 1) * 512],
                        ALU.mult, ALU.add).then_inc(ln_done, 1)

            dve.wait_ge(x_in, 16)
            for r in range(5, MX + 2):
                low(R_WO + r, S_WO + r)
            def h_low(t, ln):
                for b in range(2):
                    dve.wait_ge(h_hi_done, 2 + 2 * (ln * NT + t) + b + 1)
                    k, c = slice(4 * b, 4 * b + 4), slice(t * P, (t + 1) * P)
                    TT(h_lo[:, k, c], ps[:, LN_BANKS[ln][t][b], :].rearrange("p (k c) -> p k c", k=4),
                       h_hi[:, k, c].bitcast(F32), ALU.subtract).then_inc(hT_done, 1)

            def out_banks(banks):
                return lambda f: ps[:, banks[f], :]

            dve.wait_ge(tile0_mm, 1)
            ln_sums(0, 0, h_tok, out_banks(WO_BANKS[0]))
            ln_apply(0, 0, h_tok)
            low(R_FFN + 2, S_FFN + 2)
            h_low(0, 0)
            dve.wait_ge(parts_used, S_FFN)
            ln_sums(0, 1, h_tok, out_banks(WO_BANKS[1]))
            low(R_FFN + 3, S_FFN + 3)
            ln_apply(0, 1, h_tok)
            h_low(1, 0)
            low(R_FFN + 4, S_FFN + 4)
            low(R_FFN + 5, S_FFN + 5)

            def hidden(s):
                dve.wait_ge(f_silu, s + 1)
                TT(hid[:, s % 2, :], sil[:, s % 2, :], ps[:, 4 + s % 2, FC:], ALU.mult).then_inc(f_hid, 1)

            def hid_low(s):
                dve.wait_ge(f_hThi, s + 1)
                TT(hid_lo[:, s % 2, :, :], ps[:, 6 + s % 2, 0:2 * P].rearrange("p (j c) -> p j c", j=2),
                   hid_hi[:, s % 2, :, :].bitcast(F32), ALU.subtract).then_inc(f_hT, 1)

            def low_next(c, j):
                r = (c + 1) * (GU + DN) + j
                low(R_FFN + r, S_FFN + r, UW if c + 1 < NC else KQ)

            hidden(0)
            for c in range(NC - 1):
                low_next(c, 0)
                hid_low(2 * c)
                low_next(c, 1)
                low_next(c, 2)
                hidden(2 * c + 1)
                low_next(c, 3)
                hid_low(2 * c + 1)
                hidden(2 * c + 2)
                low_next(c, 4)
                low_next(c, 5)
            s = 2 * (NC - 1)
            low_next(NC - 1, 0)
            hid_low(s)
            low_next(NC - 1, 1)
            dve.wait_ge(tile0_mm, 2)
            ln_sums(1, 0, h_tok, out_banks((0, 1)))
            hidden(s + 1)
            low_next(NC - 1, 2)
            hid_low(s + 1)
            ln_apply(1, 0, h_tok)
            low_next(NC - 1, 3)
            h_low(0, 1)
            dve.wait_ge(parts_used, S_KVQ)
            ln_sums(1, 1, h_tok, out_banks((2, 3)))
            low_next(NC - 1, 4)
            low_next(NC - 1, 5)
            ln_apply(1, 1, h_tok)
            h_low(1, 1)
            for k in range(NPART, KD):
                low(R_KVQ + k, S_KVQ + k, KQ)

            def rotate(dst, src, t, n):
                x = src.rearrange("p (h c) -> p h c", h=n)
                y = dst.rearrange("p (h c) -> p h c", h=n)
                c = cos_t[:, t:t + 1, :].broadcast_to([P, n, HR])
                s = sin_t[:, t:t + 1, :].broadcast_to([P, n, HR])
                ra = rot_a[:, 0:n * HR].rearrange("p (h c) -> p h c", h=n)
                rb = rot_b[:, 0:n * HR].rearrange("p (h c) -> p h c", h=n)
                TT(ra, x[:, :, 0:HR], c, ALU.mult)
                step(TT(rb, x[:, :, HR:], s, ALU.mult))
                step(TT(y[:, :, 0:HR], ra, rb, ALU.subtract))
                TT(ra, x[:, :, HR:], c, ALU.mult)
                step(TT(rb, x[:, :, 0:HR], s, ALU.mult))
                return TT(y[:, :, HR:], ra, rb, ALU.add)

            dve.wait_ge(trig_done, 2)
            job = J_KQ
            for t in range(NT):
                dve.wait_ge(kq_sq, 2 * t + 2)
                TS(pow_in_t[:, job + t, 0:1], kq_ss[:, t, 0:1], 1.0 / KVL, RMS_EPS, ALU.mult, ALU.add)
                TS(pow_in_t[:, job + t, 1:2], kq_ss[:, t, 1:2], 1.0 / QL, RMS_EPS, ALU.mult, ALU.add).then_inc(pow_go, 1)
                step(rotate(k_rot[:, t, :], ps[:, 2 * t, KVL:KVL + ROPE], t, 1))
                dve.wait_ge(pow_ok, job + t + 1)
                TS(ckv_n[:, t, :], ps[:, 2 * t, 0:KVL], pow_out_t[:, job + t, 0:1], None, ALU.mult)
                TS(q_n[:, t, :], ps[:, 2 * t + 1, 0:QL], pow_out_t[:, job + t, 1:2], None, ALU.mult).then_inc(kq_done, 1)
            for t in range(NT):
                dve.wait_ge(v_mm, t + 1)
                for f in range(2):
                    last = V.tensor_copy(v_tok[:, t, f * 512:(f + 1) * 512], ps[:, 4 + 2 * t + f, :])
                last.then_inc(v_done, 1)
            for t in range(NT):
                dve.wait_ge(qr_mm, t + 1)
                ins = rotate(q_rot[:, t, :], ps[:, t, :], t, AH)
                ins.then_inc(qrot_done, 1)
                dve.wait_ge(qrot_done, t + 1)

            NA = AH * NT

            def masked_max(a):
                t = a % NT
                nk = (t + 1) * P
                dve.wait_ge(sc_mm, a + 1)
                if a >= 4:
                    dve.wait_ge(prob_tr, a - 3)
                step(V.tensor_tensor_reduce(out=prob[:, a % 4, 0:nk], in0=ps[:, SCORE_BANKS[a % 4], 0:nk],
                                            in1=causal_add[:, 2 * P - nk:], scale=1.0, scalar=NEG * 2,
                                            op0=ALU.add, op1=ALU.max, accum_out=mx[:, a:a + 1]))
                TS(negm[:, a:a + 1], mx[:, a:a + 1], -SCALE, None, ALU.mult).then_inc(max_done, 1)

            masked_max(0)
            masked_max(1)
            for a in range(NA):
                if a + 2 < NA:
                    masked_max(a + 2)
                nk = (a % NT + 1) * P
                dve.wait_ge(exp_done, a + 1)
                step(V.reciprocal(rinv[:, a:a + 1], psum_row[:, a:a + 1]))
                TS(prob[:, a % 4, 0:nk], prob[:, a % 4, 0:nk], rinv[:, a:a + 1], None, ALU.mult).then_inc(prob_done, 1)
            for r in range(EARLY):
                low(R_MOE + r, S_MOE + r)
            dve.wait_ge(tile0_mm, 3)
            ln_sums(2, 0, h_tok, out_banks((4, 5)))
            ln_apply(2, 0, h_tok)
            dve.wait_ge(direct_used, AH)
            ln_sums(2, 1, h_tok, out_banks((6, 7)))
            ln_apply(2, 1, h_tok)
            h_low(0, 2)
            h_low(1, 2)
            V.memset(scat[:], 0.0).then_inc(m_scat, 1)
            dve.wait_ge(ln_done, 2 * 3 * NT)

            dve.wait_ge(rt_mmT, 1)
            V.tensor_copy(logits_T[0:NE, :], ps[0:NE, 4, 0:SEQ]).then_inc(rt_T_ready, 1)
            dve.wait_ge(rt_mm, 1)
            step(TT(logits[:], ps[:, 4, SEQ:SEQ + NT * NE].rearrange("p (t e) -> p t e", t=NT),
                    b_rt.unsqueeze(1).broadcast_to([P, NT, NE]), ALU.add))
            for t in range(NT):
                step(V.max(top_v[:, t, :], logits[:, t, :]))
                step(V.max_index(top_i[:, t, :], top_v[:, t, :], logits[:, t, :]))
            step(V.tensor_copy(top_f[:], top_i[:, :, 0:2]))
            TT(gap[:], top_v[:, :, 1], top_v[:, :, 0], ALU.subtract).then_inc(gap_done, 1)
            for k in range(2):
                for t in range(NT):
                    ins = TS(one_hot[:, k, t, :], slot_iota[:, 0:NE], top_f[:, t, k:k + 1], None, ALU.is_equal)
            step(ins)
            step(TT(chosen[:], one_hot[:, 0, :, :], one_hot[:, 1, :, :], ALU.add))
            TT(chosen_sum[:], chosen[:, 0, :], chosen[:, 1, :], ALU.add).then_inc(chosen_done, 1)
            dve.wait_ge(gap_exp, 1)
            step(TS(den[:], gap_e[:], 1.0, None, ALU.add))
            step(V.reciprocal(w_top[:, 0, :], den[:]))
            step(TT(w_top[:, 1, :], gap_e[:], w_top[:, 0, :], ALU.mult))
            for t in range(NT):
                step(TS(gates[:, t, :], one_hot[:, 0, t, :], w_top[:, 0, t:t + 1], None, ALU.mult))
                step(STT(gates[:, t, :], one_hot[:, 1, t, :], w_top[:, 1, t:t + 1], gates[:, t, :], ALU.mult, ALU.add))
            dve.wait_ge(pos_mm, 1)
            step(STT(posm[:], ps[:, 5, 0:NT * NE].rearrange("p (t e) -> p t e", t=NT), 1.0, chosen[:], ALU.add, ALU.mult))
            step(TS(posm[:], posm[:], -1.0, None, ALU.add))
            dve.wait_ge(consts, CONSTS)
            V.tensor_copy(slot_tab[:, :, 0:NE], posm[:])
            step(V.tensor_copy(gate_tab[:, :, 0:NE], gates[:]))

            def picks(i):
                for t in range(NT):
                    TS(pick[:, t, :], slot_iota[:], slot_tab[:, t, bass.ds(i, 1)], None, ALU.is_equal)
                for t in range(NT):
                    ins = TS(pick_g[:, t, :], slot_iota[:], slot_tab[:, t, bass.ds(i, 1)],
                             gate_tab[:, t, bass.ds(i, 1)], ALU.is_equal, ALU.mult)
                ins.then_inc(m_pick, 1)

            picks(0)
            step(TS(over[:], ps[:, 5, 2 * NE:3 * NE], float(P), None, ALU.is_gt))
            V.tensor_reduce(ctl_f[:, 0:1], over[:], axis=AX.X, op=ALU.add)
            step(TT(rank_in[:], before[:], over[:].unsqueeze(1).broadcast_to([P, NE, NE]), ALU.mult))
            step(V.tensor_reduce(rank[:], rank_in[:], axis=AX.X, op=ALU.add))
            ME = MAX_EXTRA
            step(TT(sel[:], rank[:].unsqueeze(1).broadcast_to([P, ME, NE]),
                    slot_iota[:, 0:ME].unsqueeze(2).broadcast_to([P, ME, NE]), ALU.is_equal))
            step(TT(sel[:], sel[:], over[:].unsqueeze(1).broadcast_to([P, ME, NE]), ALU.mult))
            step(TT(rank_in[:, 0:ME, :], sel[:], slot_iota[:, 0:NE].unsqueeze(1).broadcast_to([P, ME, NE]), ALU.mult))
            step(V.tensor_reduce(ctl_f[:, 1:1 + ME], rank_in[:, 0:ME, :], axis=AX.X, op=ALU.add))
            V.tensor_copy(ctl[:], ctl_f[:]).then_inc(route_done, 1)
            step(TS(posm[:], posm[:], -float(P), None, ALU.add))
            for t in range(NT):
                for tab, of in ((slot_tab, posm), (gate_tab, gates)):
                    step(TT(sel_in[:], sel[:], of[:, t:t + 1, :].broadcast_to([P, ME, NE]), ALU.mult))
                    step(V.tensor_reduce(tab[:, t, NE:NE + ME], sel_in[:], axis=AX.X, op=ALU.add))

            def expert_rows_low(i):
                for b in range(2):
                    dve.wait_ge(m_xehi, 2 * i + (b + 1))
                    k = slice(4 * b, 4 * b + 4)
                    TT(h_lo[:, k, 0:P], ps[:, 2 + b, :].rearrange("p (k c) -> p k c", k=4),
                       h_hi[:, k, 0:P].bitcast(F32), ALU.subtract).then_inc(m_xe, 1)

            def accumulate(i, js):
                for j in js:
                    t, f = divmod(j, 2)
                    dve.wait_ge(m_sc, i * 4 + (j + 1))
                    a = moe_acc[:, t, f * 512:(f + 1) * 512]
                    TT(a, ps[:, 2 + j % 2, :], a, ALU.add).then_inc(m_acc, 1)

            dve.wait_ge(route_done, 1)
            TS(moe_acc[:], h_tok[:], ALPHA, None, ALU.mult).then_inc(moe_zero, 1)
            n_extra = dve.value_load(ctl[0:1, 0:1], min_val=0, max_val=MAX_EXTRA)
            n_items = dve.snap(n_extra + NE)
            dve.wait_ge(moe_zero, 1)
            with dve.Fori(0, n_items) as i:
                def low_moe(r):
                    dve.wait_ge(hi_done, i * ITEM + (S_MOE + r + 1))
                    TT(w_lo[:, (S_MOE + r) % NPART, :], unit(R_MOE + r), w_hi[:, (S_MOE + r) % NPART, :].bitcast(F32), ALU.subtract)\
                        .then_inc(lo_done, 1)

                def hidden_moe(s):
                    dve.wait_ge(m_silu, i * NC + (s + 1))
                    TT(hid[:, s % 2, :], sil[:, s % 2, :], ps[:, 4 + s % 2, FC:], ALU.mult).then_inc(m_hid, 1)

                def hid_low_moe(s):
                    dve.wait_ge(m_hThi, i * NC + (s + 1))
                    TT(hid_lo[:, s % 2, :, :], ps[:, 6 + s % 2, 0:2 * P].rearrange("p (j c) -> p j c", j=2),
                       hid_hi[:, s % 2, :, :].bitcast(F32), ALU.subtract).then_inc(m_hT, 1)

                expert_rows_low(i)
                for r in range(EARLY, NPART + 2):
                    low_moe(r)
                hidden_moe(0)
                accumulate(i, range(2))
                low_moe(NPART + 2)
                accumulate(i, range(2, 4))
                low_moe(NPART + 3)
                dve.wait_ge(m_str, i + 1)
                picks(i + 1)
                for s in range(NC - 1):
                    nxt = range(AT["gu", s + 1, 0] + NPART, min(AT["gu", s + 1, 0] + NPART + GU + DN, ITEM + EARLY))
                    low_moe(nxt[0])
                    hid_low_moe(s)
                    low_moe(nxt[1])
                    for r in nxt[2:3]:
                        low_moe(r)
                    hidden_moe(s + 1)
                    for r in nxt[3:]:
                        low_moe(r)
                hid_low_moe(NC - 1)
            accumulate(n_items, range(2))
            dve.wait_ge(m_acc, n_items * 4 + 2)
            ln_sums(3, 0, moe_acc)
            accumulate(n_items, range(2, 4))
            ln_apply(3, 0, moe_acc)
            dve.wait_ge(m_acc, n_items * 4 + 4)
            ln_sums(3, 1, moe_acc)
            ln_apply(3, 1, moe_acc)


def kernel(**inputs):
    import numpy as np
    import concourse.bacc as bacc
    from concourse.bass_utils import run_bass_kernel_spmd

    a = {k: np.asarray(v) for k, v in inputs.items()}

    def gate_up_units(gate, up):
        n = gate.ndim - 2
        w = np.stack([w.reshape(*w.shape[:n], GU, 2, P, NC, FC) for w in (gate, up)], axis=-2)
        return w.transpose(n + 3, n, *range(n), n + 2, n + 1, n + 4, n + 5).reshape(NC, GU, *gate.shape[:n], P, UW)

    def down_units(down):
        n = down.ndim - 2
        return down.reshape(*down.shape[:n], NC, DN, P, D).transpose(n, n + 1, *range(n), n + 2, n + 3)

    x = a["x"][0]
    w_in = a["ssm_w_in"][0]
    w_xbc = w_in[:, DI:DI + XBC].reshape(KD, P, NM, P).transpose(2, 1, 0, 3).reshape(NM, P, UW)
    w_z = w_in[:, 0:DI].reshape(KD // 2, 2, P, NG, GW).transpose(3, 0, 2, 1, 4).reshape(-1, P, UW)
    kvb = a["mla_w_kv_b"].reshape(KVL, AH, NOPE + VD)
    kvb = np.concatenate([kvb[:, :, :NOPE].reshape(2, P, UW), kvb[:, :, NOPE:].reshape(2, P, UW)], axis=0)
    qb = a["mla_w_q_b"][0].reshape(3, P, AH, NOPE + ROPE)
    w_qr = np.zeros((2, P, UW), np.float32)
    w_qr[0] = qb[0:2, :, :, NOPE:].reshape(2, P, -1).transpose(1, 0, 2).reshape(P, UW)
    w_qr[1, :, 0:AH * ROPE] = qb[2, :, :, NOPE:].reshape(P, -1)
    kvq = np.concatenate([a["mla_w_kv_a"], a["mla_w_q_a"][0]], axis=1)
    conv = np.concatenate([a["ssm_conv_w"][0], a["ssm_conv_b"]], axis=0)
    arrays = {
        "x_tok": x.reshape(NT, P, D).transpose(1, 0, 2),
        "x_T": x.T.reshape(KD, P, SEQ).transpose(1, 0, 2),
        "w_dt": w_in[:, DI + XBC:].reshape(KD, P, NH).transpose(1, 0, 2),
        "w_rt": a["moe_w_router"][0].reshape(KD, P, NE).transpose(1, 0, 2),
        "w_xbc": w_xbc, "w_z": w_z,
        "w_out": a["ssm_w_out"][0].reshape(MX, P, D),
        "w_ffn_gu": gate_up_units(a["ffn_w_gate"][0], a["ffn_w_up"][0]),
        "w_ffn_dn": down_units(a["ffn_w_down"][0]),
        "w_kvq": kvq.reshape(KD, P, -1),
        "w_kvb": kvb,
        "w_qb": qb[:, :, :, :NOPE].reshape(3, P, UW),
        "w_qr": w_qr,
        "w_o": a["mla_w_o"][0].reshape(AH, P, D),
        "w_moe_gu": gate_up_units(a["moe_w_gate"][0], a["moe_w_up"][0]),
        "w_moe_dn": down_units(a["moe_w_down"][0]),
        "conv_wb": conv.reshape(5, NM, P).transpose(2, 1, 0),
        "gains": np.concatenate([a["ssm_norm_g"].reshape(MX, P), a["mla_kv_norm_g"].reshape(2, P),
                                 a["mla_q_norm_g"].reshape(3, P)], axis=0).T,
        "rows": np.concatenate([a["ssm_dt_bias"][0], a["ssm_a_log"][0], a["ssm_d"][0], a["moe_b_router"][0],
                                np.array([10000.0 ** (-2.0 * k / ROPE) for k in range(HR)], np.float32)]),
        "ln_gb": np.stack([a["ln_g"].reshape(4, D), a["ln_b"].reshape(4, D)], axis=1).reshape(4, 2 * D),
        "pos": a["positions"].reshape(NT, P).T,
    }
    arrays = {k: np.ascontiguousarray(v) for k, v in arrays.items()}
    nc = bacc.Bacc("TRN2", target_bir_lowering=False, num_devices=1)
    d = {k: nc.dram_tensor(f"{k}_dram", v.shape, mybir.dt.from_np(v.dtype), kind="ExternalInput").ap()
         for k, v in arrays.items()}
    out = nc.dram_tensor("out", (SEQ, D), F32, kind="ExternalOutput").ap()
    build_kernel(nc, d, out)
    r = run_bass_kernel_spmd(nc, [{f"{k}_dram": v for k, v in arrays.items()}], core_ids=[0])
    return r.results[0]["out"].reshape(1, SEQ, D)
```
